# Optimizing a Trainium2 kernel written in Bass

```python
import math
import jax, jax.numpy as jnp
from jax import lax
import numpy as np

D_MODEL = 1024
BATCH = 1
SEQ = 256
DEPTH = 2
DEC_BATCH = 8
DEC_SEQ = 4
PAST_LEN = 2048
PAGE_SIZE = 128

N_EVEN = (DEPTH + 1) // 2
N_ODD = DEPTH // 2
RET_HEADS = 4
RET_DK = 128
RET_DV = 128
RET_WIDTH = RET_HEADS * RET_DK
RET_CHUNK = 128
ROPE_BASE = 10000.0
CONV_DIM = D_MODEL // 2
CONV_WIDTH = 3
AB_IN = 4 * RET_WIDTH + 3 * CONV_DIM
AB_OUT = RET_HEADS * RET_DV + CONV_DIM
HG_HEADS = 8
HG_DK = D_MODEL // HG_HEADS
HG_DV = D_MODEL // HG_HEADS
HG_DIM = HG_HEADS * HG_DK
HG_CHUNK = 64
PEER_HEADS = 8
PEER_DK = 256
N_KEYS = 128
N_EXPERTS = N_KEYS * N_KEYS
PEER_TOPK = 16
PEER_BLOCK = 128
NORM_EPS = 1e-6

kernel_name = 'retconv_hgrn2_peer_adaln_step'

def _chunk_size(L, target):
    c = min(L, target)
    while L % c:
        c -= 1
    return c

def _rmsnorm(x, g):
    x32 = x.astype(jnp.float32)
    y = x32 * lax.rsqrt(jnp.mean(x32 * x32, axis=-1, keepdims=True) + NORM_EPS)
    return (y * g).astype(x.dtype)

def _rope(x, pos):
    half = x.shape[-1] // 2
    inv = 1.0 / (ROPE_BASE ** jnp.linspace(0.0, 1.0, half, dtype=jnp.float32))
    ang = pos[:, None] * inv[None, :]
    cos = jnp.cos(ang)[None, :, None, :]
    sin = jnp.sin(ang)[None, :, None, :]
    x = x.astype(jnp.float32)
    x1, x2 = x[..., :half], x[..., half:]
    return jnp.concatenate([x1 * cos - x2 * sin, x1 * sin + x2 * cos], axis=-1)

def _to_blocks(t, nc, chunk):
    N, L, H, d = t.shape
    return t.reshape(N, nc, chunk, H, d).transpose(1, 0, 3, 2, 4)

def _retention_chunked(q, k, v, S0, log_gamma, chunk):
    N, L, H, dk = q.shape
    dv = v.shape[-1]
    nc = L // chunk
    pos = jnp.arange(chunk, dtype=jnp.float32)
    rel = pos[:, None] - pos[None, :]
    causal = rel >= 0
    lg = log_gamma[:, None, None]
    decay = jnp.where(causal, jnp.exp(lg * jnp.where(causal, rel, 0.0)), 0.0)
    in_decay = jnp.exp(log_gamma[:, None] * (pos + 1.0))[..., None]
    st_decay = jnp.exp(log_gamma[:, None] * (chunk - 1.0 - pos))[..., None]
    ch_decay = jnp.exp(log_gamma * chunk)[:, None, None]

    def step(S, inp):
        qb, kb, vb = inp
        att = jnp.einsum('nhid,nhjd->nhij', qb, kb) * decay
        o = jnp.einsum('nhij,nhjv->nhiv', att, vb) + jnp.einsum('nhid,nhdv->nhiv', qb * in_decay, S)
        S = S * ch_decay + jnp.einsum('nhjd,nhjv->nhdv', kb * st_decay, vb)
        return S, o

    S, o = lax.scan(step, S0.astype(jnp.float32),
                    (_to_blocks(q, nc, chunk), _to_blocks(k, nc, chunk), _to_blocks(v, nc, chunk)))
    return o.transpose(1, 0, 3, 2, 4).reshape(N, L, H, dv), S

def _gla_chunked(q, k, v, logf, S0, chunk):
    N, L, H, dk = q.shape
    dv = v.shape[-1]
    nc = L // chunk
    causal = jnp.tril(jnp.ones((chunk, chunk), dtype=bool))[:, :, None]

    def step(S, inp):
        qb, kb, vb, gb = inp
        b = jnp.cumsum(gb, axis=2)
        diff = b[:, :, :, None, :] - b[:, :, None, :, :]
        dec = jnp.exp(jnp.where(causal, diff, -jnp.inf))
        att = jnp.einsum('nhid,nhjd,nhijd->nhij', qb, kb, dec)
        o = jnp.einsum('nhij,nhjv->nhiv', att, vb) + jnp.einsum('nhid,nhdv->nhiv', qb * jnp.exp(b), S)
        b_last = b[:, :, -1:, :]
        S = S * jnp.exp(b_last[:, :, 0, :, None]) + jnp.einsum('nhjd,nhjv->nhdv', kb * jnp.exp(b_last - b), vb)
        return S, o

    S, o = lax.scan(step, S0.astype(jnp.float32),
                    (_to_blocks(q, nc, chunk), _to_blocks(k, nc, chunk),
                     _to_blocks(v, nc, chunk), _to_blocks(logf, nc, chunk)))
    return o.transpose(1, 0, 3, 2, 4).reshape(N, L, H, dv), S

def _retention_conv_mixer(h, pos, S0, zprev, w_in, ret_g, conv_w, w_out):
    N, L, _ = h.shape
    dt = h.dtype
    R, C = RET_WIDTH, CONV_DIM
    proj = h @ w_in
    q, k, v, g, bg, cg, xin = jnp.split(proj, [R, 2 * R, 3 * R, 4 * R, 4 * R + C, 4 * R + 2 * C], axis=-1)
    q = _rope(q.reshape(N, L, RET_HEADS, RET_DK), pos)
    k = _rope(k.reshape(N, L, RET_HEADS, RET_DK), pos) * (RET_DK ** -0.5)
    v = v.reshape(N, L, RET_HEADS, RET_DV).astype(jnp.float32)
    log_gamma = jnp.log(1.0 - 2.0 ** (-5.0 - jnp.arange(RET_HEADS, dtype=jnp.float32)))
    o, S = _retention_chunked(q, k, v, S0, log_gamma, _chunk_size(L, RET_CHUNK))
    o = _rmsnorm(o, ret_g).reshape(N, L, RET_HEADS * RET_DV)
    ret_out = (jax.nn.silu(g.astype(jnp.float32)) * o).astype(dt)
    z = cg * xin
    zpad = jnp.concatenate([zprev.astype(dt), z], axis=1)
    conv = sum(conv_w[i] * zpad[:, i:i + L] for i in range(CONV_WIDTH))
    conv_out = bg * conv
    y = jnp.concatenate([ret_out, conv_out], axis=-1) @ w_out
    return y, S.astype(dt), zpad[:, -(CONV_WIDTH - 1):]

def _hgrn2_mixer(h, S0, layer, w_in, lower_bounds, norm_g, w_out):
    N, L, _ = h.shape
    dt = h.dtype
    proj = h @ w_in
    q, f, i, g = jnp.split(proj, 4, axis=-1)
    q = jax.nn.silu(q.astype(jnp.float32)).reshape(N, L, HG_HEADS, HG_DK)
    sm = jax.nn.softmax(lower_bounds.astype(jnp.float32), axis=0)
    lb = (jnp.cumsum(sm, axis=0) - sm[0])[layer]
    fg = lb + (1.0 - lb) * jax.nn.sigmoid(f.astype(jnp.float32))
    logf = jnp.log(fg).reshape(N, L, HG_HEADS, HG_DK)
    kk = (1.0 - fg).reshape(N, L, HG_HEADS, HG_DK)
    iv = i.astype(jnp.float32).reshape(N, L, HG_HEADS, HG_DV)
    o, S = _gla_chunked(q, kk, iv, logf, S0, _chunk_size(L, HG_CHUNK))
    o = _rmsnorm(o, norm_g).reshape(N, L, HG_DIM) * jax.nn.silu(g.astype(jnp.float32))
    return o.astype(dt) @ w_out, S.astype(dt)

def _peer(h, wq, keys, u, v):
    N, L, D = h.shape
    blk = _chunk_size(L, PEER_BLOCK)
    hb_all = h.reshape(-1, blk, D)

    def block(hb):
        T = hb.shape[0]
        q = (hb @ wq).reshape(T, PEER_HEADS, 2, PEER_DK // 2)
        s = jnp.einsum('thpc,hpkc->thpk', q, keys).astype(jnp.float32)
        v1, i1 = lax.top_k(s[:, :, 0], PEER_TOPK)
        v2, i2 = lax.top_k(s[:, :, 1], PEER_TOPK)
        comb = (v1[..., :, None] + v2[..., None, :]).reshape(T, PEER_HEADS, PEER_TOPK * PEER_TOPK)
        vals, sel = lax.top_k(comb, PEER_TOPK)
        e1 = jnp.take_along_axis(i1, sel // PEER_TOPK, axis=-1)
        e2 = jnp.take_along_axis(i2, sel % PEER_TOPK, axis=-1)
        eid = e1 * N_KEYS + e2
        gate = jax.nn.softmax(vals, axis=-1)
        act = jax.nn.gelu(jnp.einsum('thkd,td->thk', u[eid], hb).astype(jnp.float32), approximate=False)
        w = (gate * act).astype(hb.dtype)
        return jnp.einsum('thk,thkd->td', w, v[eid])

    return lax.map(block, hb_all).reshape(N, L, D)

def _trunk(x, c, pos0, ret_S, conv_S, hg_S, p):
    N, L, _ = x.shape
    pos = pos0 + jnp.arange(L, dtype=jnp.float32)
    new_ret, new_conv, new_hg = [], [], []
    for l in range(DEPTH):
        mod = (jax.nn.silu(c) @ p['ada_w'][l] + p['ada_b'][l])[:, None, :]
        sh1, sc1, g1, sh2, sc2, g2 = jnp.split(mod, 6, axis=-1)
        h = _rmsnorm(x, p['norm_mix_g'][l]) * (1.0 + sc1) + sh1
        j = l // 2
        if l % 2 == 0:
            y, s_r, s_c = _retention_conv_mixer(h, pos, ret_S[j], conv_S[j], p['ab_w_in'][j],
                                                p['ret_norm_g'][j], p['conv_w'][j], p['ab_w_out'][j])
            new_ret.append(s_r)
            new_conv.append(s_c)
        else:
            y, s_h = _hgrn2_mixer(h, hg_S[j], l, p['hg_w_in'][j], p['hg_lower_bounds'],
                                  p['hg_norm_g'][j], p['hg_w_out'][j])
            new_hg.append(s_h)
        x = x + g1 * y
        h = _rmsnorm(x, p['norm_ffn_g'][l]) * (1.0 + sc2) + sh2
        x = x + g2 * _peer(h, p['peer_wq'][l], p['peer_keys'][l], p['peer_u'][l], p['peer_v'][l])
    y = _rmsnorm(x, p['final_norm_g'])
    return y, jnp.stack(new_ret), jnp.stack(new_conv), jnp.stack(new_hg)

def setup_inputs(seed: int = 0) -> dict:
    key = jax.random.key(seed)
    ks = jax.random.split(key, 24)
    D = D_MODEL

    def nrm(k, shape, s):
        return jax.random.normal(k, shape, jnp.float32) * s

    return {
        'x_prompt': nrm(ks[0], (BATCH, SEQ, D), 1.0),
        'x_sample': nrm(ks[1], (DEC_BATCH, DEC_SEQ, D), 1.0),
        'state_ret': nrm(ks[2], (N_EVEN, DEC_BATCH, RET_HEADS, RET_DK, RET_DV), 0.5),
        'state_conv': nrm(ks[3], (N_EVEN, DEC_BATCH, CONV_WIDTH - 1, CONV_DIM), 1.0),
        'state_hgrn': nrm(ks[4], (N_ODD, DEC_BATCH, HG_HEADS, HG_DK, HG_DV), 0.5),
        'c_prompt': nrm(ks[5], (BATCH, D), 1.0),
        'c_sample': nrm(ks[6], (DEC_BATCH, D), 1.0),
        'ada_w': nrm(ks[7], (DEPTH, D, 6 * D), 0.5 * D ** -0.5),
        'ada_b': nrm(ks[8], (DEPTH, 6 * D), 0.02),
        'norm_mix_g': 1.0 + nrm(ks[9], (DEPTH, D), 0.02),
        'norm_ffn_g': 1.0 + nrm(ks[10], (DEPTH, D), 0.02),
        'ab_w_in': nrm(ks[11], (N_EVEN, D, AB_IN), D ** -0.5),
        'ret_norm_g': 1.0 + nrm(ks[12], (N_EVEN, RET_HEADS, RET_DV), 0.02),
        'conv_w': nrm(ks[13], (N_EVEN, CONV_WIDTH, CONV_DIM), CONV_WIDTH ** -0.5),
        'ab_w_out': nrm(ks[14], (N_EVEN, AB_OUT, D), AB_OUT ** -0.5),
        'hg_w_in': nrm(ks[15], (N_ODD, D, 4 * HG_DIM), D ** -0.5),
        'hg_lower_bounds': nrm(ks[16], (DEPTH, HG_DIM), 0.1),
        'hg_norm_g': 1.0 + nrm(ks[17], (N_ODD, HG_HEADS, HG_DV), 0.02),
        'hg_w_out': nrm(ks[18], (N_ODD, HG_DIM, D), HG_DIM ** -0.5),
        'peer_wq': nrm(ks[19], (DEPTH, D, PEER_HEADS * PEER_DK), D ** -0.5),
        'peer_keys': nrm(ks[20], (DEPTH, PEER_HEADS, 2, N_KEYS, PEER_DK // 2), (PEER_DK // 2) ** -0.5),
        'peer_u': nrm(ks[21], (DEPTH, N_EXPERTS, D), D ** -0.5),
        'peer_v': nrm(ks[22], (DEPTH, N_EXPERTS, D), 0.5),
        'final_norm_g': 1.0 + nrm(ks[23], (D,), 0.02),
    }

def reference(x_prompt, x_sample, state_ret, state_conv, state_hgrn, c_prompt, c_sample,
              ada_w, ada_b, norm_mix_g, norm_ffn_g, ab_w_in, ret_norm_g, conv_w, ab_w_out,
              hg_w_in, hg_lower_bounds, hg_norm_g, hg_w_out, peer_wq, peer_keys, peer_u, peer_v,
              final_norm_g):
    p = dict(ada_w=ada_w, ada_b=ada_b, norm_mix_g=norm_mix_g, norm_ffn_g=norm_ffn_g,
             ab_w_in=ab_w_in, ret_norm_g=ret_norm_g, conv_w=conv_w, ab_w_out=ab_w_out,
             hg_w_in=hg_w_in, hg_lower_bounds=hg_lower_bounds, hg_norm_g=hg_norm_g, hg_w_out=hg_w_out,
             peer_wq=peer_wq, peer_keys=peer_keys, peer_u=peer_u, peer_v=peer_v,
             final_norm_g=final_norm_g)
    nb = x_prompt.shape[0]
    dt = x_prompt.dtype
    ret0 = jnp.zeros((N_EVEN, nb, RET_HEADS, RET_DK, RET_DV), dt)
    conv0 = jnp.zeros((N_EVEN, nb, CONV_WIDTH - 1, CONV_DIM), dt)
    hg0 = jnp.zeros((N_ODD, nb, HG_HEADS, HG_DK, HG_DV), dt)
    y_prompt, ret_p, conv_p, hg_p = _trunk(x_prompt, c_prompt, 0.0, ret0, conv0, hg0, p)
    y_sample, ret_s, conv_s, hg_s = _trunk(x_sample, c_sample, float(PAST_LEN),
                                           state_ret, state_conv, state_hgrn, p)
    return (y_prompt, y_sample, ret_p, conv_p, hg_p, ret_s, conv_s, hg_s)


_drawn_inputs = setup_inputs


def setup_inputs(seed=0):
    import zlib

    import numpy as np

    out = dict(_drawn_inputs(seed))
    spreads = {}
    factors = {'norm_ffn_g': 3.199, 'ret_norm_g': 7.177, 'hg_norm_g': 8.0, 'final_norm_g': 2.904}
    for name, (base, spread) in spreads.items():
        noise = np.random.default_rng([zlib.crc32(name.encode()), seed]).standard_normal(out[name].shape)
        drawn = base * np.exp(spread * noise) if base else spread * noise
        out[name] = __import__('jax').numpy.asarray(drawn.astype(out[name].dtype))
    for name, factor in factors.items():
        out[name] = (out[name] * factor).astype(out[name].dtype)
    return out
```

```python
from contextlib import ExitStack

import numpy as np
import concourse.bass as bass
from concourse import mybir

F32 = mybir.dt.float32
F32R = mybir.dt.float32r
U32 = mybir.dt.uint32
ALU = mybir.AluOpType
ACT = mybir.ActivationFunctionType
AX = mybir.AxisListType

P = 128
D_MODEL = 1024
KC = D_MODEL // P
T_PROMPT = 256
N_SEQ, L_SEQ = 8, 4
T_SAMPLE = N_SEQ * L_SEQ
T = T_PROMPT + T_SAMPLE
PAST_LEN = 2048
LAYERS = 2
RET_HEADS = 4
HG_HEADS = 8
PEER_HEADS = 8
TOPK = 16
N_KEYS = 128
LISTS = 2 * PEER_HEADS
EPS = 1e-6
LOWEST = -3.0e38
NS = N_SEQ + 2
TILES = [(0, P), (P, P), (T_PROMPT, T_SAMPLE)]
LEVELS = [64, 32, 16, 8, 4, 2, 1]
N_LEV = len(LEVELS)
SCALE = float(P) ** -0.5

RING = 4
ADA, AB_IN, OUT, WQ, EXP, HG_IN = 48, 28, 8, 16, 128, 32
SECTIONS = [("ada0", ADA), ("ab_in", AB_IN), ("ab_out", OUT), ("wq0", WQ), ("u0", EXP), ("v0", EXP),
            ("ada1", ADA), ("hg_in", HG_IN), ("hg_out", OUT), ("wq1", WQ), ("u1", EXP), ("v1", EXP)]
FIRST, LINEAR = {}, {}
_n = _m = 0
for _name, _count in SECTIONS:
    FIRST[_name], LINEAR[_name] = _n, _m
    _n += _count
    _m += 0 if _name[0] in "uv" else _count
N_BLOCKS = _n

LOG_GAMMA = np.log(1.0 - 2.0 ** (-5.0 - np.arange(RET_HEADS)))


class Tally:

    def __init__(self):
        self.base = self.local = self.per = 0
        self.i = None

    def enter(self, i, per):
        self.base, self.local, self.i, self.per = self.base + self.local, 0, i, per

    def leave(self, times):
        assert self.local == self.per
        self.base, self.local, self.i = self.base + self.per * times, 0, None

    def count(self):
        self.local += 1

    def static(self):
        return self.base + self.local

    def at(self, more=0):
        v = self.base + self.local + more
        return v if self.i is None else self.i * self.per + v


def trunk(nc, t):
    with ExitStack() as ctx:
        def sb(name, shape, dt=F32):
            return ctx.enter_context(nc.sbuf_tensor(name, shape, dt))

        def sem(name):
            return ctx.enter_context(nc.semaphore(name))

        big = sb("big", [P, N_KEYS * T])
        hs = sb("hs", [P, 2, KC, T], F32R)
        raw = sb("raw", [P, RING, D_MODEL])
        spl = sb("spl", [P, 2, 2, D_MODEL], F32R)
        mod = sb("mod", [P, ADA, NS])
        cs = sb("cs", [P, 2, KC, NS], F32R)
        choice = sb("choice", [P, 3, T])
        onehot = sb("onehot", [P, 4, 2, P])
        ident = sb("ident", [P, P])
        ones = sb("ones", [P, P])
        iota = sb("iota", [P, P])
        rstd = sb("rstd", [P, T])
        small = sb("small", [P, 96])
        ps = ctx.enter_context(nc.psum_tensor("ps", [P, 8, 512], F32))

        onehot_flat = onehot[:].rearrange("p a b c -> p (a b c)")
        gelu_out = [onehot_flat[:, 512 * s:512 * s + T] for s in range(2)]
        samp_tmp = small[:, 0:32].rearrange("p (s j) -> p s j", j=L_SEQ)
        ret_gain = small[:, 32:36]
        hg_gain = small[:, 36:44]
        conv_w = small[:, 44:56].rearrange("p (w c) -> p w c", c=4)
        final_gain = small[:, 56:64]
        topk_scratch = small[:, 64:96]

        class Region:
            def __init__(self, start):
                self.at = start

            def take(self, *shape):
                n = int(np.prod(shape))
                v = big[:, self.at:self.at + n]
                self.at += n
                assert self.at <= N_KEYS * T, self.at
                names = " ".join("abcde"[:len(shape)])
                if len(shape) == 1:
                    return v
                sizes = {"abcde"[k]: shape[k] for k in range(1, len(shape))}
                return v.rearrange(f"p ({names}) -> p {names}", **sizes)

        base = Region(0)
        x = base.take(KC, T)
        h = base.take(KC, T)
        after_h = base.at

        r0 = Region(after_h)
        proj0 = r0.take(AB_IN, T)
        cos_t = r0.take(T)
        sin_t = r0.take(T)
        swap = r0.take(P)
        q_decay = r0.take(RET_HEADS, T)
        att_decay = r0.take(RET_HEADS, P)
        att_decay_s = r0.take(RET_HEADS, T_SAMPLE)
        key_decay = r0.take(3, RET_HEADS)
        seq_mask = r0.take(N_SEQ)
        roped = r0.take(2 * RET_HEADS, T)
        swapped = r0.take(2 * RET_HEADS, T)
        qd = r0.take(RET_HEADS, T)
        vtok = r0.take(3, RET_HEADS, P)
        ktok = r0.take(3, RET_HEADS, P)
        att = r0.take(3, RET_HEADS, P)
        ret_s1 = r0.take(RET_HEADS, P)
        ret_s2 = r0.take(RET_HEADS, P)
        ret_state = r0.take(N_SEQ, RET_HEADS, P)
        conv_z = r0.take(4, T_PROMPT + 2)
        conv_zs = r0.take(4, N_SEQ, L_SEQ + 2)
        conv_tail = r0.take(4, 2)
        conv_tails = r0.take(4, N_SEQ, 2)
        ret_vmask = swapped.rearrange("p a b -> p (a b)")[0:T_SAMPLE, 0:1024].rearrange("p (s v) -> p s v", v=P)

        r1 = Region(after_h)
        proj1 = r1.take(HG_IN, T)
        logf = r1.take(HG_HEADS, T)
        restart = r1.take(T)
        fac = r1.take(N_LEV + 2, T)
        qe = r1.take(T)
        stage = r1.take(3, T)
        h_vtok = r1.take(3, P)
        h_ktok = r1.take(3, P)
        h_att = r1.take(2, 8, P)
        h_atts = r1.take(3, T_SAMPLE)
        h_vmask = r1.take(N_SEQ, P)
        lev_mask = r1.take(8, P)
        lev_masks = r1.take(3, T_SAMPLE)
        h_seq_mask = r1.take(N_SEQ)
        h_s1 = r1.take(P)
        h_out = r1.take(HG_HEADS, P)
        hg_states = r1.take(HG_HEADS, N_SEQ, P)
        s0_stage = r1.take(N_SEQ, P)
        bounds = r1.take(2, HG_HEADS)
        lb = r1.take(HG_HEADS)
        one_lb = r1.take(HG_HEADS)
        lbt = r1.take(HG_HEADS)

        r2 = Region(after_h)
        query = r2.take(LISTS, T)
        keys = Region(N_KEYS * T - LISTS * P).take(LISTS, P)
        score = r2.take(3, LISTS, P)
        score2 = r2.take(LISTS, P)
        comb = r2.take(PEER_HEADS, 256)
        comb2 = r2.take(PEER_HEADS, 256)
        eq = r2.take(P, TOPK)
        topv = r2.take(LISTS, TOPK)
        topi_u = r2.take(LISTS, TOPK).bitcast(U32)
        topi = r2.take(LISTS, TOPK)
        best = r2.take(PEER_HEADS, TOPK)
        pos_u = r2.take(PEER_HEADS, TOPK).bitcast(U32)
        half_u = r2.take(2, P).bitcast(U32)
        half = r2.take(2, P)
        pick = r2.take(3, 3, P)
        norm_s = r2.take(PEER_HEADS)
        assert r2.at <= N_KEYS * T - LISTS * P

        gates = big[:].rearrange("p (e t) -> p e t", t=T)
        c_in = Region(after_h + 16000).take(KC, NS)

        ada_b = sb("ada_b", [P, LAYERS, ADA])
        norm_g = sb("norm_g", [P, 2 * LAYERS, KC])
        amp = sb("amp", [P, KC, NS])

        const_landed = sem("const_landed")
        x_landed = sem("x_landed")
        raw_landed = [sem(f"raw_landed{s}") for s in range(RING)]
        high_ready, low_ready, block_done = sem("high_ready"), sem("low_ready"), sem("block_done")
        lin_free = sem("lin_free")
        glue_full, glue_free = sem("glue_full"), sem("glue_free")
        chain, act_chain = sem("chain"), sem("act_chain")
        c_silu, c_high, c_low = sem("c_silu"), sem("c_high"), sem("c_low")
        x_ready = sem("x_ready")
        sq_ready, var_ready, std_ready = sem("sq_ready"), sem("var_ready"), sem("std_ready")
        h_ready, h_high, h_low = sem("h_ready"), sem("h_high"), sem("h_low")
        ret_tables = sem("ret_tables")
        roped_ready, vtok_ready, ktok_ready = sem("roped_ready"), sem("vtok_ready"), sem("ktok_ready")
        qd_ready, att_ready, s1_ready, vmask_ready = sem("qd_ready"), sem("att_ready"), sem("s1_ready"), sem("vmask_ready")
        state_ready, state_stored = sem("state_ready"), sem("state_stored")
        sqo_ready, varo_ready, stdo_ready = sem("sqo_ready"), sem("varo_ready"), sem("stdo_ready")
        mixer_done, keys_landed = sem("mixer_done"), sem("keys_landed")
        scores_read = sem("scores_read")
        x_spilled, x_back = sem("x_spilled"), sem("x_back")
        shifted, exped, picks_ready = sem("shifted"), sem("exped"), sem("picks_ready")
        onehot_ready, onehot_used, gates_out = sem("onehot_ready"), sem("onehot_used"), sem("gates_out")
        gelu_ready, w_ready = sem("gelu_ready"), sem("w_ready")
        w_high, w_low = sem("w_high"), sem("w_low")
        hg_tables, keep_ready, log_ready, bound_in, bound_out = sem("hg_tables"), sem("keep_ready"), sem("log_ready"), sem("bound_in"), sem("bound_out")
        head_free, staged = sem("head_free"), sem("staged")
        diff_ready, fac_ready, x_lev_ready = sem("diff_ready"), sem("fac_ready"), sem("x_lev_ready")
        h_tok_ready, h_att_ready, h_s1_ready, h_vm_ready = sem("h_tok_ready"), sem("h_att_ready"), sem("h_s1_ready"), sem("h_vm_ready")
        y_ready, out_done = sem("y_ready"), sem("out_done")

        x_spill = t["x_spill"]
        block = ctx.enter_context(nc.Block())

        def section(eng, name, step, first=False, last=False, groups=None):
            lo, hi = groups or (0, dict(SECTIONS)[name] // RING)
            if first:
                for s in range(RING):
                    step(lo, s)
                lo += 1
            end = hi - 1 if last else hi
            if end > lo:
                with eng.Fori(lo, end) as i:
                    for s in range(RING):
                        step(i, s)
            if last:
                for s in range(RING):
                    step(hi - 1, s)

        @block.sync
        def _(sp):
            def load(name, src):
                n0 = FIRST[name]

                def step(i, s):
                    if not (isinstance(i, int) and n0 + 4 * i + s < RING):
                        sp.wait_ge(low_ready, i * 4 + (n0 + s - 3))
                    sp.dma_start(raw[:, s, :], src[i * 4 + s]).then_inc(raw_landed[s], 16)
                section(sp, name, step, first=n0 == 0)

            load("ada0", t["ada_w"][0])
            load("ab_in", t["ab_w_in"])
            load("ab_out", t["ab_w_out"])
            load("wq0", t["peer_wq"][0])
            load("u0", t["peer_u"][0])
            load("v0", t["peer_v"][0])
            load("ada1", t["ada_w"][1])
            load("hg_in", t["hg_w_in"])
            load("hg_out", t["hg_w_out"])
            load("wq1", t["peer_wq"][1])
            load("u1", t["peer_u"][1])
            load("v1", t["peer_v"][1])

        @block.gpsimd
        def _(pool):
            for dst, src in ((ident[:], t["ident"]), (ones[:], t["ones"]), (iota[:], t["iota"]),
                             (ada_b[:], t["ada_b"]), (norm_g[:], t["norm_g"]), (small[:, 32:64], t["gains"]),
                             (c_in, t["c"])):
                pool.dma_start(dst, src).then_inc(const_landed, 16)
            pool.dma_start(x, t["x"]).then_inc(x_landed, 16)
            for dst, src in ((cos_t, t["cos"]), (sin_t, t["sin"]), (swap, t["swap"]), (q_decay, t["q_decay"]),
                             (att_decay, t["att_decay"]), (att_decay_s[0:T_SAMPLE], t["att_decay_s"]),
                             (key_decay, t["key_decay"]), (seq_mask[0:T_SAMPLE], t["seq_mask"]),
                             (ret_state, t["state_ret"]), (conv_zs[:, :, :, 0:2], t["state_conv"])):
                pool.dma_start(dst, src).then_inc(ret_tables, 16)

            def peer(l):
                pool.wait_ge(mixer_done, l + 1)
                pool.dma_start(keys, t["peer_keys"][l]).then_inc(keys_landed, 16)
                pool.wait_ge(x_ready, 2 * l + 1)
                pool.dma_start(x_spill, x).then_inc(x_spilled, 16)
                pool.wait_ge(block_done, FIRST[f"v{l}"] + KC + 1)
                pool.dma_start(x, x_spill).then_inc(x_back, 16)

            pool.wait_ge(state_ready, 1)
            pool.dma_start(t["ret_p"], ret_s2).then_inc(state_stored, 16)
            pool.dma_start(t["ret_s"], ret_state).then_inc(state_stored, 16)
            pool.dma_start(t["conv_p"], conv_tail).then_inc(state_stored, 16)
            pool.dma_start(t["conv_s"], conv_tails).then_inc(state_stored, 16)
            peer(0)
            pool.wait_ge(block_done, FIRST["v0"] + EXP)
            for dst, src in ((restart, t["restart"]), (lev_mask, t["lev_mask"]), (lev_masks[0:T_SAMPLE], t["lev_masks"]),
                             (h_seq_mask[0:T_SAMPLE], t["seq_mask"]), (bounds, t["bounds"]), (hg_states, t["state_hgrn"])):
                pool.dma_start(dst, src).then_inc(hg_tables, 16)
            pool.wait_ge(state_ready, 2)
            pool.dma_start(t["hg_p"], h_out).then_inc(state_stored, 16)
            pool.dma_start(t["hg_s"], hg_states).then_inc(state_stored, 16)
            peer(1)
            pool.wait_ge(y_ready, 1)
            pool.dma_start(t["y"], h).then_inc(out_done, 16)
            pool.wait_ge(out_done, 16)
            pool.wait_ge(state_stored, 16 * 6)
            pool.wait_ge(x_spilled, 32)

        @block.scalar
        def _(act):
            def split_high(name, i, s):
                n0 = FIRST[name]
                act.wait_ge(raw_landed[(s + 1) % 4], (i + (n0 // 4 + (s + 1) // 4 + 1)) * 16)
                if not (isinstance(i, int) and n0 + 4 * i + s < 1):
                    act.wait_ge(block_done, i * 4 + (n0 + s))
                act.activation(spl[:, (s + 1) % 2, 0, :], raw[:, (s + 1) % 4, :], ACT.Copy).then_inc(high_ready, 1)

            def copy_out(name, dst, func, groups, first=False):
                def step(i, s):
                    split_high(name, i, s)
                    act.wait_ge(block_done, i * 4 + (FIRST[name] + s + 1))
                    act.activation(dst[:, bass.ds(i * 4 + s, 1), :], ps[:, s % 2:s % 2 + 1, 0:T], func).then_inc(lin_free, 1)
                section(act, name, step, groups=groups)

            def only_split(name, first=False, last=False):
                section(act, name, lambda i, s: split_high(name, i, s), first=first)

            def norm(j):
                if j == 0:
                    act.wait_ge(x_landed, 16)
                else:
                    act.wait_ge(x_ready, j)
                act.activation(h, x, ACT.Square).then_inc(sq_ready, 1)
                act.wait_ge(var_ready, j + 1)
                act.activation(rstd[:], rstd[:], ACT.Sqrt).then_inc(std_ready, 1)

            def high_input(k):
                act.wait_ge(h_ready, k)
                act.activation(hs[:, 0, :, :], h, ACT.Copy).then_inc(h_high, 1)

            def peer(l):
                norm(2 * l + 1)
                high_input(3 * l + 3)
                act.wait_ge(state_stored, 64 if l == 0 else 96)
                copy_out(f"wq{l}", query, ACT.Copy, (0, WQ // 4))
                for c in range(3):
                    act.wait_ge(shifted, 3 * l + c + 1)
                    act.activation(best, best, ACT.Exp).then_inc(exped, 1)
                act.wait_ge(x_spilled, 16 * (l + 1))
                with act.Fori(0, T // 8) as i:
                    for g in range(2):
                        act.wait_ge(onehot_used, i * 8 + (T * l + 4 * g + 4))
                        act.activation(gates[:, :, bass.ds(i * 8 + 4 * g, 4)],
                                       ps[:, 6 + g, :].rearrange("p (j e) -> p e j", j=4), ACT.Copy).then_inc(gates_out, 1)

                def expert_in(i, s):
                    split_high(f"u{l}", i, s)
                    q = EXP * l + s
                    act.wait_ge(block_done, i * 4 + (FIRST[f"u{l}"] + s + 1))
                    if not (isinstance(i, int) and 4 * i + q < 2):
                        act.wait_ge(w_ready, i * 4 + (q - 1))
                    act.activation(gelu_out[s % 2], ps[:, s % 2, 0:T], ACT.Gelu).then_inc(gelu_ready, 1)
                section(act, f"u{l}", expert_in, first=l == 0)

                def weight_high(e, slot):
                    act.activation(hs[:, 0, bass.ds(slot, 1), :], gates[:, bass.ds(e, 1), :], ACT.Copy).then_inc(w_high, 1)

                act.wait_ge(block_done, FIRST[f"v{l}"])
                act.wait_ge(w_ready, EXP * (l + 1))
                weight_high(0, 0)

                def expert_out(i, s):
                    if isinstance(i, int) and 4 * i + s == EXP - 1:
                        if l == 0:
                            split_high(f"v{l}", i, s)
                        return
                    split_high(f"v{l}", i, s)
                    weight_high(i * 4 + (s + 1), (s + 1) % 2)
                section(act, f"v{l}", expert_out, last=True)

            act.wait_ge(raw_landed[0], 16)
            act.activation(spl[:, 0, 0, :], raw[:, 0, :], ACT.Copy).then_inc(high_ready, 1)
            act.wait_ge(const_landed, 16 * 7)
            act.activation(c_in, c_in, ACT.Silu).then_inc(c_silu, 1)
            act.wait_ge(c_silu, 1)
            act.activation(cs[:, 0, :, :], c_in, ACT.Copy).then_inc(c_high, 1)
            only_split("ada0", first=True)
            norm(0)
            high_input(1)
            copy_out("ab_in", proj0, ACT.Copy, (0, 3))
            copy_out("ab_in", proj0, ACT.Silu, (3, 4))
            copy_out("ab_in", proj0, ACT.Copy, (4, 7))
            act.wait_ge(sqo_ready, 1)
            act.activation(swapped[:, 0:RET_HEADS, :], h[:, 0:RET_HEADS, :], ACT.Square).then_inc(sqo_ready, 1)
            act.wait_ge(varo_ready, 1)
            act.activation(roped[:, 0:RET_HEADS, :], roped[:, 0:RET_HEADS, :], ACT.Sqrt).then_inc(stdo_ready, 1)
            high_input(2)
            only_split("ab_out")
            peer(0)
            only_split("ada1")
            norm(2)
            high_input(4)
            copy_out("hg_in", proj1, ACT.Silu, (0, 2))
            copy_out("hg_in", proj1, ACT.Sigmoid, (2, 4))
            copy_out("hg_in", proj1, ACT.Copy, (4, 6))
            copy_out("hg_in", proj1, ACT.Silu, (6, 8))
            act.wait_ge(bound_in, 1)
            act.activation(bounds, bounds, ACT.Exp).then_inc(bound_out, 1)
            act.wait_ge(keep_ready, 1)
            act.activation(logf, proj1[:, 8:16, :], ACT.Ln).then_inc(log_ready, 1)
            with act.Fori(0, HG_HEADS) as i:
                act.wait_ge(head_free, i + 1)
                for k in range(3):
                    act.activation(stage[:, k:k + 1, :], proj1[:, bass.ds(i + 8 * k, 1), :], ACT.Copy).then_inc(staged, 1)
                act.activation(s0_stage, hg_states[:, bass.ds(i, 1), :, :], ACT.Copy).then_inc(staged, 1)
                act.wait_ge(diff_ready, i + 1)
                act.activation(fac, fac, ACT.Exp).then_inc(fac_ready, 1)
            act.wait_ge(sqo_ready, 3)
            act.activation(logf, h, ACT.Square).then_inc(sqo_ready, 1)
            act.wait_ge(varo_ready, 2)
            act.activation(proj1[:, 8:16, :], proj1[:, 8:16, :], ACT.Sqrt).then_inc(stdo_ready, 1)
            high_input(5)
            only_split("hg_out")
            peer(1)
            norm(4)

        @block.vector
        def _(dve):
            chained, taken = Tally(), Tally()

            def link(ins):
                chained.count()
                ins.then_inc(chain, 1)
                dve.wait_ge(chain, chained.at())

            def product():
                bank = 2 + taken.static() % 4
                taken.count()
                dve.wait_ge(glue_full, taken.at())
                return ps[:, bank, :]

            def released():
                dve.wait_ge(glue_free, taken.at())

            def split_low(name, i, s):
                dve.wait_ge(high_ready, i * 4 + (FIRST[name] + s + 2))
                dve.tensor_tensor(spl[:, (s + 1) % 2, 1, :], raw[:, (s + 1) % 4, :],
                                  spl[:, (s + 1) % 2, 0, :].bitcast(F32), ALU.subtract).then_inc(low_ready, 1)

            def only_split(name, groups=None):
                section(dve, name, lambda i, s: split_low(name, i, s), groups=groups)

            def ada(l):
                def step(i, s):
                    name = f"ada{l}"
                    split_low(name, i, s)
                    dve.wait_ge(block_done, i * 4 + (FIRST[name] + s + 1))
                    dve.tensor_scalar(mod[:, bass.ds(i * 4 + s, 1), :], ps[:, s % 2:s % 2 + 1, 0:NS],
                                      ada_b[:, l, bass.ds(i * 4 + s, 1)], None, ALU.add).then_inc(lin_free, 1)
                section(dve, f"ada{l}", step)
                dve.wait_ge(lin_free, LINEAR[f"ada{l}"] + ADA)

            def mean_root(j):
                s = product()
                dve.tensor_scalar(rstd[:], s[:, 0:T], 1.0 / D_MODEL, None, ALU.mult).then_inc(glue_free, 1)
                released()
                dve.tensor_scalar(rstd[:], rstd[:], EPS, None, ALU.add).then_inc(var_ready, 1)
                dve.wait_ge(std_ready, j + 1)
                link(dve.reciprocal(rstd[:], rstd[:]))

            def norm(j):
                l, part = j // 2, 24 * (j % 2)
                gain = norm_g[:, j, :, None].broadcast_to([P, KC, NS])
                link(dve.tensor_scalar(amp[:], mod[:, part + 8:part + 16, :], 1.0, None, ALU.add))
                link(dve.tensor_tensor(amp[:], amp[:], gain, ALU.mult))
                mean_root(j)
                link(dve.tensor_tensor(h, x, rstd[:, None, :].broadcast_to([P, KC, T]), ALU.mult))
                hs_view = h[:, :, T_PROMPT:T].rearrange("p k (s j) -> p k s j", j=L_SEQ)
                for k in range(KC):
                    dve.tensor_scalar(h[:, k, 0:T_PROMPT], h[:, k, 0:T_PROMPT], amp[:, k, 0:1], mod[:, part + k, 0:1],
                                      ALU.mult, ALU.add)
                    per_seq = amp[:, k, 1:9, None].broadcast_to([P, N_SEQ, L_SEQ])
                    ins = dve.tensor_tensor(hs_view[:, k], hs_view[:, k], per_seq, ALU.mult)
                link(ins)
                for k in range(KC):
                    per_seq = mod[:, part + k, 1:9, None].broadcast_to([P, N_SEQ, L_SEQ])
                    ins = dve.tensor_tensor(hs_view[:, k], hs_view[:, k], per_seq, ALU.add)
                ins.then_inc(h_ready, 1)

            def low_input(k):
                dve.wait_ge(h_high, k)
                dve.tensor_tensor(hs[:, 1, :, :], h, hs[:, 0, :, :].bitcast(F32), ALU.subtract).then_inc(h_low, 1)

            def add_to_x(k, k_static, bank, gate, freed, freed_value):
                xk = x[:, k, :] if k_static else x[:, bass.ds(k, 1), :]
                xk = xk if k_static else xk.rearrange("p a t -> p (a t)")
                if k_static:
                    gp, gsq = mod[:, gate + k, 0:1], mod[:, gate + k, 1:9]
                else:
                    gp = mod[:, bass.ds(k + gate, 1), 0:1].rearrange("p a t -> p (a t)")
                    gsq = mod[:, bass.ds(k + gate, 1), 1:9].rearrange("p a t -> p (a t)")
                dve.scalar_tensor_tensor(out=xk[:, 0:T_PROMPT], in0=bank[:, 0:T_PROMPT], scalar=gp,
                                         in1=xk[:, 0:T_PROMPT], op0=ALU.mult, op1=ALU.add)
                dve.tensor_tensor(samp_tmp, bank[:, T_PROMPT:T].rearrange("p (s j) -> p s j", j=L_SEQ),
                                  gsq[:, :, None].broadcast_to([P, N_SEQ, L_SEQ]), ALU.mult).then_inc(freed, 1)
                dve.wait_ge(freed, freed_value)
                xs = xk[:, T_PROMPT:T].rearrange("p (s j) -> p s j", j=L_SEQ)
                return dve.tensor_tensor(xs, xs, samp_tmp, ALU.add)

            def project_out(name, gate):
                def step(i, s):
                    split_low(name, i, s)
                    dve.wait_ge(block_done, i * 4 + (FIRST[name] + s + 1))
                    ins = add_to_x(i * 4 + s, False, ps[:, s % 2, :], gate, lin_free, i * 4 + (LINEAR[name] + s + 1))
                    link(ins)
                with dve.Fori(0, OUT // RING) as i:
                    chained.enter(i, RING)
                    for s in range(RING):
                        step(i, s)
                chained.leave(OUT // RING)
                dve.sem_inc(x_ready, 1)

            def retention():
                dve.wait_ge(ret_tables, 16 * 10)
                dve.wait_ge(lin_free, LINEAR["ab_out"])
                for c in range(2 * RET_HEADS):
                    s = product()
                    dve.tensor_tensor(swapped[:, c, :], s[:, 0:T], sin_t, ALU.mult).then_inc(glue_free, 1)
                link(dve.tensor_tensor(roped, proj0[:, 0:8, :], cos_t[:, None, :].broadcast_to([P, 8, T]), ALU.mult))
                released()
                dve.tensor_tensor(roped, roped, swapped, ALU.add).then_inc(roped_ready, 1)
                dve.wait_ge(roped_ready, 1)
                dve.tensor_tensor(qd, roped[:, 0:4, :], q_decay, ALU.mult).then_inc(qd_ready, 1)
                for c, (_, n) in enumerate(TILES):
                    s = product()
                    dve.tensor_copy(vtok[0:n, c, :, :], s[0:n, :].rearrange("p (h v) -> p h v", v=P)).then_inc(glue_free, 1)
                released()
                dve.tensor_tensor(ret_vmask[:, :, :], vtok[0:32, 2, 0:1, :].broadcast_to([T_SAMPLE, N_SEQ, P]),
                                  seq_mask[0:32, :, None].broadcast_to([T_SAMPLE, N_SEQ, P]), ALU.mult).then_inc(vmask_ready, 1)
                for c, (_, n) in enumerate(TILES):
                    s = product()
                    dve.tensor_tensor(ktok[0:n, c, :, :], s[0:n, :].rearrange("p (h v) -> p h v", v=P),
                                      key_decay[0:n, c, :, None].broadcast_to([n, RET_HEADS, P]), ALU.mult).then_inc(glue_free, 1)
                for c, (_, n) in enumerate(TILES):
                    s = product()
                    mask = att_decay if n == P else att_decay_s[0:n]
                    dve.tensor_tensor(att[0:n, c, :, 0:n], s[0:n, 0:RET_HEADS * n].rearrange("p (h i) -> p h i", i=n),
                                      mask, ALU.mult).then_inc(glue_free, 1)
                s = product()
                dve.tensor_copy(ret_s1, s.rearrange("p (h v) -> p h v", v=P)).then_inc(glue_free, 1)
                released()
                s = product()
                for hd in range(RET_HEADS):
                    ins = dve.scalar_tensor_tensor(out=ret_s2[:, hd, :], in0=ret_s1[:, hd, :], scalar=float(np.exp(LOG_GAMMA[hd] * P)),
                                                   in1=s[:, hd * P:(hd + 1) * P], op0=ALU.mult, op1=ALU.add)
                ins.then_inc(glue_free, 1)
                for hd in range(RET_HEADS):
                    s = product()
                    dve.tensor_copy(h[:, hd, :], s[:, 0:T]).then_inc(glue_free, 1)
                for hd in range(RET_HEADS):
                    for half_seq in range(2):
                        s = product()
                        st = ret_state[:, 4 * half_seq:4 * half_seq + 4, hd, :]
                        dve.scalar_tensor_tensor(out=st, in0=st, scalar=float(np.exp(LOG_GAMMA[hd] * L_SEQ)),
                                                 in1=s.rearrange("p (q v) -> p q v", v=P), op0=ALU.mult, op1=ALU.add).then_inc(glue_free, 1)
                    if hd + 1 < RET_HEADS:
                        dve.tensor_tensor(ret_vmask[:, :, :], vtok[0:32, 2, hd + 1:hd + 2, :].broadcast_to([T_SAMPLE, N_SEQ, P]),
                                          seq_mask[0:32, :, None].broadcast_to([T_SAMPLE, N_SEQ, P]), ALU.mult).then_inc(vmask_ready, 1)
                released()
                dve.memset(conv_z[:, :, 0:2], 0.0)
                dve.tensor_tensor(conv_z[:, :, 2:], proj0[:, 20:24, 0:T_PROMPT], proj0[:, 24:28, 0:T_PROMPT], ALU.mult)
                for c in range(4):
                    cg = proj0[:, 20 + c, T_PROMPT:T].rearrange("p (s j) -> p s j", j=L_SEQ)
                    xin = proj0[:, 24 + c, T_PROMPT:T].rearrange("p (s j) -> p s j", j=L_SEQ)
                    ins = dve.tensor_tensor(conv_zs[:, c, :, 2:6], cg, xin, ALU.mult)
                link(ins)
                dve.tensor_copy(conv_tail, conv_z[:, :, T_PROMPT:T_PROMPT + 2])
                dve.tensor_copy(conv_tails, conv_zs[:, :, :, 4:6]).then_inc(state_ready, 1)

                def dst(c):
                    return h[:, 4 + c, 0:T_PROMPT], h[:, 4 + c, T_PROMPT:T].rearrange("p (s j) -> p s j", j=L_SEQ)
                for c in range(4):
                    a, b = dst(c)
                    dve.tensor_scalar(a, conv_z[:, c, 0:T_PROMPT], conv_w[:, 0, c:c + 1], None, ALU.mult)
                    ins = dve.tensor_scalar(b, conv_zs[:, c, :, 0:4], conv_w[:, 0, c:c + 1], None, ALU.mult)
                link(ins)
                for w in (1, 2):
                    for c in range(4):
                        a, b = dst(c)
                        dve.scalar_tensor_tensor(out=a, in0=conv_z[:, c, w:w + T_PROMPT], scalar=conv_w[:, w, c:c + 1],
                                                 in1=a, op0=ALU.mult, op1=ALU.add)
                        ins = dve.scalar_tensor_tensor(out=b, in0=conv_zs[:, c, :, w:w + 4], scalar=conv_w[:, w, c:c + 1],
                                                       in1=b, op0=ALU.mult, op1=ALU.add)
                    link(ins)
                link(dve.tensor_tensor(h[:, 4:8, :], h[:, 4:8, :], proj0[:, 16:20, :], ALU.mult))

            def head_norm(heads, mean, gate, gain, k):
                dve.sem_inc(sqo_ready, 1)
                for hd in range(heads):
                    s = product()
                    dve.tensor_scalar(mean[:, hd, :], s[:, 0:T], 1.0 / P, EPS, ALU.mult, ALU.add).then_inc(glue_free, 1)
                released()
                dve.sem_inc(varo_ready, 1)
                dve.wait_ge(stdo_ready, k)
                link(dve.reciprocal(mean, mean))
                o = h[:, 0:heads, :]
                link(dve.tensor_tensor(o, o, mean, ALU.mult))
                link(dve.tensor_tensor(o, o, gate, ALU.mult))
                link(dve.tensor_tensor(o, o, gain[:, :, None].broadcast_to([P, heads, T]), ALU.mult))
                dve.sem_inc(mixer_done, 1)
                dve.sem_inc(h_ready, 1)

            def hgrn():
                dve.wait_ge(hg_tables, 16 * 6)
                dve.wait_ge(lin_free, LINEAR["hg_out"])
                link(dve.tensor_tensor(lbt, bounds[:, 0, :], bounds[:, 1, :], ALU.max))
                dve.tensor_tensor(bounds, bounds, lbt[:, None, :].broadcast_to([P, 2, HG_HEADS]), ALU.subtract).then_inc(bound_in, 1)
                dve.wait_ge(bound_out, 1)
                link(dve.tensor_tensor(lbt, bounds[:, 0, :], bounds[:, 1, :], ALU.add))
                link(dve.reciprocal(lbt, lbt))
                link(dve.tensor_tensor(lb, bounds[:, 1, :], lbt, ALU.mult))
                link(dve.tensor_scalar(one_lb, lb, -1.0, 1.0, ALU.mult, ALU.add))
                for hd in range(HG_HEADS):
                    f = proj1[:, 8 + hd, :]
                    ins = dve.tensor_scalar(f, f, one_lb[:, hd:hd + 1], lb[:, hd:hd + 1], ALU.mult, ALU.add)
                ins.then_inc(keep_ready, 1)
                dve.memset(fac, 0.0)
                dve.wait_ge(log_ready, 1)
                link(dve.tensor_scalar(proj1[:, 8:16, :], proj1[:, 8:16, :], -1.0, 1.0, ALU.mult, ALU.add))
                dve.sem_inc(head_free, 1)
                b = fac[:, 8, :]

                def halves(v, m):
                    n = T_PROMPT if m > 2 else T
                    w = v[:, 0:n].rearrange("p (n m) -> p n m", m=2 * m)
                    return w[:, :, 0:m], w[:, :, m:2 * m], w[:, :, m - 1:m].broadcast_to([P, n // (2 * m), m])

                with dve.Fori(0, HG_HEADS) as i:
                    chained.enter(i, 3)
                    taken.enter(i, 12)
                    link(dve.tensor_tensor_scan(b, restart, logf[:, bass.ds(i, 1), :].rearrange("p a t -> p (a t)"), 0.0, ALU.mult, ALU.add))
                    for lev, m in enumerate(LEVELS):
                        b1, b2, mid = halves(b, m)
                        d1, d2, _ = halves(fac[:, lev, :], m)
                        dve.tensor_tensor(d1, mid, b1, ALU.subtract)
                        dve.tensor_tensor(d2, b2, mid, ALU.subtract)
                    for lo, hi, m in ((0, T_PROMPT, P), (T_PROMPT, T, L_SEQ)):
                        bb = b[:, lo:hi].rearrange("p (n m) -> p n m", m=m)
                        dd = fac[:, 7, lo:hi].rearrange("p (n m) -> p n m", m=m)
                        ins = dve.tensor_tensor(dd, bb[:, :, m - 1:m].broadcast_to([P, (hi - lo) // m, m]), bb, ALU.subtract)
                    ins.then_inc(diff_ready, 1)
                    dve.wait_ge(fac_ready, i + 1)
                    dve.wait_ge(staged, i * 4 + 4)
                    for lev, m in enumerate(LEVELS):
                        f1, f2, _ = halves(fac[:, lev, :], m)
                        k1, _, _ = halves(stage[:, 1, :], m)
                        _, q2, _ = halves(stage[:, 0, :], m)
                        dve.tensor_tensor(f1, f1, k1, ALU.mult)
                        dve.tensor_tensor(f2, f2, q2, ALU.mult)
                    dve.tensor_tensor(fac[:, 7, :], fac[:, 7, :], stage[:, 1, :], ALU.mult)
                    dve.tensor_tensor(qe, fac[:, 8, :], stage[:, 0, :], ALU.mult).then_inc(x_lev_ready, 1)
                    for dst in (h_vtok, h_ktok):
                        s = product()
                        dve.tensor_copy(dst[:, 0:2, :], s[:, 0:2 * P].rearrange("p (c v) -> p c v", v=P))
                        dve.tensor_copy(dst[0:32, 2, :], s[0:32, 2 * P:3 * P]).then_inc(glue_free, 1)
                    released()
                    dve.tensor_tensor(h_vmask[0:32], h_vtok[0:32, 2:3, :].broadcast_to([T_SAMPLE, N_SEQ, P]),
                                      h_seq_mask[0:32, :, None].broadcast_to([T_SAMPLE, N_SEQ, P]), ALU.mult).then_inc(h_vm_ready, 1)
                    for c in range(2):
                        for g in range(2):
                            s = product()
                            dve.tensor_tensor(h_att[:, c, 4 * g:4 * g + 4, :], s.rearrange("p (l i) -> p l i", i=P),
                                              lev_mask[:, 4 * g:4 * g + 4, :], ALU.mult).then_inc(glue_free, 1)
                    s = product()
                    dve.tensor_tensor(h_atts[0:32], s[0:32, 0:96].rearrange("p (l i) -> p l i", i=32), lev_masks[0:32], ALU.mult).then_inc(glue_free, 1)
                    s = product()
                    dve.tensor_copy(h_s1, s[:, 0:P]).then_inc(glue_free, 1)
                    released()
                    dve.sem_inc(h_s1_ready, 1)
                    s = product()
                    dve.scalar_tensor_tensor(out=h_out[:, bass.ds(i, 1), :].rearrange("p a v -> p (a v)"), in0=h_s1, scalar=fac[:, 8, T_PROMPT - 1:T_PROMPT],
                                             in1=s[:, 0:P], op0=ALU.mult, op1=ALU.add).then_inc(glue_free, 1)
                    s = product()
                    dve.tensor_copy(h[:, bass.ds(i, 1), :].rearrange("p a t -> p (a t)"), s[:, 0:T]).then_inc(glue_free, 1)
                    st = hg_states[:, bass.ds(i, 1), :, :].rearrange("p a s v -> p (a s) v")
                    last = fac[:, 8, T_PROMPT:T].rearrange("p (s j) -> p s j", j=L_SEQ)[:, :, L_SEQ - 1:L_SEQ]
                    link(dve.tensor_tensor(st, s0_stage, last.broadcast_to([P, N_SEQ, P]), ALU.mult))
                    for g in range(2):
                        s = product()
                        half_st = hg_states[:, bass.ds(i, 1), 4 * g:4 * g + 4, :].rearrange("p a s v -> p (a s) v")
                        dve.tensor_tensor(half_st, half_st, s.rearrange("p (q v) -> p q v", v=P), ALU.add).then_inc(glue_free, 1)
                    released()
                    link(dve.memset(fac[:, 0:5, T_PROMPT:T], 0.0))
                    dve.sem_inc(head_free, 1)
                chained.leave(HG_HEADS)
                taken.leave(HG_HEADS)
                dve.sem_inc(state_ready, 1)

            def topk(l):
                for c, (_, n) in enumerate(TILES):
                    for g in range(4):
                        s = product()
                        dve.tensor_copy(score[0:n, c, 4 * g:4 * g + 4, :], s[0:n, :].rearrange("p (l k) -> p l k", k=P)).then_inc(glue_free, 1)
                released()
                for c, (_, n) in enumerate(TILES):
                    sc, sc2 = score[0:n, c], score2[0:n]
                    for j in range(LISTS):
                        ins = dve.max(topv[0:n, j, 0:8], sc[:, j, :])
                    link(ins)
                    for j in range(LISTS):
                        dve.max_index(topi_u[0:n, j, 0:8], topv[0:n, j, 0:8], sc[:, j, :])
                        ins = dve.match_replace(sc2[:, j, :], topv[0:n, j, 0:8], sc[:, j, :], LOWEST)
                    link(ins)
                    for j in range(LISTS):
                        ins = dve.max(topv[0:n, j, 8:16], sc2[:, j, :])
                    link(ins)
                    for j in range(LISTS):
                        ins = dve.max_index(topi_u[0:n, j, 8:16], topv[0:n, j, 8:16], sc2[:, j, :])
                    link(ins)
                    dve.tensor_copy(topi[0:n], topi_u[0:n])
                    tv = topv[0:n].rearrange("p (h q) k -> p h q k", q=2)
                    for hd in range(PEER_HEADS):
                        ins = dve.tensor_tensor(comb[0:n, hd, :].rearrange("p (a b) -> p a b", b=TOPK),
                                                tv[:, hd, 0, :, None].broadcast_to([n, TOPK, TOPK]),
                                                tv[:, hd, 1:2, :].broadcast_to([n, TOPK, TOPK]), ALU.add)
                    link(ins)
                    for hd in range(PEER_HEADS):
                        ins = dve.max(best[0:n, hd, 0:8], comb[0:n, hd, :])
                    link(ins)
                    for hd in range(PEER_HEADS):
                        dve.max_index(pos_u[0:n, hd, 0:8], best[0:n, hd, 0:8], comb[0:n, hd, :])
                        ins = dve.match_replace(comb2[0:n, hd, :], best[0:n, hd, 0:8], comb[0:n, hd, :], LOWEST)
                    link(ins)
                    for hd in range(PEER_HEADS):
                        ins = dve.max(best[0:n, hd, 8:16], comb2[0:n, hd, :])
                    link(ins)
                    for hd in range(PEER_HEADS):
                        ins = dve.max_index(pos_u[0:n, hd, 8:16], best[0:n, hd, 8:16], comb2[0:n, hd, :])
                    link(ins)
                    link(dve.tensor_copy(norm_s[0:n], best[0:n, :, 0]))
                    dve.tensor_tensor(best[0:n], best[0:n], norm_s[0:n, :, None].broadcast_to([n, PEER_HEADS, TOPK]),
                                      ALU.subtract).then_inc(shifted, 1)
                    pu = pos_u[0:n].rearrange("p h k -> p (h k)")
                    dve.tensor_single_scalar(half_u[0:n, 0, :], pu, 4, ALU.logical_shift_right)
                    link(dve.tensor_single_scalar(half_u[0:n, 1, :], pu, 15, ALU.bitwise_and))
                    link(dve.tensor_copy(half[0:n], half_u[0:n]))
                    ti = topi[0:n].rearrange("p (h q) k -> p h q k", q=2)
                    for q in range(2):
                        link(dve.tensor_tensor(eq[0:n], half[0:n, q, :, None].broadcast_to([n, P, TOPK]),
                                               iota[0:n, None, 0:TOPK].broadcast_to([n, P, TOPK]), ALU.is_equal))
                        for hd in range(PEER_HEADS):
                            e = eq[0:n, TOPK * hd:TOPK * hd + TOPK, :]
                            ins = dve.tensor_tensor(e, e, ti[:, hd, q:q + 1, :].broadcast_to([n, TOPK, TOPK]), ALU.mult)
                        link(ins)
                        link(dve.tensor_reduce(pick[0:n, c, q, :], eq[0:n], AX.X, ALU.add))
                    dve.wait_ge(exped, 3 * l + c + 1)
                    link(dve.tensor_reduce(norm_s[0:n], best[0:n], AX.X, ALU.add))
                    link(dve.reciprocal(norm_s[0:n], norm_s[0:n]))
                    ins = dve.tensor_tensor(pick[0:n, c, 2, :].rearrange("p (h k) -> p h k", k=TOPK), best[0:n],
                                            norm_s[0:n, :, None].broadcast_to([n, PEER_HEADS, TOPK]), ALU.mult)
                    ins.then_inc(picks_ready, 1)
                for c, (t0, n) in enumerate(TILES):
                    s = product()
                    dve.tensor_copy(choice[:, :, t0:t0 + n], s[:, 0:3 * P].rearrange("p (q i) -> p q i", i=P)[:, :, 0:n]).then_inc(glue_free, 1)
                released()

            def one_hots(l):
                def step(i, j):
                    tok = i * 8 + j
                    if not (l == 0 and isinstance(i, int) and tok < 4):
                        dve.wait_ge(onehot_used, tok + (T * l - 3))
                    sl = j % 4
                    dve.tensor_scalar(onehot[:, sl, 0, :], iota[:], choice[:, 0, bass.ds(tok, 1)], choice[:, 2, bass.ds(tok, 1)],
                                      ALU.is_equal, ALU.mult)
                    dve.tensor_scalar(onehot[:, sl, 1, :], iota[:], choice[:, 1, bass.ds(tok, 1)], None,
                                      ALU.is_equal).then_inc(onehot_ready, 1)
                if l == 0:
                    for j in range(8):
                        step(0, j)
                with dve.Fori(1 if l == 0 else 0, T // 8) as i:
                    for j in range(8):
                        step(i, j)

            def peer(l):
                norm(2 * l + 1)
                low_input(3 * l + 3)
                only_split(f"wq{l}")
                dve.wait_ge(state_stored, 64 if l == 0 else 96)
                topk(l)
                one_hots(l)

                def expert_in(i, s):
                    split_low(f"u{l}", i, s)
                    dve.wait_ge(gelu_ready, i * 4 + (EXP * l + s + 1))
                    if isinstance(i, int) and i == 0 and s == 0:
                        dve.wait_ge(gates_out, (T // 4) * (l + 1))
                    g = gates[:, bass.ds(i * 4 + s, 1), :].rearrange("p a t -> p (a t)")
                    dve.tensor_tensor(g, g, gelu_out[s % 2], ALU.mult).then_inc(w_ready, 1)
                section(dve, f"u{l}", expert_in, first=True)

                def weight_low(e, slot):
                    dve.tensor_tensor(hs[:, 1, slot, :], gates[:, bass.ds(e, 1), :].rearrange("p a t -> p (a t)"),
                                      hs[:, 0, slot, :].bitcast(F32), ALU.subtract).then_inc(w_low, 1)

                dve.wait_ge(w_high, EXP * l + 1)
                weight_low(0, 0)

                def expert_out(i, s):
                    if isinstance(i, int) and 4 * i + s == EXP - 1:
                        if l == 0:
                            split_low(f"v{l}", i, s)
                        return
                    split_low(f"v{l}", i, s)
                    dve.wait_ge(w_high, i * 4 + (EXP * l + s + 2))
                    weight_low(i * 4 + (s + 1), (s + 1) % 2)
                section(dve, f"v{l}", expert_out, last=True)
                dve.wait_ge(block_done, FIRST[f"v{l}"] + EXP)
                dve.wait_ge(x_back, 16 * (l + 1))
                for k in range(KC):
                    chained.count()
                    ins = add_to_x(k, True, ps[:, k, :], 40, chain, chained.at())
                    link(ins)
                dve.sem_inc(x_ready, 1)

            dve.wait_ge(high_ready, 1)
            dve.tensor_tensor(spl[:, 0, 1, :], raw[:, 0, :], spl[:, 0, 0, :].bitcast(F32), ALU.subtract).then_inc(low_ready, 1)
            dve.wait_ge(c_high, 1)
            dve.tensor_tensor(cs[:, 1, :, :], c_in, cs[:, 0, :, :].bitcast(F32), ALU.subtract).then_inc(c_low, 1)
            ada(0)
            norm(0)
            low_input(1)
            only_split("ab_in")
            retention()
            head_norm(RET_HEADS, roped[:, 0:RET_HEADS, :], proj0[:, 12:16, :], ret_gain, 1)
            low_input(2)
            project_out("ab_out", 16)
            peer(0)
            ada(1)
            norm(2)
            low_input(4)
            only_split("hg_in")
            hgrn()
            head_norm(HG_HEADS, proj1[:, 8:16, :], proj1[:, 24:32, :], hg_gain, 2)
            low_input(5)
            project_out("hg_out", 16)
            peer(1)
            mean_root(4)
            link(dve.tensor_tensor(h, x, rstd[:, None, :].broadcast_to([P, KC, T]), ALU.mult))
            dve.tensor_tensor(h, h, final_gain[:, :, None].broadcast_to([P, KC, T]), ALU.mult).then_inc(y_ready, 1)

        @block.tensor
        def _(pe):
            made = Tally()

            def bank():
                n = 2 + made.static() % 4
                if made.static() >= 4 or made.i is not None:
                    pe.wait_ge(glue_free, made.at(-3))
                made.count()
                return ps[:, n, :]

            def three(out, slot, cols, high, low, start, stop):
                pe.matmul(out, spl[:, slot, 0, cols], high, start=start, stop=False, skip_group_check=True)
                pe.matmul(out, spl[:, slot, 0, cols], low, start=False, stop=False, skip_group_check=True)
                return pe.matmul(out, spl[:, slot, 1, cols], high, start=False, stop=stop, skip_group_check=True)

            def linear(name, src, n, first=False, read=lin_free, read_before=None):
                m0 = LINEAR[name] if read_before is None else read_before

                def step(i, s):
                    pe.wait_ge(low_ready, i * 4 + (FIRST[name] + s + 1))
                    if not (isinstance(i, int) and 4 * i + m0 + s < 2):
                        pe.wait_ge(read, i * 4 + (m0 + s - 1))
                    for k in range(KC):
                        ins = three(ps[:, s % 2, 0:n], s % 2, slice(k * P, k * P + P), src[:, 0, k, 0:n], src[:, 1, k, 0:n],
                                    k == 0, k == KC - 1)
                    ins.then_inc(block_done, 1)
                section(pe, name, step, first=first)

            def sum_squares(src, j):
                pe.wait_ge(sq_ready, j + 1)
                s = bank()
                for k in range(KC):
                    ins = pe.matmul(s[:, 0:T], ones[:], src[:, k, :], start=k == 0, stop=k == KC - 1)
                ins.then_inc(glue_full, 1)

            def head_squares(heads, src, k):
                pe.wait_ge(sqo_ready, k)
                for hd in range(heads):
                    s = bank()
                    pe.matmul(s[:, 0:T], ones[:], src[:, hd, :], start=True, stop=True).then_inc(glue_full, 1)

            def retention():
                pe.wait_ge(ret_tables, 16 * 10)
                pe.wait_ge(lin_free, LINEAR["ab_out"])
                for c in range(2 * RET_HEADS):
                    s = bank()
                    pe.matmul(s[:, 0:T], swap, proj0[:, c, :], start=True, stop=True).then_inc(glue_full, 1)
                for t0, n in TILES:
                    s = bank()
                    for hd in range(RET_HEADS):
                        ins = pe.transpose(s[0:n, hd * P:hd * P + P], proj0[:, 8 + hd, t0:t0 + n], ident[:])
                    ins.then_inc(glue_full, 1)
                pe.wait_ge(roped_ready, 1)
                for t0, n in TILES:
                    s = bank()
                    for hd in range(RET_HEADS):
                        ins = pe.transpose(s[0:n, hd * P:hd * P + P], roped[:, 4 + hd, t0:t0 + n], ident[:])
                    ins.then_inc(glue_full, 1)
                for t0, n in TILES:
                    s = bank()
                    for hd in range(RET_HEADS):
                        ins = pe.matmul(s[0:n, hd * n:hd * n + n], roped[:, 4 + hd, t0:t0 + n], roped[:, hd, t0:t0 + n], start=True, stop=True)
                    ins.then_inc(glue_full, 1)
                pe.wait_ge(glue_free, made.at(-3))
                for c in range(2):
                    s = bank()
                    for hd in range(RET_HEADS):
                        ins = pe.matmul(s[:, hd * P:hd * P + P], ktok[:, c, hd, :], vtok[:, c, hd, :], start=True, stop=True)
                    ins.then_inc(glue_full, 1)
                pe.wait_ge(qd_ready, 1)
                pe.wait_ge(glue_free, made.at(-1))
                for hd in range(RET_HEADS):
                    s = bank()
                    for c in range(2):
                        pe.matmul(s[:, c * P:c * P + P], vtok[:, c, hd, :], att[:, c, hd, :], start=True, stop=c == 0, skip_group_check=True)
                    pe.matmul(s[:, P:2 * P], ret_s1[:, hd, :], qd[:, hd, P:2 * P], start=False, stop=True, skip_group_check=True)
                    pe.matmul(s[:, T_PROMPT:T], vtok[0:32, 2, hd, :], att[0:32, 2, hd, 0:32], start=True, stop=False, skip_group_check=True)
                    for q in range(N_SEQ):
                        lo = T_PROMPT + L_SEQ * q
                        ins = pe.matmul(s[:, lo:lo + L_SEQ], ret_state[:, q, hd, :], qd[:, hd, lo:lo + L_SEQ],
                                        start=False, stop=q == N_SEQ - 1, skip_group_check=True)
                    ins.then_inc(glue_full, 1)
                for hd in range(RET_HEADS):
                    pe.wait_ge(vmask_ready, hd + 1)
                    for g in range(2):
                        s = bank()
                        pe.matmul(s, ktok[0:32, 2, hd, :], ret_vmask[:, 4 * g:4 * g + 4, :], start=True, stop=True).then_inc(glue_full, 1)

            def hgrn():
                pe.wait_ge(hg_tables, 16 * 6)
                with pe.Fori(0, HG_HEADS) as i:
                    made.enter(i, 12)
                    pe.wait_ge(staged, i * 4 + 4)
                    s = bank()
                    for c, (t0, n) in enumerate(TILES):
                        ins = pe.transpose(s[0:n, c * P:c * P + P], stage[:, 2, t0:t0 + n], ident[:])
                    ins.then_inc(glue_full, 1)
                    pe.wait_ge(x_lev_ready, i + 1)
                    s = bank()
                    for c, (t0, n) in enumerate(TILES):
                        ins = pe.transpose(s[0:n, c * P:c * P + P], fac[:, 7, t0:t0 + n], ident[:])
                    ins.then_inc(glue_full, 1)
                    for c in range(2):
                        cols = slice(c * P, c * P + P)
                        for g in range(2):
                            s = bank()
                            for lev in range(4 * g, 4 * g + 4):
                                a, b = (fac[:, lev, cols],) * 2 if lev < N_LEV else (stage[:, 1, cols], stage[:, 0, cols])
                                lo = (lev - 4 * g) * P
                                ins = pe.matmul(s[:, lo:lo + P], a, b, start=True, stop=True)
                            ins.then_inc(glue_full, 1)
                    s = bank()
                    for k, lev in enumerate((5, 6, 7)):
                        cols = slice(T_PROMPT, T)
                        a, b = (fac[:, lev, cols],) * 2 if lev < N_LEV else (stage[:, 1, cols], stage[:, 0, cols])
                        ins = pe.matmul(s[0:32, 32 * k:32 * k + 32], a, b, start=True, stop=True)
                    ins.then_inc(glue_full, 1)
                    for c in range(2):
                        s = bank()
                        pe.matmul(s[:, 0:P], h_ktok[:, c, :], h_vtok[:, c, :], start=True, stop=True).then_inc(glue_full, 1)
                    s = bank()
                    pe.wait_ge(h_s1_ready, i + 1)
                    for c in range(2):
                        for lev in range(8):
                            pe.matmul(s[:, c * P:c * P + P], h_vtok[:, c, :], h_att[:, c, lev, :], start=lev == 0,
                                      stop=lev == 7 and c == 0, skip_group_check=True)
                    pe.matmul(s[:, P:2 * P], h_s1, qe[:, P:2 * P], start=False, stop=True, skip_group_check=True)
                    for lev in range(3):
                        pe.matmul(s[:, T_PROMPT:T], h_vtok[0:32, 2, :], h_atts[0:32, lev, :], start=lev == 0, stop=False, skip_group_check=True)
                    for q in range(N_SEQ):
                        lo = T_PROMPT + L_SEQ * q
                        ins = pe.matmul(s[:, lo:lo + L_SEQ], s0_stage[:, q, :], qe[:, lo:lo + L_SEQ],
                                        start=False, stop=q == N_SEQ - 1, skip_group_check=True)
                    ins.then_inc(glue_full, 1)
                    pe.wait_ge(h_vm_ready, i + 1)
                    for g in range(2):
                        s = bank()
                        pe.matmul(s, h_ktok[0:32, 2, :], h_vmask[0:32, 4 * g:4 * g + 4, :], start=True, stop=True).then_inc(glue_full, 1)
                made.leave(HG_HEADS)

            def peer(l):
                sum_squares(h, 2 * l + 1)
                pe.wait_ge(h_low, 3 * l + 3)
                linear(f"wq{l}", hs, T)
                pe.wait_ge(lin_free, LINEAR[f"wq{l}"] + WQ)
                pe.wait_ge(keys_landed, 16 * (l + 1))
                for t0, n in TILES:
                    for g in range(4):
                        s = bank()
                        for j in range(4 * g, 4 * g + 4):
                            lo = (j - 4 * g) * P
                            ins = pe.matmul(s[0:n, lo:lo + P], query[:, j, t0:t0 + n], keys[:, j, :], start=True, stop=True)
                        ins.then_inc(glue_full, 1)
                for c, (t0, n) in enumerate(TILES):
                    pe.wait_ge(picks_ready, 3 * l + c + 1)
                    s = bank()
                    for q in range(3):
                        ins = pe.transpose(s[:, q * P:q * P + n], pick[0:n, c, q, :], ident[0:n, 0:n])
                    ins.then_inc(glue_full, 1)

                def token_group(i, g):
                    if not (l == 0 and isinstance(i, int)):
                        pe.wait_ge(gates_out, i * 2 + ((T // 4) * l + g - 1))
                    for j in range(4):
                        pe.wait_ge(onehot_ready, i * 8 + (T * l + 4 * g + j + 1))
                        pe.matmul(ps[:, 6 + g, j * P:j * P + P], onehot[:, j, 0, :], onehot[:, j, 1, :],
                                  start=True, stop=True).then_inc(onehot_used, 1)
                if l == 0:
                    token_group(0, 0)
                    token_group(0, 1)
                with pe.Fori(1 if l == 0 else 0, T // 8) as i:
                    for g in range(2):
                        token_group(i, g)

                linear(f"u{l}", hs, T, first=l == 0, read=gelu_ready, read_before=EXP * l)
                pe.wait_ge(gelu_ready, EXP * (l + 1))
                pe.wait_ge(gates_out, (T // 4) * (l + 1))
                pe.wait_ge(glue_free, made.at())

                def expert_out(i, s):
                    e = 4 * i + s if isinstance(i, int) else None
                    pe.wait_ge(low_ready, i * 4 + (FIRST[f"v{l}"] + s + 1))
                    pe.wait_ge(w_low, i * 4 + (EXP * l + s + 1))
                    for k in range(KC):
                        ins = three(ps[:, k, 0:T], s % 2, slice(k * P, k * P + P), hs[:, 0, s % 2, :], hs[:, 1, s % 2, :],
                                    e == 0, e == EXP - 1)
                    ins.then_inc(block_done, 1)
                section(pe, f"v{l}", expert_out, first=True, last=True)
                pe.wait_ge(x_ready, 2 * l + 2)

            pe.wait_ge(const_landed, 16 * 7)
            pe.wait_ge(c_low, 1)
            linear("ada0", cs, NS, first=True)
            sum_squares(h, 0)
            pe.wait_ge(h_low, 1)
            linear("ab_in", hs, T)
            retention()
            head_squares(RET_HEADS, swapped, 2)
            pe.wait_ge(h_low, 2)
            linear("ab_out", hs, T)
            peer(0)
            linear("ada1", cs, NS)
            sum_squares(h, 2)
            pe.wait_ge(h_low, 4)
            linear("hg_in", hs, T)
            hgrn()
            head_squares(HG_HEADS, logf, 4)
            pe.wait_ge(h_low, 5)
            linear("hg_out", hs, T)
            peer(1)
            sum_squares(h, 4)


def tables():
    f = np.float32
    half = P // 2
    inv = (1.0 / (f(10000.0) ** np.linspace(0.0, 1.0, half, dtype=f))).astype(f)
    step = np.concatenate([np.arange(T_PROMPT), np.tile(np.arange(L_SEQ), N_SEQ) + PAST_LEN]).astype(f)
    ang = (step[:, None] * inv[None, :]).astype(f)
    cos, sin = np.cos(ang).T, np.sin(ang).T
    rows = np.arange(P)
    swap = (rows[:, None] == (rows[None, :] + half) % P).astype(f)
    in_chunk = np.concatenate([np.arange(T_PROMPT) % P, np.tile(np.arange(L_SEQ), N_SEQ)])
    lg = LOG_GAMMA
    q_decay = np.broadcast_to(np.exp(lg[:, None] * (in_chunk + 1.0))[None], (P, RET_HEADS, T)).astype(f)
    rel = rows[None, :] - rows[:, None]
    att = (np.where(rel >= 0, np.exp(lg[:, None, None] * np.maximum(rel, 0)), 0.0) * SCALE).transpose(1, 0, 2).astype(f)
    same = (rows[:32, None] // L_SEQ == rows[None, :32] // L_SEQ)
    att_s = (np.where((rel[:32, :32] >= 0) & same, np.exp(lg[:, None, None] * np.maximum(rel[:32, :32], 0)), 0.0) * SCALE)
    key = np.zeros((P, 3, RET_HEADS))
    key[:, 0:2] = (np.exp(lg[None, :] * (P - 1.0 - rows[:, None])) * SCALE)[:, None, :]
    key[:32, 2] = np.exp(lg[None, :] * (L_SEQ - 1.0 - rows[:32, None] % L_SEQ)) * SCALE
    seq_mask = (rows[:32, None] // L_SEQ == np.arange(N_SEQ)[None, :]).astype(f)
    restart = np.broadcast_to((in_chunk != 0).astype(f), (P, T)).copy()
    lev = np.zeros((P, 8, P), f)
    for n, m in enumerate(LEVELS):
        lev[:, n] = (rows[:, None] // (2 * m) == rows[None, :] // (2 * m)) & (rows[:, None] % (2 * m) < m) & (rows[None, :] % (2 * m) >= m)
    lev[:, 7] = np.eye(P)
    return {
        "ident": np.eye(P, dtype=f), "ones": np.ones((P, P), f), "iota": np.broadcast_to(np.arange(P, dtype=f), (P, P)).copy(),
        "cos": np.concatenate([cos, cos]).astype(f), "sin": np.concatenate([-sin, sin]).astype(f), "swap": swap,
        "q_decay": q_decay.copy(), "att_decay": att.copy(), "att_decay_s": att_s.transpose(1, 0, 2).astype(f).copy(),
        "key_decay": key.astype(f), "seq_mask": seq_mask, "restart": restart, "lev_mask": lev,
        "lev_masks": lev[:32, 5:8, :32].copy(),
    }


def kernel(x_prompt, x_sample, state_ret, state_conv, state_hgrn, c_prompt, c_sample,
           ada_w, ada_b, norm_mix_g, norm_ffn_g, ab_w_in, ret_norm_g, conv_w, ab_w_out,
           hg_w_in, hg_lower_bounds, hg_norm_g, hg_w_out, peer_wq, peer_keys, peer_u, peer_v,
           final_norm_g):
    import concourse.bacc as bacc
    from concourse.bass_utils import run_bass_kernel_spmd as run

    def blocks(w):
        w = np.asarray(w)
        lead, n = w.shape[:-2], w.shape[-1] // P
        w = w.reshape(*lead, KC, P, n, P)
        k = len(lead)
        return np.ascontiguousarray(w.transpose(*range(k), k + 2, k + 1, k, k + 3)).reshape(*lead, n, P, D_MODEL)

    def columns(v):
        v = np.asarray(v)
        return np.ascontiguousarray(np.moveaxis(v.reshape(*v.shape[:-1], -1, P), -1, 0))

    xt = np.concatenate([np.asarray(x_prompt)[0], np.asarray(x_sample).reshape(T_SAMPLE, D_MODEL)])
    c = np.concatenate([np.asarray(c_prompt), np.asarray(c_sample), np.asarray(c_sample)[-1:]])
    u = np.asarray(peer_u).reshape(LAYERS, N_KEYS, N_KEYS, KC, P)
    gains = np.concatenate([np.asarray(ret_norm_g)[0].T, np.asarray(hg_norm_g)[0].T,
                            np.asarray(conv_w)[0].reshape(3, 4, P).transpose(2, 0, 1).reshape(P, 12),
                            np.asarray(final_norm_g).reshape(KC, P).T], axis=1)
    norm_g = np.stack([np.asarray(norm_mix_g)[0], np.asarray(norm_ffn_g)[0], np.asarray(norm_mix_g)[1], np.asarray(norm_ffn_g)[1]])
    ins = {
        "x": xt.T.reshape(KC, P, T).transpose(1, 0, 2),
        "c": c.T.reshape(KC, P, NS).transpose(1, 0, 2),
        "state_ret": np.asarray(state_ret)[0].transpose(2, 0, 1, 3),
        "state_conv": np.asarray(state_conv)[0].reshape(N_SEQ, 2, 4, P).transpose(3, 2, 0, 1),
        "state_hgrn": np.asarray(state_hgrn)[0].transpose(2, 1, 0, 3),
        "ada_w": blocks(ada_w), "ada_b": columns(ada_b), "norm_g": columns(norm_g), "gains": gains,
        "ab_w_in": blocks(np.asarray(ab_w_in)[0]), "ab_w_out": blocks(np.asarray(ab_w_out)[0]),
        "hg_w_in": blocks(np.asarray(hg_w_in)[0]), "hg_w_out": blocks(np.asarray(hg_w_out)[0]),
        "bounds": columns(hg_lower_bounds),
        "peer_wq": blocks(peer_wq),
        "peer_keys": np.asarray(peer_keys).reshape(LAYERS, LISTS, N_KEYS, P).transpose(0, 3, 1, 2),
        "peer_u": u.transpose(0, 2, 4, 3, 1).reshape(LAYERS, N_KEYS, P, D_MODEL),
        "peer_v": np.asarray(peer_v).reshape(LAYERS, N_KEYS, N_KEYS, D_MODEL).transpose(0, 2, 1, 3),
    }
    ins.update(tables())
    outs = {"y": (P, KC, T), "ret_p": (P, RET_HEADS, P), "ret_s": (P, N_SEQ, RET_HEADS, P), "conv_p": (P, 4, 2),
            "conv_s": (P, 4, N_SEQ, 2), "hg_p": (P, HG_HEADS, P), "hg_s": (P, HG_HEADS, N_SEQ, P)}
    nc = bacc.Bacc("TRN2", target_bir_lowering=False, num_devices=1)
    arrays, t = {}, {}
    for name, a in ins.items():
        arrays[f"in_{name}"] = np.ascontiguousarray(a)
        t[name] = nc.dram_tensor(f"in_{name}", a.shape, F32, kind="ExternalInput").ap()
    for name, shape in outs.items():
        t[name] = nc.dram_tensor(f"out_{name}", shape, F32, kind="ExternalOutput").ap()
    t["x_spill"] = nc.dram_tensor("x_spill", (P, KC, T), F32, kind="Internal").ap()
    trunk(nc, t)
    r = run(nc, [arrays], core_ids=[0]).results[0]
    y = np.asarray(r["out_y"]).transpose(2, 1, 0).reshape(T, D_MODEL)
    return (y[:T_PROMPT][None], y[T_PROMPT:].reshape(N_SEQ, L_SEQ, D_MODEL),
            np.asarray(r["out_ret_p"]).transpose(1, 0, 2)[None, None],
            np.asarray(r["out_conv_p"]).transpose(2, 1, 0).reshape(1, 1, 2, 512),
            np.asarray(r["out_hg_p"]).transpose(1, 0, 2)[None, None],
            np.asarray(r["out_ret_s"]).transpose(1, 2, 0, 3)[None],
            np.asarray(r["out_conv_s"]).transpose(2, 3, 1, 0).reshape(1, N_SEQ, 2, 512),
            np.asarray(r["out_hg_s"]).transpose(2, 1, 0, 3)[None])
```

```python
from contextlib import ExitStack

import numpy as np
import concourse.bass as bass
from concourse import mybir

F32 = mybir.dt.float32
F32R = mybir.dt.float32r
U32 = mybir.dt.uint32
ALU = mybir.AluOpType
ACT = mybir.ActivationFunctionType
AX = mybir.AxisListType

P = 128
D_MODEL = 1024
KC = D_MODEL // P
T_PROMPT = 256
N_SEQ, L_SEQ = 8, 4
T_SAMPLE = N_SEQ * L_SEQ
T = T_PROMPT + T_SAMPLE
PAST_LEN = 2048
LAYERS = 2
RET_HEADS = 4
HG_HEADS = 8
PEER_HEADS = 8
TOPK = 16
N_KEYS = 128
LISTS = 2 * PEER_HEADS
EPS = 1e-6
LOWEST = -3.0e38
NS = N_SEQ + 2
TILES = [(0, P), (P, P), (T_PROMPT, T_SAMPLE)]
LEVELS = [64, 32, 16, 8, 4, 2, 1]
N_LEV = len(LEVELS)
SCALE = float(P) ** -0.5

RING = 4
HALF = D_MODEL // 2
ADA, AB_IN, OUT, WQ, EXP, HG_IN = 48, 28, 8, 16, 128, 32
ROWS = 512
SECTIONS = [("ada0a", 16), ("ab_in", AB_IN), ("ada0b", 32), ("ab_out", OUT), ("wq0", WQ), ("u0", EXP), ("ada1", ADA),
            ("v0", EXP), ("hg_in", HG_IN), ("hg_out", OUT), ("wq1", WQ), ("u1", EXP), ("v1", EXP)]
COUNT = dict(SECTIONS)
FIRST, SPLIT, LINEAR = {}, {}, {}
_n = _b = _m = 0
for _name, _count in SECTIONS:
    FIRST[_name], SPLIT[_name], LINEAR[_name] = _n, _b, _m
    _n += _count
    _b += 0 if _name.startswith("ada") else _count
    _m += 0 if _name[0] in "uv" or _name.startswith("ada") else _count
FOLLOWED = {"ab_out": "wq0", "wq0": "u0", "v0": "hg_in", "hg_in": "hg_out", "hg_out": "wq1", "wq1": "u1", "u1": "v1"}
TOKENS = 24

LOG_GAMMA = np.log(1.0 - 2.0 ** (-5.0 - np.arange(RET_HEADS)))


class Tally:

    def __init__(self):
        self.base = self.local = self.per = 0
        self.i = None

    def enter(self, i, per):
        self.base, self.local, self.i, self.per = self.base + self.local, 0, i, per

    def leave(self, times):
        assert self.local == self.per
        self.base, self.local, self.i = self.base + self.per * times, 0, None

    def count(self):
        self.local += 1

    def static(self):
        return self.base + self.local

    def at(self, more=0):
        v = self.base + self.local + more
        return v if self.i is None else self.i * self.per + v


def trunk(nc, t):
    with ExitStack() as ctx:
        def sb(name, shape, dt=F32):
            return ctx.enter_context(nc.sbuf_tensor(name, shape, dt))

        def sem(name):
            return ctx.enter_context(nc.semaphore(name))

        big = sb("big", [P, N_KEYS * T])
        hs = sb("hs", [P, 2, KC, T], F32R)
        raw = sb("raw", [P, RING, D_MODEL])
        spl = sb("spl", [P, 2, 2, D_MODEL], F32R)
        mod = sb("mod", [P, ADA, NS])
        cs = sb("cs", [P, KC, NS])
        choice = sb("choice", [P, 3, T])
        onehot = sb("onehot", [P, 8, P])
        ident = sb("ident", [P, P])
        ones = sb("ones", [P, P])
        iota = sb("iota", [P, P])
        rstd = sb("rstd", [P, T])
        small = sb("small", [P, 96])
        ps = ctx.enter_context(nc.psum_tensor("ps", [P, 8, 512], F32))

        onehot_flat = onehot[:].rearrange("p a b -> p (a b)")
        cond_rows = rstd[0:NS, 0:ROWS // 2]
        best_of = [rstd[:, P * c:P * c + w].rearrange("p (h k) -> p h k", k=TOPK) for c, w in enumerate((P, P, 32))]
        pick_of = [onehot_flat[:, 3 * P * c:3 * P * c + 3 * w].rearrange("p (q i) -> p q i", q=3) for c, w in enumerate((P, P, 32))]
        samp_tmp = small[:, 0:32].rearrange("p (s j) -> p s j", j=L_SEQ)
        apart, seconds = (hs[:].rearrange("p a b c -> p (a b c)")[:, 8 * P * w:8 * P * w + 8 * P].rearrange("p (s j e) -> p s j e", s=2, j=4)
                          for w in range(2))
        ret_gain = small[:, 32:36]
        hg_gain = small[:, 36:44]
        conv_w = small[:, 44:56].rearrange("p (w c) -> p w c", c=4)
        final_gain = small[:, 56:64]

        class Region:
            def __init__(self, start):
                self.at = start

            def take(self, *shape):
                n = int(np.prod(shape))
                v = big[:, self.at:self.at + n]
                self.at += n
                assert self.at <= N_KEYS * T, self.at
                names = " ".join("abcde"[:len(shape)])
                if len(shape) == 1:
                    return v
                sizes = {"abcde"[k]: shape[k] for k in range(1, len(shape))}
                return v.rearrange(f"p ({names}) -> p {names}", **sizes)

        base = Region(0)
        x = base.take(KC, T)
        h = base.take(KC, T)
        after_h = base.at

        r0 = Region(after_h)
        proj0 = r0.take(AB_IN, T)
        cos_t = r0.take(T)
        sin_t = r0.take(T)
        swap = r0.take(P)
        q_decay = r0.take(RET_HEADS, T)
        att_decay = r0.take(RET_HEADS, P)
        att_decay_s = r0.take(RET_HEADS, T_SAMPLE)
        key_decay = r0.take(3, RET_HEADS)
        seq_mask = r0.take(N_SEQ)
        roped = r0.take(2 * RET_HEADS, T)
        swapped = r0.take(2 * RET_HEADS, T)
        qd = r0.take(RET_HEADS, T)
        vtok = r0.take(3, RET_HEADS, P)
        ktok = r0.take(3, RET_HEADS, P)
        att = r0.take(3, RET_HEADS, P)
        ret_s1 = r0.take(RET_HEADS, P)
        ret_s2 = r0.take(RET_HEADS, P)
        ret_state = r0.take(N_SEQ, RET_HEADS, P)
        conv_z = r0.take(4, T_PROMPT + 2)
        conv_zs = r0.take(4, N_SEQ, L_SEQ + 2)
        conv_tail = r0.take(4, 2)
        conv_tails = r0.take(4, N_SEQ, 2)
        ret_vmask = swapped.rearrange("p a b -> p (a b)")[0:T_SAMPLE, 0:1024].rearrange("p (s v) -> p s v", v=P)

        r1 = Region(after_h)
        proj1 = r1.take(HG_IN, T)
        logf = r1.take(HG_HEADS, T)
        restart = r1.take(T)
        fac = r1.take(N_LEV + 2, T)
        qe = r1.take(T)
        stage = r1.take(3, T)
        h_vtok = r1.take(3, P)
        h_ktok = r1.take(3, P)
        h_att = r1.take(2, 8, P)
        h_atts = r1.take(3, T_SAMPLE)
        h_vmask = r1.take(N_SEQ, P)
        lev_mask = r1.take(8, P)
        lev_masks = r1.take(3, T_SAMPLE)
        h_seq_mask = r1.take(N_SEQ)
        h_s1 = r1.take(P)
        h_out = r1.take(HG_HEADS, P)
        hg_states = r1.take(HG_HEADS, N_SEQ, P)
        s0_stage = r1.take(N_SEQ, P)
        bounds = r1.take(2, HG_HEADS)
        lb = r1.take(HG_HEADS)
        one_lb = r1.take(HG_HEADS)
        lbt = r1.take(HG_HEADS)

        r2 = Region(after_h)
        query = r2.take(LISTS, T)
        keys = r2.take(LISTS, P)
        score_size = [LISTS * P, LISTS * P, 4 * P]
        r3 = Region(N_KEYS * T - sum(score_size) - LISTS * P - 12 * P)
        assert r3.at >= r2.at
        topk_row = r3.at // T
        score_of = [r3.take(n // P, P) for n in score_size]
        spare = r3.take(LISTS * P)
        topv = r3.take(LISTS, TOPK)
        topi_u = r3.take(LISTS, TOPK).bitcast(U32)
        topi = r3.take(LISTS, TOPK)
        pos_u = r3.take(P).bitcast(U32)
        half_u = r3.take(2, P).bitcast(U32)
        half = r3.take(2, P)
        sums_of = [small[:, 64 + 8 * c:72 + 8 * c] for c in range(3)]

        gates = big[:].rearrange("p (e t) -> p e t", t=T)
        ada_b = sb("ada_b", [P, LAYERS, ADA])
        norm_g = sb("norm_g", [P, 2 * LAYERS, KC])
        amp = sb("amp", [P, KC, NS])

        const_landed = sem("const_landed")
        x_landed = sem("x_landed")
        raw_landed = [sem(f"raw_landed{s}") for s in range(RING)]
        high_ready, low_ready, half_done = sem("high_ready"), sem("low_ready"), sem("half_done")
        lin_free = sem("lin_free")
        glue_full, glue_free = sem("glue_full"), sem("glue_free")
        chain, act_chain = sem("chain"), sem("act_chain")
        c_silu = sem("c_silu")
        ada_full = sem("ada_full")
        ada_row, ada_turned, ada_read = sem("ada_row"), sem("ada_turned"), sem("ada_read")
        x_ready = sem("x_ready")
        sq_ready, var_ready, std_ready = sem("sq_ready"), sem("var_ready"), sem("std_ready")
        h_ready, h_high, h_low = sem("h_ready"), sem("h_high"), sem("h_low")
        ret_tables = sem("ret_tables")
        roped_ready, vtok_ready, ktok_ready = sem("roped_ready"), sem("vtok_ready"), sem("ktok_ready")
        qd_ready, att_ready, s1_ready, vmask_ready = sem("qd_ready"), sem("att_ready"), sem("s1_ready"), sem("vmask_ready")
        state_ready, state_stored = sem("state_ready"), sem("state_stored")
        sqo_ready, varo_ready, stdo_ready = sem("sqo_ready"), sem("varo_ready"), sem("stdo_ready")
        mixer_done, keys_landed = sem("mixer_done"), sem("keys_landed")
        x_spilled, x_back = sem("x_spilled"), sem("x_back")
        shifted, exped, picks_ready = sem("shifted"), sem("exped"), sem("picks_ready")
        first_ready, second_ready = sem("first_ready"), sem("second_ready")
        onehot_free = sem("onehot_free")
        apart_ready, apart_squared = sem("apart_ready"), sem("apart_squared")
        gate_free = sem("gate_free")
        gelu_ready, topk_done, choice_ready, w_ready = sem("gelu_ready"), sem("topk_done"), sem("choice_ready"), sem("w_ready")
        w_high, w_low = sem("w_high"), sem("w_low")
        hg_tables, keep_ready, log_ready, bound_in, bound_out = sem("hg_tables"), sem("keep_ready"), sem("log_ready"), sem("bound_in"), sem("bound_out")
        head_free, staged = sem("head_free"), sem("staged")
        diff_ready, fac_ready, x_lev_ready = sem("diff_ready"), sem("fac_ready"), sem("x_lev_ready")
        h_tok_ready, h_att_ready, h_s1_ready, h_vm_ready = sem("h_tok_ready"), sem("h_att_ready"), sem("h_s1_ready"), sem("h_vm_ready")
        y_ready, out_done = sem("y_ready"), sem("out_done")

        x_spill = t["x_spill"]
        block = ctx.enter_context(nc.Block())

        def section(eng, name, step, first=False, groups=None):
            n = COUNT[name] // RING
            lo, hi = groups or (0, n)
            if first:
                for s in range(RING):
                    step(lo, s)
                lo += 1
            end = hi - 1 if hi == n else hi
            if end > lo:
                with eng.Fori(lo, end) as i:
                    for s in range(RING):
                        step(i, s)
            if hi == n:
                for s in range(RING):
                    step(n - 1, s)

        def after(name, i, s, ahead=1):
            if isinstance(i, int) and 4 * i + s + ahead >= COUNT[name]:
                nxt = FOLLOWED.get(name)
                return (SPLIT[nxt], FIRST[nxt] // 4) if nxt and 4 * i + s + ahead == COUNT[name] else None
            return i * 4 + (SPLIT[name] + s + ahead), i + (FIRST[name] // 4 + (s + ahead) // 4)

        @block.sync
        def _(sp):
            def load(name, src, before=None, groups_before=0):
                def step(i, s):
                    if isinstance(i, int) and i == 0:
                        if before is not None and before.startswith("ada"):
                            sp.wait_ge(ada_full, groups_before)
                        elif before is not None:
                            sp.wait_ge(low_ready, 2 * (SPLIT[before] + COUNT[before] + s - 3))
                    elif name.startswith("ada"):
                        sp.wait_ge(ada_full, i + groups_before)
                    else:
                        sp.wait_ge(low_ready, i * 8 + 2 * (SPLIT[name] + s - 3))
                    sp.dma_start(raw[:, s, :], src[i * 4 + s]).then_inc(raw_landed[s], 16)
                section(sp, name, step, first=True)

            load("ada0a", t["ada_w"][0][0:16])
            load("ab_in", t["ab_w_in"], "ada0a", 4)
            load("ada0b", t["ada_w"][0][16:48], "ab_in", 4)
            load("ab_out", t["ab_w_out"], "ada0b", 12)
            load("wq0", t["peer_wq"][0], "ab_out")
            load("u0", t["peer_u"][0], "wq0")
            load("ada1", t["ada_w"][1], "u0", 12)
            load("v0", t["peer_v"][0], "ada1", 24)
            load("hg_in", t["hg_w_in"], "v0")
            load("hg_out", t["hg_w_out"], "hg_in")
            load("wq1", t["peer_wq"][1], "hg_out")
            load("u1", t["peer_u"][1], "wq1")
            load("v1", t["peer_v"][1], "u1")

        @block.gpsimd
        def _(pool):
            for dst, src in ((ident[:], t["ident"]), (ones[:], t["ones"]), (iota[:], t["iota"]),
                             (ada_b[:], t["ada_b"]), (norm_g[:], t["norm_g"]), (small[:, 32:64], t["gains"]),
                             (cs[:], t["c"])):
                pool.dma_start(dst, src).then_inc(const_landed, 16)
            pool.dma_start(x, t["x"]).then_inc(x_landed, 16)
            for dst, src in ((cos_t, t["cos"]), (sin_t, t["sin"]), (swap, t["swap"]), (q_decay, t["q_decay"]),
                             (att_decay, t["att_decay"]), (att_decay_s[0:T_SAMPLE], t["att_decay_s"]),
                             (key_decay, t["key_decay"]), (seq_mask[0:T_SAMPLE], t["seq_mask"]),
                             (ret_state, t["state_ret"]), (conv_zs[:, :, :, 0:2], t["state_conv"])):
                pool.dma_start(dst, src).then_inc(ret_tables, 16)

            def peer(l):
                pool.wait_ge(mixer_done, l + 1)
                pool.dma_start(keys, t["peer_keys"][l]).then_inc(keys_landed, 16)
                pool.wait_ge(x_ready, 2 * l + 1)
                pool.dma_start(x_spill, x).then_inc(x_spilled, 16)
                pool.wait_ge(choice_ready, l + 1)
                pool.wait_ge(gelu_ready, EXP * (l + 1))
                with pool.Fori(0, T // TOKENS) as i:
                    for g in range(TOKENS // 4):
                        n = i * (TOKENS // 4) + (T // 4 * l + g)
                        pool.wait_ge(second_ready, n + 1)
                        pool.tensor_tensor(apart[:, g % 2], iota[:, None, :].broadcast_to([P, 4, P]),
                                           choice[:, 1, bass.ds(i * TOKENS + 4 * g, 4)][:, :, None].broadcast_to([P, 4, P]),
                                           ALU.subtract).then_inc(apart_ready, 1)
                pool.wait_ge(half_done, 2 * (SPLIT[f"v{l}"] + KC + 1))
                pool.dma_start(x, x_spill).then_inc(x_back, 16)

            pool.wait_ge(state_ready, 1)
            pool.dma_start(t["ret_p"], ret_s2).then_inc(state_stored, 16)
            pool.dma_start(t["ret_s"], ret_state).then_inc(state_stored, 16)
            pool.dma_start(t["conv_p"], conv_tail).then_inc(state_stored, 16)
            pool.dma_start(t["conv_s"], conv_tails).then_inc(state_stored, 16)
            peer(0)
            pool.wait_ge(half_done, 2 * (SPLIT["v0"] + EXP))
            for dst, src in ((restart, t["restart"]), (lev_mask, t["lev_mask"]), (lev_masks[0:T_SAMPLE], t["lev_masks"]),
                             (h_seq_mask[0:T_SAMPLE], t["seq_mask"]), (bounds, t["bounds"]), (hg_states, t["state_hgrn"])):
                pool.dma_start(dst, src).then_inc(hg_tables, 16)
            pool.wait_ge(state_ready, 2)
            pool.dma_start(t["hg_p"], h_out).then_inc(state_stored, 16)
            pool.dma_start(t["hg_s"], hg_states).then_inc(state_stored, 16)
            peer(1)
            pool.wait_ge(y_ready, 1)
            pool.dma_start(t["y"], h).then_inc(out_done, 16)
            pool.wait_ge(out_done, 16)
            pool.wait_ge(state_stored, 16 * 6)
            pool.wait_ge(x_spilled, 32)

        @block.scalar
        def _(act):
            def high_half(number, group, slot, part):
                act.wait_ge(raw_landed[slot], (group + 1) * 16)
                if not (isinstance(number, int) and number < 2):
                    act.wait_ge(half_done, number * 2 + (part - 3))
                cols = slice(HALF * part, HALF * part + HALF)
                act.activation(spl[:, slot % 2, 0, cols], raw[:, slot, cols], ACT.Copy).then_inc(high_ready, 1)

            def high(number, group, slot):
                high_half(number, group, slot, 0)
                high_half(number, group, slot, 1)

            def split_high(name, i, s, ahead=1, parts=(0, 1)):
                if (nxt := after(name, i, s, ahead)) is not None:
                    for part in parts:
                        high_half(*nxt, (s + ahead) % 4, part)

            def read_out(name, reader, groups, first=False):
                if groups[0] == 0:
                    split_high(name, 0, 0)
                    split_high(name, 0, 0, ahead=2, parts=(0,))

                def step(i, s):
                    act.wait_ge(half_done, i * 8 + 2 * (SPLIT[name] + s + 1))
                    reader(i, s)
                    split_high(name, i, s, ahead=2, parts=(1,))
                    split_high(name, i, s, ahead=3, parts=(0,))
                section(act, name, step, first=first, groups=groups)

            def cond_row(g, r):
                act.wait_ge(ada_full, g + 1)
                act.activation(cond_rows, ps[0:NS, 0, 256 * r:256 * r + 256], ACT.Copy).then_inc(ada_row, 1)

            def cond_column(g, r, layer, chunk):
                act.wait_ge(ada_turned, g * 2 + (r + 1))
                for q in range(2):
                    c = chunk + (2 * r + q)
                    ins = act.activation(mod[:, bass.ds(c, 1), :].rearrange("p a n -> p (a n)"), ps[:, 1, NS * q:NS * q + NS],
                                         ACT.Identity, bias=ada_b[:, layer, bass.ds(c, 1)])
                ins.then_inc(ada_read, 1)

            def conditioning(g):
                for r in range(2):
                    cond_row(g, r)
                    cond_column(g, r, 0, 4 * g)

            def copy_out(name, dst, func, groups, first=False):
                def reader(i, s):
                    act.activation(dst[:, bass.ds(i * 4 + s, 1), :], ps[:, s % 2:s % 2 + 1, 0:T], func).then_inc(lin_free, 1)
                read_out(name, reader, groups, first)

            def only_split(name):
                section(act, name, lambda i, s: split_high(name, i, s))

            def norm(j):
                if j == 0:
                    act.wait_ge(x_landed, 16)
                else:
                    act.wait_ge(x_ready, j)
                act.activation(h, x, ACT.Square).then_inc(sq_ready, 1)
                act.wait_ge(var_ready, j + 1)
                act.activation(rstd[:], rstd[:], ACT.Sqrt).then_inc(std_ready, 1)

            def high_input(k):
                act.wait_ge(h_ready, k)
                act.activation(hs[:, 0, :, :], h, ACT.Copy).then_inc(h_high, 1)

            def peer(l):
                norm(2 * l + 1)
                high_input(3 * l + 3)
                act.wait_ge(state_stored, 64 if l == 0 else 96)
                copy_out(f"wq{l}", query, ACT.Copy, (0, WQ // 4))
                act.wait_ge(x_spilled, 16 * (l + 1))

                def expert_in(i, s):
                    act.activation(gates[:, bass.ds(i * 4 + s, 1), :], ps[:, s % 2:s % 2 + 1, 0:T], ACT.Gelu).then_inc(gelu_ready, 1)
                read_out(f"u{l}", expert_in, groups=(0, topk_row // 4))
                act.wait_ge(topk_done, l + 1)
                act.activation(rstd[:], rstd[:], ACT.Exp).then_inc(exped, 1)
                read_out(f"u{l}", expert_in, groups=(topk_row // 4, EXP // 4))
                if l == 0:
                    act.sem_inc(second_ready, 2)
                with act.Fori(0, T // TOKENS) as i:
                    for g in range(TOKENS // 4):
                        n = i * (TOKENS // 4) + (T // 4 * l + g)
                        act.wait_ge(apart_ready, n + 1)
                        act.activation(apart[:, g % 2], apart[:, g % 2].bitcast(F32), ACT.Square).then_inc(apart_squared, 1)
                        act.wait_ge(apart_squared, n + 1)
                        act.wait_ge(onehot_free, i * TOKENS + (T * l + 4 * g + 4))
                        act.activation(seconds[:, g % 2], apart[:, g % 2].bitcast(F32), ACT.Relu, bias=1.0, scale=-1.0).then_inc(second_ready, 1)
                        if l == 0:
                            if g in (2, 4):
                                cond_column(i + 12, g // 2 - 1, 1, i * 4)
                            if g in (0, 2):
                                cond_row(i + 12, g // 2)
                if l == 0:
                    high(SPLIT["v0"], FIRST["v0"] // 4, 0)

                def weight_high(e, slot):
                    act.activation(hs[:, 0, bass.ds(slot, 1), :], gates[:, bass.ds(e, 1), :], ACT.Copy).then_inc(w_high, 1)

                act.wait_ge(w_ready, (T // 4) * (l + 1))
                weight_high(0, 0)

                def expert_out(i, s):
                    split_high(f"v{l}", i, s)
                    if not (isinstance(i, int) and 4 * i + s == EXP - 1):
                        act.wait_ge(half_done, i * 8 + 2 * (SPLIT[f"v{l}"] + s))
                        weight_high(i * 4 + (s + 1), (s + 1) % 2)
                section(act, f"v{l}", expert_out)

            act.wait_ge(const_landed, 16 * 7)
            act.activation(cs[:], cs[:], ACT.Silu).then_inc(c_silu, 1)
            for g in range(4):
                conditioning(g)
            high(0, FIRST["ab_in"] // 4, 0)
            norm(0)
            high_input(1)
            copy_out("ab_in", proj0, ACT.Copy, (0, 3), first=True)
            copy_out("ab_in", proj0, ACT.Silu, (3, 4))
            copy_out("ab_in", proj0, ACT.Copy, (4, 7))
            for g in range(4, 12):
                conditioning(g)
            high(SPLIT["ab_out"], FIRST["ab_out"] // 4, 0)
            act.wait_ge(sqo_ready, 1)
            act.activation(swapped[:, 0:RET_HEADS, :], h[:, 0:RET_HEADS, :], ACT.Square).then_inc(sqo_ready, 1)
            act.wait_ge(varo_ready, 1)
            act.activation(roped[:, 0:RET_HEADS, :], roped[:, 0:RET_HEADS, :], ACT.Sqrt).then_inc(stdo_ready, 1)
            high_input(2)
            only_split("ab_out")
            peer(0)
            norm(2)
            high_input(4)
            copy_out("hg_in", proj1, ACT.Silu, (0, 2))
            copy_out("hg_in", proj1, ACT.Sigmoid, (2, 4))
            copy_out("hg_in", proj1, ACT.Copy, (4, 6))
            copy_out("hg_in", proj1, ACT.Silu, (6, 8))
            act.wait_ge(bound_in, 1)
            act.activation(bounds, bounds, ACT.Exp).then_inc(bound_out, 1)
            act.wait_ge(keep_ready, 1)
            act.activation(logf, proj1[:, 8:16, :], ACT.Ln).then_inc(log_ready, 1)
            with act.Fori(0, HG_HEADS) as i:
                act.wait_ge(head_free, i + 1)
                for k in range(3):
                    act.activation(stage[:, k:k + 1, :], proj1[:, bass.ds(i + 8 * k, 1), :], ACT.Copy).then_inc(staged, 1)
                act.activation(s0_stage, hg_states[:, bass.ds(i, 1), :, :], ACT.Copy).then_inc(staged, 1)
                act.wait_ge(diff_ready, i + 1)
                act.activation(fac, fac, ACT.Exp).then_inc(fac_ready, 1)
            act.wait_ge(sqo_ready, 3)
            act.activation(logf, h, ACT.Square).then_inc(sqo_ready, 1)
            act.wait_ge(varo_ready, 2)
            act.activation(proj1[:, 8:16, :], proj1[:, 8:16, :], ACT.Sqrt).then_inc(stdo_ready, 1)
            high_input(5)
            only_split("hg_out")
            peer(1)
            norm(4)

        @block.vector
        def _(dve):
            chained, taken = Tally(), Tally()

            def link(ins):
                chained.count()
                ins.then_inc(chain, 1)
                dve.wait_ge(chain, chained.at())

            def product():
                bank = 2 + taken.static() % 4
                taken.count()
                dve.wait_ge(glue_full, taken.at())
                return ps[:, bank, :]

            def released():
                dve.wait_ge(glue_free, taken.at())

            def low(number, slot):
                for part in range(2):
                    dve.wait_ge(high_ready, number * 2 + (part + 1))
                    cols = slice(HALF * part, HALF * part + HALF)
                    dve.tensor_tensor(spl[:, slot % 2, 1, cols], raw[:, slot, cols],
                                      spl[:, slot % 2, 0, cols].bitcast(F32), ALU.subtract).then_inc(low_ready, 1)

            def split_low(name, i, s):
                if (nxt := after(name, i, s)) is not None:
                    low(nxt[0], (s + 1) % 4)

            def only_split(name, first=False, groups=None):
                section(dve, name, lambda i, s: split_low(name, i, s), first=first, groups=groups)

            def mean_root(j):
                s = product()
                dve.tensor_scalar(rstd[:], s[:, 0:T], 1.0 / D_MODEL, None, ALU.mult).then_inc(glue_free, 1)
                released()
                dve.tensor_scalar(rstd[:], rstd[:], EPS, None, ALU.add).then_inc(var_ready, 1)
                dve.wait_ge(std_ready, j + 1)
                link(dve.reciprocal(rstd[:], rstd[:]))

            def norm(j):
                l, part = j // 2, 24 * (j % 2)
                gain = norm_g[:, j, :, None].broadcast_to([P, KC, NS])
                link(dve.tensor_scalar(amp[:], mod[:, part + 8:part + 16, :], 1.0, None, ALU.add))
                link(dve.tensor_tensor(amp[:], amp[:], gain, ALU.mult))
                mean_root(j)
                link(dve.tensor_tensor(h, x, rstd[:, None, :].broadcast_to([P, KC, T]), ALU.mult))
                hs_view = h[:, :, T_PROMPT:T].rearrange("p k (s j) -> p k s j", j=L_SEQ)
                for k in range(KC):
                    dve.tensor_scalar(h[:, k, 0:T_PROMPT], h[:, k, 0:T_PROMPT], amp[:, k, 0:1], mod[:, part + k, 0:1],
                                      ALU.mult, ALU.add)
                    per_seq = amp[:, k, 1:9, None].broadcast_to([P, N_SEQ, L_SEQ])
                    ins = dve.tensor_tensor(hs_view[:, k], hs_view[:, k], per_seq, ALU.mult)
                link(ins)
                for k in range(KC):
                    per_seq = mod[:, part + k, 1:9, None].broadcast_to([P, N_SEQ, L_SEQ])
                    ins = dve.tensor_tensor(hs_view[:, k], hs_view[:, k], per_seq, ALU.add)
                ins.then_inc(h_ready, 1)

            def low_input(k):
                dve.wait_ge(h_high, k)
                dve.tensor_tensor(hs[:, 1, :, :], h, hs[:, 0, :, :].bitcast(F32), ALU.subtract).then_inc(h_low, 1)

            def add_to_x(k, k_static, bank, gate, freed, freed_value):
                xk = x[:, k, :] if k_static else x[:, bass.ds(k, 1), :]
                xk = xk if k_static else xk.rearrange("p a t -> p (a t)")
                if k_static:
                    gp, gsq = gate[:, k, 0:1], gate[:, k, 1:9]
                else:
                    gp = mod[:, bass.ds(k + gate, 1), 0:1].rearrange("p a t -> p (a t)")
                    gsq = mod[:, bass.ds(k + gate, 1), 1:9].rearrange("p a t -> p (a t)")
                dve.scalar_tensor_tensor(out=xk[:, 0:T_PROMPT], in0=bank[:, 0:T_PROMPT], scalar=gp,
                                         in1=xk[:, 0:T_PROMPT], op0=ALU.mult, op1=ALU.add)
                dve.tensor_tensor(samp_tmp, bank[:, T_PROMPT:T].rearrange("p (s j) -> p s j", j=L_SEQ),
                                  gsq[:, :, None].broadcast_to([P, N_SEQ, L_SEQ]), ALU.mult).then_inc(freed, 1)
                dve.wait_ge(freed, freed_value)
                xs = xk[:, T_PROMPT:T].rearrange("p (s j) -> p s j", j=L_SEQ)
                return dve.tensor_tensor(xs, xs, samp_tmp, ALU.add)

            def project_out(name, gate):
                def step(i, s):
                    split_low(name, i, s)
                    dve.wait_ge(half_done, i * 8 + 2 * (SPLIT[name] + s + 1))
                    ins = add_to_x(i * 4 + s, False, ps[:, s % 2, :], gate, lin_free, i * 4 + (LINEAR[name] + s + 1))
                    link(ins)
                for i in range(OUT // RING):
                    for s in range(RING):
                        step(i, s)
                dve.sem_inc(x_ready, 1)

            def retention():
                dve.wait_ge(ret_tables, 16 * 10)
                dve.wait_ge(lin_free, LINEAR["ab_out"])
                for c in range(2 * RET_HEADS):
                    s = product()
                    dve.tensor_tensor(swapped[:, c, :], s[:, 0:T], sin_t, ALU.mult).then_inc(glue_free, 1)
                link(dve.tensor_tensor(roped, proj0[:, 0:8, :], cos_t[:, None, :].broadcast_to([P, 8, T]), ALU.mult))
                released()
                dve.tensor_tensor(roped, roped, swapped, ALU.add).then_inc(roped_ready, 1)
                dve.wait_ge(roped_ready, 1)
                dve.tensor_tensor(qd, roped[:, 0:4, :], q_decay, ALU.mult).then_inc(qd_ready, 1)
                for c, (_, n) in enumerate(TILES):
                    s = product()
                    dve.tensor_copy(vtok[0:n, c, :, :], s[0:n, :].rearrange("p (h v) -> p h v", v=P)).then_inc(glue_free, 1)
                released()
                dve.tensor_tensor(ret_vmask[:, :, :], vtok[0:32, 2, 0:1, :].broadcast_to([T_SAMPLE, N_SEQ, P]),
                                  seq_mask[0:32, :, None].broadcast_to([T_SAMPLE, N_SEQ, P]), ALU.mult).then_inc(vmask_ready, 1)
                for c, (_, n) in enumerate(TILES):
                    s = product()
                    dve.tensor_tensor(ktok[0:n, c, :, :], s[0:n, :].rearrange("p (h v) -> p h v", v=P),
                                      key_decay[0:n, c, :, None].broadcast_to([n, RET_HEADS, P]), ALU.mult).then_inc(glue_free, 1)
                for c, (_, n) in enumerate(TILES):
                    s = product()
                    mask = att_decay if n == P else att_decay_s[0:n]
                    dve.tensor_tensor(att[0:n, c, :, 0:n], s[0:n, 0:RET_HEADS * n].rearrange("p (h i) -> p h i", i=n),
                                      mask, ALU.mult).then_inc(glue_free, 1)
                s = product()
                dve.tensor_copy(ret_s1, s.rearrange("p (h v) -> p h v", v=P)).then_inc(glue_free, 1)
                released()
                s = product()
                for hd in range(RET_HEADS):
                    ins = dve.scalar_tensor_tensor(out=ret_s2[:, hd, :], in0=ret_s1[:, hd, :], scalar=float(np.exp(LOG_GAMMA[hd] * P)),
                                                   in1=s[:, hd * P:(hd + 1) * P], op0=ALU.mult, op1=ALU.add)
                ins.then_inc(glue_free, 1)
                for hd in range(RET_HEADS):
                    s = product()
                    dve.tensor_copy(h[:, hd, :], s[:, 0:T]).then_inc(glue_free, 1)
                for hd in range(RET_HEADS):
                    for half_seq in range(2):
                        s = product()
                        st = ret_state[:, 4 * half_seq:4 * half_seq + 4, hd, :]
                        dve.scalar_tensor_tensor(out=st, in0=st, scalar=float(np.exp(LOG_GAMMA[hd] * L_SEQ)),
                                                 in1=s.rearrange("p (q v) -> p q v", v=P), op0=ALU.mult, op1=ALU.add).then_inc(glue_free, 1)
                    if hd + 1 < RET_HEADS:
                        dve.tensor_tensor(ret_vmask[:, :, :], vtok[0:32, 2, hd + 1:hd + 2, :].broadcast_to([T_SAMPLE, N_SEQ, P]),
                                          seq_mask[0:32, :, None].broadcast_to([T_SAMPLE, N_SEQ, P]), ALU.mult).then_inc(vmask_ready, 1)
                released()
                dve.memset(conv_z[:, :, 0:2], 0.0)
                dve.tensor_tensor(conv_z[:, :, 2:], proj0[:, 20:24, 0:T_PROMPT], proj0[:, 24:28, 0:T_PROMPT], ALU.mult)
                for c in range(4):
                    cg = proj0[:, 20 + c, T_PROMPT:T].rearrange("p (s j) -> p s j", j=L_SEQ)
                    xin = proj0[:, 24 + c, T_PROMPT:T].rearrange("p (s j) -> p s j", j=L_SEQ)
                    ins = dve.tensor_tensor(conv_zs[:, c, :, 2:6], cg, xin, ALU.mult)
                link(ins)
                dve.tensor_copy(conv_tail, conv_z[:, :, T_PROMPT:T_PROMPT + 2])
                dve.tensor_copy(conv_tails, conv_zs[:, :, :, 4:6]).then_inc(state_ready, 1)

                def dst(c):
                    return h[:, 4 + c, 0:T_PROMPT], h[:, 4 + c, T_PROMPT:T].rearrange("p (s j) -> p s j", j=L_SEQ)
                for c in range(4):
                    a, b = dst(c)
                    dve.tensor_scalar(a, conv_z[:, c, 0:T_PROMPT], conv_w[:, 0, c:c + 1], None, ALU.mult)
                    ins = dve.tensor_scalar(b, conv_zs[:, c, :, 0:4], conv_w[:, 0, c:c + 1], None, ALU.mult)
                link(ins)
                for w in (1, 2):
                    for c in range(4):
                        a, b = dst(c)
                        dve.scalar_tensor_tensor(out=a, in0=conv_z[:, c, w:w + T_PROMPT], scalar=conv_w[:, w, c:c + 1],
                                                 in1=a, op0=ALU.mult, op1=ALU.add)
                        ins = dve.scalar_tensor_tensor(out=b, in0=conv_zs[:, c, :, w:w + 4], scalar=conv_w[:, w, c:c + 1],
                                                       in1=b, op0=ALU.mult, op1=ALU.add)
                    link(ins)
                link(dve.tensor_tensor(h[:, 4:8, :], h[:, 4:8, :], proj0[:, 16:20, :], ALU.mult))

            def head_norm(heads, mean, gate, gain, k):
                dve.sem_inc(sqo_ready, 1)
                for hd in range(heads):
                    s = product()
                    dve.tensor_scalar(mean[:, hd, :], s[:, 0:T], 1.0 / P, EPS, ALU.mult, ALU.add).then_inc(glue_free, 1)
                released()
                dve.sem_inc(varo_ready, 1)
                dve.wait_ge(stdo_ready, k)
                link(dve.reciprocal(mean, mean))
                o = h[:, 0:heads, :]
                link(dve.tensor_tensor(o, o, mean, ALU.mult))
                link(dve.tensor_tensor(o, o, gate, ALU.mult))
                link(dve.tensor_tensor(o, o, gain[:, :, None].broadcast_to([P, heads, T]), ALU.mult))
                dve.sem_inc(mixer_done, 1)
                dve.sem_inc(h_ready, 1)

            def hgrn():
                dve.wait_ge(hg_tables, 16 * 6)
                dve.wait_ge(lin_free, LINEAR["hg_out"])
                link(dve.tensor_tensor(lbt, bounds[:, 0, :], bounds[:, 1, :], ALU.max))
                dve.tensor_tensor(bounds, bounds, lbt[:, None, :].broadcast_to([P, 2, HG_HEADS]), ALU.subtract).then_inc(bound_in, 1)
                dve.wait_ge(bound_out, 1)
                link(dve.tensor_tensor(lbt, bounds[:, 0, :], bounds[:, 1, :], ALU.add))
                link(dve.reciprocal(lbt, lbt))
                link(dve.tensor_tensor(lb, bounds[:, 1, :], lbt, ALU.mult))
                link(dve.tensor_scalar(one_lb, lb, -1.0, 1.0, ALU.mult, ALU.add))
                for hd in range(HG_HEADS):
                    f = proj1[:, 8 + hd, :]
                    ins = dve.tensor_scalar(f, f, one_lb[:, hd:hd + 1], lb[:, hd:hd + 1], ALU.mult, ALU.add)
                ins.then_inc(keep_ready, 1)
                dve.memset(fac, 0.0)
                dve.wait_ge(log_ready, 1)
                link(dve.tensor_scalar(proj1[:, 8:16, :], proj1[:, 8:16, :], -1.0, 1.0, ALU.mult, ALU.add))
                dve.sem_inc(head_free, 1)
                b = fac[:, 8, :]

                def halves(v, m):
                    n = T_PROMPT if m > 2 else T
                    w = v[:, 0:n].rearrange("p (n m) -> p n m", m=2 * m)
                    return w[:, :, 0:m], w[:, :, m:2 * m], w[:, :, m - 1:m].broadcast_to([P, n // (2 * m), m])

                with dve.Fori(0, HG_HEADS) as i:
                    chained.enter(i, 3)
                    taken.enter(i, 12)
                    link(dve.tensor_tensor_scan(b, restart, logf[:, bass.ds(i, 1), :].rearrange("p a t -> p (a t)"), 0.0, ALU.mult, ALU.add))
                    for lev, m in enumerate(LEVELS):
                        b1, b2, mid = halves(b, m)
                        d1, d2, _ = halves(fac[:, lev, :], m)
                        dve.tensor_tensor(d1, mid, b1, ALU.subtract)
                        dve.tensor_tensor(d2, b2, mid, ALU.subtract)
                    for lo, hi, m in ((0, T_PROMPT, P), (T_PROMPT, T, L_SEQ)):
                        bb = b[:, lo:hi].rearrange("p (n m) -> p n m", m=m)
                        dd = fac[:, 7, lo:hi].rearrange("p (n m) -> p n m", m=m)
                        ins = dve.tensor_tensor(dd, bb[:, :, m - 1:m].broadcast_to([P, (hi - lo) // m, m]), bb, ALU.subtract)
                    ins.then_inc(diff_ready, 1)
                    dve.wait_ge(fac_ready, i + 1)
                    dve.wait_ge(staged, i * 4 + 4)
                    for lev, m in enumerate(LEVELS):
                        f1, f2, _ = halves(fac[:, lev, :], m)
                        k1, _, _ = halves(stage[:, 1, :], m)
                        _, q2, _ = halves(stage[:, 0, :], m)
                        dve.tensor_tensor(f1, f1, k1, ALU.mult)
                        dve.tensor_tensor(f2, f2, q2, ALU.mult)
                    dve.tensor_tensor(fac[:, 7, :], fac[:, 7, :], stage[:, 1, :], ALU.mult)
                    dve.tensor_tensor(qe, fac[:, 8, :], stage[:, 0, :], ALU.mult).then_inc(x_lev_ready, 1)
                    for dst in (h_vtok, h_ktok):
                        s = product()
                        dve.tensor_copy(dst[:, 0:2, :], s[:, 0:2 * P].rearrange("p (c v) -> p c v", v=P))
                        dve.tensor_copy(dst[0:32, 2, :], s[0:32, 2 * P:3 * P]).then_inc(glue_free, 1)
                    released()
                    dve.tensor_tensor(h_vmask[0:32], h_vtok[0:32, 2:3, :].broadcast_to([T_SAMPLE, N_SEQ, P]),
                                      h_seq_mask[0:32, :, None].broadcast_to([T_SAMPLE, N_SEQ, P]), ALU.mult).then_inc(h_vm_ready, 1)
                    for c in range(2):
                        for g in range(2):
                            s = product()
                            dve.tensor_tensor(h_att[:, c, 4 * g:4 * g + 4, :], s.rearrange("p (l i) -> p l i", i=P),
                                              lev_mask[:, 4 * g:4 * g + 4, :], ALU.mult).then_inc(glue_free, 1)
                    s = product()
                    dve.tensor_tensor(h_atts[0:32], s[0:32, 0:96].rearrange("p (l i) -> p l i", i=32), lev_masks[0:32], ALU.mult).then_inc(glue_free, 1)
                    s = product()
                    dve.tensor_copy(h_s1, s[:, 0:P]).then_inc(glue_free, 1)
                    released()
                    dve.sem_inc(h_s1_ready, 1)
                    s = product()
                    dve.scalar_tensor_tensor(out=h_out[:, bass.ds(i, 1), :].rearrange("p a v -> p (a v)"), in0=h_s1, scalar=fac[:, 8, T_PROMPT - 1:T_PROMPT],
                                             in1=s[:, 0:P], op0=ALU.mult, op1=ALU.add).then_inc(glue_free, 1)
                    s = product()
                    dve.tensor_copy(h[:, bass.ds(i, 1), :].rearrange("p a t -> p (a t)"), s[:, 0:T]).then_inc(glue_free, 1)
                    st = hg_states[:, bass.ds(i, 1), :, :].rearrange("p a s v -> p (a s) v")
                    last = fac[:, 8, T_PROMPT:T].rearrange("p (s j) -> p s j", j=L_SEQ)[:, :, L_SEQ - 1:L_SEQ]
                    link(dve.tensor_tensor(st, s0_stage, last.broadcast_to([P, N_SEQ, P]), ALU.mult))
                    for g in range(2):
                        s = product()
                        half_st = hg_states[:, bass.ds(i, 1), 4 * g:4 * g + 4, :].rearrange("p a s v -> p (a s) v")
                        dve.tensor_tensor(half_st, half_st, s.rearrange("p (q v) -> p q v", v=P), ALU.add).then_inc(glue_free, 1)
                    released()
                    link(dve.memset(fac[:, 0:5, T_PROMPT:T], 0.0))
                    dve.sem_inc(head_free, 1)
                chained.leave(HG_HEADS)
                taken.leave(HG_HEADS)
                dve.sem_inc(state_ready, 1)

            def topk(l):
                fed = [0]

                def feed():
                    split_low(f"u{l}", fed[0] // 4, fed[0] % 4)
                    fed[0] += 1

                for c, (_, n) in enumerate(TILES):
                    for g in range(4 if n == P else 1):
                        s = product()
                        dve.tensor_copy(score_of[c][:, 4 * g:4 * g + 4, :], s.rearrange("p (l k) -> p l k", k=P)).then_inc(glue_free, 1)
                        if 4 * c + g in (1, 5, 7):
                            feed()
                released()
                for c in range(3):
                    lists = (LISTS, LISTS, 4)[c]
                    heads = lists // 2
                    sc, sc2 = score_of[c], spare[:, 0:lists * P].rearrange("p (j k) -> p j k", k=P)
                    for j in range(lists):
                        ins = dve.max(topv[:, j, 0:8], sc[:, j, :])
                        if j % 8 == 7:
                            feed()
                    link(ins)
                    for j in range(lists):
                        dve.max_index(topi_u[:, j, 0:8], topv[:, j, 0:8], sc[:, j, :])
                        ins = dve.match_replace(sc2[:, j, :], topv[:, j, 0:8], sc[:, j, :], LOWEST)
                        if j % 3 == 2:
                            feed()
                    link(ins)
                    for j in range(lists):
                        ins = dve.max(topv[:, j, 8:16], sc2[:, j, :])
                        if j % 8 == 7:
                            feed()
                    link(ins)
                    for j in range(lists):
                        ins = dve.max_index(topi_u[:, j, 8:16], topv[:, j, 8:16], sc2[:, j, :])
                        if j % 4 == 3:
                            feed()
                    link(ins)
                    dve.tensor_copy(topi[:, 0:lists], topi_u[:, 0:lists])
                    tv = topv[:, 0:lists].rearrange("p (h q) k -> p h q k", q=2)
                    comb, comb2 = (v.rearrange("p (h q) k -> p h (q k)", q=2) for v in (sc, sc2))
                    best, pos = best_of[c], pos_u[:, 0:heads * TOPK].rearrange("p (h k) -> p h k", k=TOPK)
                    for hd in range(heads):
                        ins = dve.tensor_tensor(comb[:, hd, :].rearrange("p (a b) -> p a b", b=TOPK),
                                                tv[:, hd, 0, :, None].broadcast_to([P, TOPK, TOPK]),
                                                tv[:, hd, 1:2, :].broadcast_to([P, TOPK, TOPK]), ALU.add)
                        if hd % 4 == 3:
                            feed()
                    link(ins)
                    for hd in range(heads):
                        ins = dve.max(best[:, hd, 0:8], comb[:, hd, :])
                        if hd % 4 == 3:
                            feed()
                    link(ins)
                    for hd in range(heads):
                        dve.max_index(pos[:, hd, 0:8], best[:, hd, 0:8], comb[:, hd, :])
                        ins = dve.match_replace(comb2[:, hd, :], best[:, hd, 0:8], comb[:, hd, :], LOWEST)
                        if hd % 2:
                            feed()
                    link(ins)
                    for hd in range(heads):
                        ins = dve.max(best[:, hd, 8:16], comb2[:, hd, :])
                        if hd % 4 == 3:
                            feed()
                    link(ins)
                    for hd in range(heads):
                        ins = dve.max_index(pos[:, hd, 8:16], best[:, hd, 8:16], comb2[:, hd, :])
                        if hd % 4 == 3:
                            feed()
                    link(ins)
                    top = sums_of[c][:, 0:heads]
                    link(dve.tensor_copy(top, best[:, :, 0]))
                    dve.tensor_tensor(best, best, top[:, :, None].broadcast_to([P, heads, TOPK]), ALU.subtract)
                    n = heads * TOPK
                    dve.tensor_single_scalar(half_u[:, 0, 0:n], pos_u[:, 0:n], 4, ALU.logical_shift_right)
                    link(dve.tensor_single_scalar(half_u[:, 1, 0:n], pos_u[:, 0:n], 15, ALU.bitwise_and))
                    link(dve.tensor_copy(half[:, :, 0:n], half_u[:, :, 0:n]))
                    ti = topi[:, 0:lists].rearrange("p (h q) k -> p h q k", q=2)
                    eq = spare[:, 0:n * TOPK].rearrange("p (i a) -> p i a", a=TOPK)
                    for q in range(2):
                        link(dve.tensor_tensor(eq, half[:, q, 0:n, None].broadcast_to([P, n, TOPK]),
                                               iota[:, None, 0:TOPK].broadcast_to([P, n, TOPK]), ALU.is_equal))
                        feed()
                        for hd in range(heads):
                            e = eq[:, TOPK * hd:TOPK * hd + TOPK, :]
                            ins = dve.tensor_tensor(e, e, ti[:, hd, q:q + 1, :].broadcast_to([P, TOPK, TOPK]), ALU.mult)
                        link(ins)
                        feed()
                        link(dve.tensor_reduce(pick_of[c][:, q, :], eq, AX.X, ALU.add))
                        feed()
                dve.sem_inc(topk_done, 1)
                while fed[0] % 4:
                    feed()
                assert fed[0] < topk_row // 4 * 4, (fed[0], topk_row)
                return fed[0] // 4

            def gate_picks(l):
                dve.wait_ge(exped, l + 1)
                for c in range(3):
                    heads = (8, 8, 2)[c]
                    ins = dve.tensor_reduce(sums_of[c][:, 0:heads], best_of[c], AX.X, ALU.add)
                link(ins)
                for c in range(3):
                    ins = dve.reciprocal(sums_of[c][:, 0:(8, 8, 2)[c]], sums_of[c][:, 0:(8, 8, 2)[c]])
                link(ins)
                for c in range(3):
                    heads = (8, 8, 2)[c]
                    ins = dve.tensor_tensor(pick_of[c][:, 2, :].rearrange("p (h k) -> p h k", k=TOPK), best_of[c],
                                            sums_of[c][:, 0:heads, None].broadcast_to([P, heads, TOPK]), ALU.mult)
                ins.then_inc(picks_ready, 1)

            def turn_picks(l):
                for c in range(2):
                    s = product()
                    dve.tensor_copy(choice[:, :, P * c:P * c + P], s[:, 0:3 * P].rearrange("p (q i) -> p q i", i=P)).then_inc(glue_free, 1)
                dve.wait_ge(picks_ready, l + 1)
                for q in range(3):
                    ins = dve.transpose(choice[:, q, T_PROMPT:T], pick_of[2][:, q, :])
                link(ins)
                released()
                dve.sem_inc(choice_ready, 1)

            def weigh(l):
                if l == 0:
                    dve.sem_inc(gate_free, 2)

                def firsts(i, g):
                    for j in range(4):
                        tok = i * TOKENS + (4 * g + j)
                        dve.wait_ge(onehot_free, tok + (T * l + 1))
                        dve.tensor_scalar(onehot[:, (4 * g + j) % 8, :], iota[:], choice[:, 0, bass.ds(tok, 1)], choice[:, 2, bass.ds(tok, 1)],
                                          ALU.is_equal, ALU.mult).then_inc(first_ready, 1)

                def apply(i, g):
                    dve.wait_ge(onehot_free, i * TOKENS + (T * l + 4 * g + 4 + 8))
                    w = gates[:, :, bass.ds(i * TOKENS + 4 * g, 4)]
                    dve.tensor_tensor(w, w, ps[:, 6 + g % 2, :].rearrange("p (j e) -> p e j", j=4), ALU.mult).then_inc(gate_free, 1)
                with dve.Fori(0, T // TOKENS) as i:
                    firsts(i, 0)
                    for g in range(1, TOKENS // 4):
                        firsts(i, g)
                        apply(i, g - 1)
                    apply(i, TOKENS // 4 - 1)
                dve.wait_ge(gate_free, (T // 4) * (l + 1) + 2)
                dve.sem_inc(w_ready, T // 4)

            def peer(l):
                norm(2 * l + 1)
                low_input(3 * l + 3)
                only_split(f"wq{l}")
                dve.wait_ge(state_stored, 64 if l == 0 else 96)
                dve.tensor_copy(amp[:], mod[:, 40:48, :])
                group = topk(l)
                middle = topk_row // 4 + 1
                only_split(f"u{l}", groups=(group, middle))
                gate_picks(l)
                only_split(f"u{l}", groups=(middle, EXP // 4))
                turn_picks(l)
                dve.wait_ge(gelu_ready, EXP * (l + 1))
                weigh(l)
                if l == 0:
                    low(SPLIT["v0"], 0)

                def weight_low(e, slot):
                    dve.tensor_tensor(hs[:, 1, slot, :], gates[:, bass.ds(e, 1), :].rearrange("p a t -> p (a t)"),
                                      hs[:, 0, slot, :].bitcast(F32), ALU.subtract).then_inc(w_low, 1)

                dve.wait_ge(w_high, EXP * l + 1)
                weight_low(0, 0)

                def expert_out(i, s):
                    split_low(f"v{l}", i, s)
                    if not (isinstance(i, int) and 4 * i + s == EXP - 1):
                        dve.wait_ge(w_high, i * 4 + (EXP * l + s + 2))
                        weight_low(i * 4 + (s + 1), (s + 1) % 2)
                section(dve, f"v{l}", expert_out)
                dve.wait_ge(half_done, 2 * (SPLIT[f"v{l}"] + EXP))
                dve.wait_ge(x_back, 16 * (l + 1))
                for k in range(KC):
                    chained.count()
                    ins = add_to_x(k, True, ps[:, k, :], amp, chain, chained.at())
                    link(ins)
                dve.sem_inc(x_ready, 1)

            dve.wait_ge(ada_read, 2 * 4)
            low(0, 0)
            norm(0)
            low_input(1)
            only_split("ab_in", first=True)
            retention()
            low(SPLIT["ab_out"], 0)
            head_norm(RET_HEADS, roped[:, 0:RET_HEADS, :], proj0[:, 12:16, :], ret_gain, 1)
            low_input(2)
            dve.wait_ge(ada_read, 2 * 12)
            project_out("ab_out", 16)
            peer(0)
            dve.wait_ge(ada_read, 2 * 24)
            norm(2)
            low_input(4)
            only_split("hg_in")
            hgrn()
            head_norm(HG_HEADS, proj1[:, 8:16, :], proj1[:, 24:32, :], hg_gain, 2)
            low_input(5)
            project_out("hg_out", 16)
            peer(1)
            mean_root(4)
            link(dve.tensor_tensor(h, x, rstd[:, None, :].broadcast_to([P, KC, T]), ALU.mult))
            dve.tensor_tensor(h, h, final_gain[:, :, None].broadcast_to([P, KC, T]), ALU.mult).then_inc(y_ready, 1)

        @block.tensor
        def _(pe):
            made = Tally()

            def bank():
                n = 2 + made.static() % 4
                if made.static() >= 4 or made.i is not None:
                    pe.wait_ge(glue_free, made.at(-3))
                made.count()
                return ps[:, n, :]

            def three(out, slot, cols, high, low, start, stop):
                pe.matmul(out, spl[:, slot, 0, cols], high, start=start, stop=False, skip_group_check=True)
                pe.matmul(out, spl[:, slot, 0, cols], low, start=False, stop=False, skip_group_check=True)
                return pe.matmul(out, spl[:, slot, 1, cols], high, start=False, stop=stop, skip_group_check=True)

            def linear(name, src, first=False, read=lin_free, read_before=None, groups=None):
                m0 = LINEAR[name] if read_before is None else read_before

                def step(i, s):
                    if not (isinstance(i, int) and 4 * i + m0 + s < 2):
                        pe.wait_ge(read, i * 4 + (m0 + s - 1))
                    for k in range(KC):
                        if k % 4 == 0:
                            pe.wait_ge(low_ready, i * 8 + (2 * (SPLIT[name] + s) + k // 4 + 1))
                        ins = three(ps[:, s % 2, 0:T], s % 2, slice(k * P, k * P + P), src[:, 0, k, :], src[:, 1, k, :],
                                    k == 0, k == KC - 1)
                        if k % 4 == 3:
                            ins.then_inc(half_done, 1)
                section(pe, name, step, first=first, groups=groups)

            def condition(g, group):
                for s in range(RING):
                    pe.wait_ge(raw_landed[s], (group + 1) * 16)
                if not (isinstance(g, int) and g == 0):
                    pe.wait_ge(ada_row, g * 2)
                for k in range(KC):
                    ins = pe.matmul(ps[0:NS, 0, :], cs[:, k, :], raw[:, k // 2, ROWS * (k % 2):ROWS * (k % 2) + ROWS],
                                    start=k == 0, stop=k == KC - 1)
                ins.then_inc(ada_full, 1)

            def turn(g, r):
                pe.wait_ge(ada_row, g * 2 + (r + 1))
                if not (isinstance(g, int) and g == 0 and r == 0):
                    pe.wait_ge(ada_read, g * 2 + r)
                for q in range(2):
                    ins = pe.matmul(ps[:, 1, NS * q:NS * q + NS], cond_rows[:, P * q:P * q + P], ident[0:NS, 0:NS], start=True, stop=True)
                ins.then_inc(ada_turned, 1)

            def condition_all(g):
                condition(g, (FIRST["ada0a"] // 4 + g) if g < 4 else (FIRST["ada0b"] // 4 + g - 4))
                turn(g, 0)
                turn(g, 1)

            def sum_squares(src, j):
                pe.wait_ge(sq_ready, j + 1)
                s = bank()
                for k in range(KC):
                    ins = pe.matmul(s[:, 0:T], ones[:], src[:, k, :], start=k == 0, stop=k == KC - 1)
                ins.then_inc(glue_full, 1)

            def head_squares(heads, src, k):
                pe.wait_ge(sqo_ready, k)
                for hd in range(heads):
                    s = bank()
                    pe.matmul(s[:, 0:T], ones[:], src[:, hd, :], start=True, stop=True).then_inc(glue_full, 1)

            def retention():
                pe.wait_ge(ret_tables, 16 * 10)
                pe.wait_ge(lin_free, LINEAR["ab_out"])
                for c in range(2 * RET_HEADS):
                    s = bank()
                    pe.matmul(s[:, 0:T], swap, proj0[:, c, :], start=True, stop=True).then_inc(glue_full, 1)
                for t0, n in TILES:
                    s = bank()
                    for hd in range(RET_HEADS):
                        ins = pe.transpose(s[0:n, hd * P:hd * P + P], proj0[:, 8 + hd, t0:t0 + n], ident[:])
                    ins.then_inc(glue_full, 1)
                condition_all(4)
                condition_all(5)
                pe.wait_ge(roped_ready, 1)
                for t0, n in TILES:
                    s = bank()
                    for hd in range(RET_HEADS):
                        ins = pe.transpose(s[0:n, hd * P:hd * P + P], roped[:, 4 + hd, t0:t0 + n], ident[:])
                    ins.then_inc(glue_full, 1)
                for t0, n in TILES:
                    s = bank()
                    for hd in range(RET_HEADS):
                        ins = pe.matmul(s[0:n, hd * n:hd * n + n], roped[:, 4 + hd, t0:t0 + n], roped[:, hd, t0:t0 + n], start=True, stop=True)
                    ins.then_inc(glue_full, 1)
                condition_all(6)
                pe.wait_ge(glue_free, made.at(-3))
                for c in range(2):
                    s = bank()
                    for hd in range(RET_HEADS):
                        ins = pe.matmul(s[:, hd * P:hd * P + P], ktok[:, c, hd, :], vtok[:, c, hd, :], start=True, stop=True)
                    ins.then_inc(glue_full, 1)
                condition_all(7)
                pe.wait_ge(qd_ready, 1)
                pe.wait_ge(glue_free, made.at(-1))
                for hd in range(RET_HEADS):
                    s = bank()
                    for c in range(2):
                        pe.matmul(s[:, c * P:c * P + P], vtok[:, c, hd, :], att[:, c, hd, :], start=True, stop=c == 0, skip_group_check=True)
                    pe.matmul(s[:, P:2 * P], ret_s1[:, hd, :], qd[:, hd, P:2 * P], start=False, stop=True, skip_group_check=True)
                    pe.matmul(s[:, T_PROMPT:T], vtok[0:32, 2, hd, :], att[0:32, 2, hd, 0:32], start=True, stop=False, skip_group_check=True)
                    for q in range(N_SEQ):
                        lo = T_PROMPT + L_SEQ * q
                        ins = pe.matmul(s[:, lo:lo + L_SEQ], ret_state[:, q, hd, :], qd[:, hd, lo:lo + L_SEQ],
                                        start=False, stop=q == N_SEQ - 1, skip_group_check=True)
                    ins.then_inc(glue_full, 1)
                condition_all(8)
                for hd in range(RET_HEADS):
                    pe.wait_ge(vmask_ready, hd + 1)
                    for g in range(2):
                        s = bank()
                        pe.matmul(s, ktok[0:32, 2, hd, :], ret_vmask[:, 4 * g:4 * g + 4, :], start=True, stop=True).then_inc(glue_full, 1)
                for g in range(9, 12):
                    condition_all(g)

            def hgrn():
                pe.wait_ge(hg_tables, 16 * 6)
                with pe.Fori(0, HG_HEADS) as i:
                    made.enter(i, 12)
                    pe.wait_ge(staged, i * 4 + 4)
                    s = bank()
                    for c, (t0, n) in enumerate(TILES):
                        ins = pe.transpose(s[0:n, c * P:c * P + P], stage[:, 2, t0:t0 + n], ident[:])
                    ins.then_inc(glue_full, 1)
                    pe.wait_ge(x_lev_ready, i + 1)
                    s = bank()
                    for c, (t0, n) in enumerate(TILES):
                        ins = pe.transpose(s[0:n, c * P:c * P + P], fac[:, 7, t0:t0 + n], ident[:])
                    ins.then_inc(glue_full, 1)
                    for c in range(2):
                        cols = slice(c * P, c * P + P)
                        for g in range(2):
                            s = bank()
                            for lev in range(4 * g, 4 * g + 4):
                                a, b = (fac[:, lev, cols],) * 2 if lev < N_LEV else (stage[:, 1, cols], stage[:, 0, cols])
                                lo = (lev - 4 * g) * P
                                ins = pe.matmul(s[:, lo:lo + P], a, b, start=True, stop=True)
                            ins.then_inc(glue_full, 1)
                    s = bank()
                    for k, lev in enumerate((5, 6, 7)):
                        cols = slice(T_PROMPT, T)
                        a, b = (fac[:, lev, cols],) * 2 if lev < N_LEV else (stage[:, 1, cols], stage[:, 0, cols])
                        ins = pe.matmul(s[0:32, 32 * k:32 * k + 32], a, b, start=True, stop=True)
                    ins.then_inc(glue_full, 1)
                    for c in range(2):
                        s = bank()
                        pe.matmul(s[:, 0:P], h_ktok[:, c, :], h_vtok[:, c, :], start=True, stop=True).then_inc(glue_full, 1)
                    s = bank()
                    pe.wait_ge(h_s1_ready, i + 1)
                    for c in range(2):
                        for lev in range(8):
                            pe.matmul(s[:, c * P:c * P + P], h_vtok[:, c, :], h_att[:, c, lev, :], start=lev == 0,
                                      stop=lev == 7 and c == 0, skip_group_check=True)
                    pe.matmul(s[:, P:2 * P], h_s1, qe[:, P:2 * P], start=False, stop=True, skip_group_check=True)
                    for lev in range(3):
                        pe.matmul(s[:, T_PROMPT:T], h_vtok[0:32, 2, :], h_atts[0:32, lev, :], start=lev == 0, stop=False, skip_group_check=True)
                    for q in range(N_SEQ):
                        lo = T_PROMPT + L_SEQ * q
                        ins = pe.matmul(s[:, lo:lo + L_SEQ], s0_stage[:, q, :], qe[:, lo:lo + L_SEQ],
                                        start=False, stop=q == N_SEQ - 1, skip_group_check=True)
                    ins.then_inc(glue_full, 1)
                    pe.wait_ge(h_vm_ready, i + 1)
                    for g in range(2):
                        s = bank()
                        pe.matmul(s, h_ktok[0:32, 2, :], h_vmask[0:32, 4 * g:4 * g + 4, :], start=True, stop=True).then_inc(glue_full, 1)
                made.leave(HG_HEADS)

            def peer(l):
                sum_squares(h, 2 * l + 1)
                pe.wait_ge(h_low, 3 * l + 3)
                linear(f"wq{l}", hs)
                pe.wait_ge(lin_free, LINEAR[f"wq{l}"] + WQ)
                pe.wait_ge(keys_landed, 16 * (l + 1))
                for t0, n in TILES[0:2]:
                    for g in range(4):
                        s = bank()
                        for j in range(4 * g, 4 * g + 4):
                            lo = (j - 4 * g) * P
                            ins = pe.matmul(s[:, lo:lo + P], query[:, j, t0:t0 + n], keys[:, j, :], start=True, stop=True)
                        ins.then_inc(glue_full, 1)
                s = bank()
                for j in range(LISTS):
                    g, lo = 32 * (j // 4), (j % 4) * P
                    ins = pe.matmul(s[g:g + 32, lo:lo + P], query[:, j, T_PROMPT:T], keys[:, j, :], start=True, stop=True)
                ins.then_inc(glue_full, 1)
                middle = topk_row // 4 + 3
                linear(f"u{l}", hs, first=l == 0, read=gelu_ready, read_before=EXP * l, groups=(0, middle))
                pe.wait_ge(picks_ready, l + 1)
                for c in range(2):
                    s = bank()
                    for q in range(3):
                        ins = pe.transpose(s[:, q * P:q * P + P], pick_of[c][:, q, :], ident[:])
                    ins.then_inc(glue_full, 1)
                linear(f"u{l}", hs, read=gelu_ready, read_before=EXP * l, groups=(middle, EXP // 4))

                pe.wait_ge(gelu_ready, EXP * (l + 1))
                pe.wait_ge(choice_ready, l + 1)
                if l == 0:
                    pe.sem_inc(onehot_free, 8)
                with pe.Fori(0, T // TOKENS) as i:
                    if l == 0:
                        condition(i + 12, i + FIRST["ada1"] // 4)
                    for g in range(TOKENS // 4):
                        pe.wait_ge(gate_free, i * (TOKENS // 4) + ((T // 4) * l + g + 1))
                        for j in range(4):
                            pe.wait_ge(first_ready, i * TOKENS + (T * l + 4 * g + j + 1))
                            if j == 0:
                                pe.wait_ge(second_ready, i * (TOKENS // 4) + (T // 4 * l + g + 1 + 2))
                            pe.matmul(ps[:, 6 + g % 2, j * P:j * P + P], onehot[:, (4 * g + j) % 8, :], seconds[:, g % 2, j, :].bitcast(F32),
                                      start=True, stop=True).then_inc(onehot_free, 1)
                        if l == 0 and g in (1, 3):
                            turn(i + 12, g // 2)
                pe.wait_ge(w_ready, (T // 4) * (l + 1))
                pe.wait_ge(glue_free, made.at())
                if l == 0:
                    pe.wait_ge(ada_read, 2 * 24)

                def expert_out(i, s):
                    e = 4 * i + s if isinstance(i, int) else None
                    pe.wait_ge(w_low, i * 4 + (EXP * l + s + 1))
                    for k in range(KC):
                        if k % 4 == 0:
                            pe.wait_ge(low_ready, i * 8 + (2 * (SPLIT[f"v{l}"] + s) + k // 4 + 1))
                        ins = three(ps[:, k, 0:T], s % 2, slice(k * P, k * P + P), hs[:, 0, s % 2, :], hs[:, 1, s % 2, :],
                                    e == 0, e == EXP - 1)
                        if k % 4 == 3:
                            ins.then_inc(half_done, 1)
                section(pe, f"v{l}", expert_out, first=True)
                pe.wait_ge(x_ready, 2 * l + 2)

            pe.wait_ge(const_landed, 16 * 7)
            pe.wait_ge(c_silu, 1)
            for g in range(4):
                condition_all(g)
            pe.wait_ge(ada_read, 2 * 4)
            sum_squares(h, 0)
            pe.wait_ge(h_low, 1)
            linear("ab_in", hs, first=True)
            retention()
            head_squares(RET_HEADS, swapped, 2)
            pe.wait_ge(h_low, 2)
            pe.wait_ge(ada_read, 2 * 12)
            linear("ab_out", hs)
            peer(0)
            sum_squares(h, 2)
            pe.wait_ge(h_low, 4)
            linear("hg_in", hs)
            hgrn()
            head_squares(HG_HEADS, logf, 4)
            pe.wait_ge(h_low, 5)
            linear("hg_out", hs)
            peer(1)
            sum_squares(h, 4)


def tables():
    f = np.float32
    half = P // 2
    inv = (1.0 / (f(10000.0) ** np.linspace(0.0, 1.0, half, dtype=f))).astype(f)
    step = np.concatenate([np.arange(T_PROMPT), np.tile(np.arange(L_SEQ), N_SEQ) + PAST_LEN]).astype(f)
    ang = (step[:, None] * inv[None, :]).astype(f)
    cos, sin = np.cos(ang).T, np.sin(ang).T
    rows = np.arange(P)
    swap = (rows[:, None] == (rows[None, :] + half) % P).astype(f)
    in_chunk = np.concatenate([np.arange(T_PROMPT) % P, np.tile(np.arange(L_SEQ), N_SEQ)])
    lg = LOG_GAMMA
    q_decay = np.broadcast_to(np.exp(lg[:, None] * (in_chunk + 1.0))[None], (P, RET_HEADS, T)).astype(f)
    rel = rows[None, :] - rows[:, None]
    att = (np.where(rel >= 0, np.exp(lg[:, None, None] * np.maximum(rel, 0)), 0.0) * SCALE).transpose(1, 0, 2).astype(f)
    same = (rows[:32, None] // L_SEQ == rows[None, :32] // L_SEQ)
    att_s = (np.where((rel[:32, :32] >= 0) & same, np.exp(lg[:, None, None] * np.maximum(rel[:32, :32], 0)), 0.0) * SCALE)
    key = np.zeros((P, 3, RET_HEADS))
    key[:, 0:2] = (np.exp(lg[None, :] * (P - 1.0 - rows[:, None])) * SCALE)[:, None, :]
    key[:32, 2] = np.exp(lg[None, :] * (L_SEQ - 1.0 - rows[:32, None] % L_SEQ)) * SCALE
    seq_mask = (rows[:32, None] // L_SEQ == np.arange(N_SEQ)[None, :]).astype(f)
    restart = np.broadcast_to((in_chunk != 0).astype(f), (P, T)).copy()
    lev = np.zeros((P, 8, P), f)
    for n, m in enumerate(LEVELS):
        lev[:, n] = (rows[:, None] // (2 * m) == rows[None, :] // (2 * m)) & (rows[:, None] % (2 * m) < m) & (rows[None, :] % (2 * m) >= m)
    lev[:, 7] = np.eye(P)
    return {
        "ident": np.eye(P, dtype=f), "ones": np.ones((P, P), f), "iota": np.broadcast_to(np.arange(P, dtype=f), (P, P)).copy(),
        "cos": np.concatenate([cos, cos]).astype(f), "sin": np.concatenate([-sin, sin]).astype(f), "swap": swap,
        "q_decay": q_decay.copy(), "att_decay": att.copy(), "att_decay_s": att_s.transpose(1, 0, 2).astype(f).copy(),
        "key_decay": key.astype(f), "seq_mask": seq_mask, "restart": restart, "lev_mask": lev,
        "lev_masks": lev[:32, 5:8, :32].copy(),
    }


def kernel(x_prompt, x_sample, state_ret, state_conv, state_hgrn, c_prompt, c_sample,
           ada_w, ada_b, norm_mix_g, norm_ffn_g, ab_w_in, ret_norm_g, conv_w, ab_w_out,
           hg_w_in, hg_lower_bounds, hg_norm_g, hg_w_out, peer_wq, peer_keys, peer_u, peer_v,
           final_norm_g):
    import concourse.bacc as bacc
    from concourse.bass_utils import run_bass_kernel_spmd as run

    def blocks(w):
        w = np.asarray(w)
        lead, n = w.shape[:-2], w.shape[-1] // P
        w = w.reshape(*lead, KC, P, n, P)
        k = len(lead)
        return np.ascontiguousarray(w.transpose(*range(k), k + 2, k + 1, k, k + 3)).reshape(*lead, n, P, D_MODEL)

    def row_blocks(w):
        w = np.asarray(w).reshape(LAYERS, RING, 2, P, 6 * D_MODEL // ROWS, ROWS)
        return w.transpose(0, 4, 1, 3, 2, 5).reshape(LAYERS, ADA, P, D_MODEL)

    def columns(v):
        v = np.asarray(v)
        return np.ascontiguousarray(np.moveaxis(v.reshape(*v.shape[:-1], -1, P), -1, 0))

    xt = np.concatenate([np.asarray(x_prompt)[0], np.asarray(x_sample).reshape(T_SAMPLE, D_MODEL)])
    c = np.concatenate([np.asarray(c_prompt), np.asarray(c_sample), np.asarray(c_sample)[-1:]])
    u = np.asarray(peer_u).reshape(LAYERS, N_KEYS, N_KEYS, KC, P)
    gains = np.concatenate([np.asarray(ret_norm_g)[0].T, np.asarray(hg_norm_g)[0].T,
                            np.asarray(conv_w)[0].reshape(3, 4, P).transpose(2, 0, 1).reshape(P, 12),
                            np.asarray(final_norm_g).reshape(KC, P).T], axis=1)
    norm_g = np.stack([np.asarray(norm_mix_g)[0], np.asarray(norm_ffn_g)[0], np.asarray(norm_mix_g)[1], np.asarray(norm_ffn_g)[1]])
    ins = {
        "x": xt.T.reshape(KC, P, T).transpose(1, 0, 2),
        "c": c.T.reshape(KC, P, NS).transpose(1, 0, 2),
        "state_ret": np.asarray(state_ret)[0].transpose(2, 0, 1, 3),
        "state_conv": np.asarray(state_conv)[0].reshape(N_SEQ, 2, 4, P).transpose(3, 2, 0, 1),
        "state_hgrn": np.asarray(state_hgrn)[0].transpose(2, 1, 0, 3),
        "ada_w": row_blocks(ada_w), "ada_b": columns(ada_b), "norm_g": columns(norm_g), "gains": gains,
        "ab_w_in": blocks(np.asarray(ab_w_in)[0]), "ab_w_out": blocks(np.asarray(ab_w_out)[0]),
        "hg_w_in": blocks(np.asarray(hg_w_in)[0]), "hg_w_out": blocks(np.asarray(hg_w_out)[0]),
        "bounds": columns(hg_lower_bounds),
        "peer_wq": blocks(peer_wq),
        "peer_keys": np.asarray(peer_keys).reshape(LAYERS, LISTS, N_KEYS, P).transpose(0, 3, 1, 2),
        "peer_u": u.transpose(0, 2, 4, 3, 1).reshape(LAYERS, N_KEYS, P, D_MODEL),
        "peer_v": np.asarray(peer_v).reshape(LAYERS, N_KEYS, N_KEYS, D_MODEL).transpose(0, 2, 1, 3),
    }
    ins.update(tables())
    outs = {"y": (P, KC, T), "ret_p": (P, RET_HEADS, P), "ret_s": (P, N_SEQ, RET_HEADS, P), "conv_p": (P, 4, 2),
            "conv_s": (P, 4, N_SEQ, 2), "hg_p": (P, HG_HEADS, P), "hg_s": (P, HG_HEADS, N_SEQ, P)}
    nc = bacc.Bacc("TRN2", target_bir_lowering=False, num_devices=1)
    arrays, t = {}, {}
    for name, a in ins.items():
        arrays[f"in_{name}"] = np.ascontiguousarray(a)
        t[name] = nc.dram_tensor(f"in_{name}", a.shape, F32, kind="ExternalInput").ap()
    for name, shape in outs.items():
        t[name] = nc.dram_tensor(f"out_{name}", shape, F32, kind="ExternalOutput").ap()
    t["x_spill"] = nc.dram_tensor("x_spill", (P, KC, T), F32, kind="Internal").ap()
    trunk(nc, t)
    r = run(nc, [arrays], core_ids=[0]).results[0]
    y = np.asarray(r["out_y"]).transpose(2, 1, 0).reshape(T, D_MODEL)
    return (y[:T_PROMPT][None], y[T_PROMPT:].reshape(N_SEQ, L_SEQ, D_MODEL),
            np.asarray(r["out_ret_p"]).transpose(1, 0, 2)[None, None],
            np.asarray(r["out_conv_p"]).transpose(2, 1, 0).reshape(1, 1, 2, 512),
            np.asarray(r["out_hg_p"]).transpose(1, 0, 2)[None, None],
            np.asarray(r["out_ret_s"]).transpose(1, 2, 0, 3)[None],
            np.asarray(r["out_conv_s"]).transpose(2, 3, 1, 0).reshape(1, N_SEQ, 2, 512),
            np.asarray(r["out_hg_s"]).transpose(2, 1, 0, 3)[None])
```

```python
from contextlib import ExitStack

import numpy as np
import concourse.bass as bass
from concourse import mybir

F32 = mybir.dt.float32
F32R = mybir.dt.float32r
U32 = mybir.dt.uint32
ALU = mybir.AluOpType
ACT = mybir.ActivationFunctionType
AX = mybir.AxisListType

P = 128
D_MODEL = 1024
KC = D_MODEL // P
T_PROMPT = 256
N_SEQ, L_SEQ = 8, 4
T_SAMPLE = N_SEQ * L_SEQ
T = T_PROMPT + T_SAMPLE
PAST_LEN = 2048
LAYERS = 2
RET_HEADS = 4
HG_HEADS = 8
PEER_HEADS = 8
TOPK = 16
N_KEYS = 128
LISTS = 2 * PEER_HEADS
EPS = 1e-6
LOWEST = -3.0e38
NS = N_SEQ + 2
TILES = [(0, P), (P, P), (T_PROMPT, T_SAMPLE)]
LEVELS = [64, 32, 16, 8, 4, 2, 1]
N_LEV = len(LEVELS)
SCALE = float(P) ** -0.5

PAIRS = KC // 2
RING = 4
HALF = D_MODEL // 2
ADA, AB_IN, OUT, WQ, EXP, HG_IN = 48, 28, 8, 16, 128, 32
ROWS = 512
SECTIONS = [("ada0a", 16), ("ab_in", AB_IN), ("ada0b", 32), ("ab_out", OUT), ("wq0", WQ), ("u0", EXP), ("ada1", ADA),
            ("v0", EXP), ("hg_in", HG_IN), ("hg_out", OUT), ("wq1", WQ), ("u1", EXP), ("v1", EXP)]
COUNT = dict(SECTIONS)
FIRST, SPLIT, LINEAR = {}, {}, {}
_n = _b = _m = 0
for _name, _count in SECTIONS:
    FIRST[_name], SPLIT[_name], LINEAR[_name] = _n, _b, _m
    _n += _count
    _b += 0 if _name.startswith("ada") else _count
    _m += 0 if _name[0] in "uv" or _name.startswith("ada") else _count
FOLLOWED = {"ab_out": "wq0", "wq0": "u0", "v0": "hg_in", "hg_in": "hg_out", "hg_out": "wq1", "wq1": "u1", "u1": "v1"}
TOKENS = 24

LOG_GAMMA = np.log(1.0 - 2.0 ** (-5.0 - np.arange(RET_HEADS)))


class Tally:

    def __init__(self):
        self.base = self.local = self.per = 0
        self.i = None

    def enter(self, i, per):
        self.base, self.local, self.i, self.per = self.base + self.local, 0, i, per

    def leave(self, times):
        assert self.local == self.per
        self.base, self.local, self.i = self.base + self.per * times, 0, None

    def count(self):
        self.local += 1

    def static(self):
        return self.base + self.local

    def at(self, more=0):
        v = self.base + self.local + more
        return v if self.i is None else self.i * self.per + v


def trunk(nc, t):
    with ExitStack() as ctx:
        def sb(name, shape, dt=F32):
            return ctx.enter_context(nc.sbuf_tensor(name, shape, dt))

        def sem(name):
            return ctx.enter_context(nc.semaphore(name))

        big = sb("big", [P, N_KEYS * T])
        hs = sb("hs", [P, 2, KC, T], F32R)
        raw = sb("raw", [P, RING, D_MODEL])
        spl = sb("spl", [P, 2, 2, D_MODEL], F32R)
        mod = sb("mod", [P, ADA, NS])
        cs = sb("cs", [P, KC, NS])
        choice = sb("choice", [P, 3, T])
        onehot = sb("onehot", [P, 8, P])
        ident = sb("ident", [P, P])
        ones = sb("ones", [P, P])
        iota = sb("iota", [P, P])
        rstd = sb("rstd", [P, T])
        small = sb("small", [P, 96])
        ps = ctx.enter_context(nc.psum_tensor("ps", [P, 8, 512], F32))

        onehot_flat = onehot[:].rearrange("p a b -> p (a b)")
        cond_rows = [onehot_flat[0:NS, ROWS * j:ROWS * j + ROWS] for j in range(2)]
        half_rows = rstd[0:NS, 0:ROWS // 2]
        best_of = [rstd[:, P * c:P * c + w].rearrange("p (h k) -> p h k", k=TOPK) for c, w in enumerate((P, P, 32))]
        pick_of = [onehot_flat[:, 3 * P * c:3 * P * c + 3 * w].rearrange("p (q i) -> p q i", q=3) for c, w in enumerate((P, P, 32))]
        samp_tmp = small[:, 0:32].rearrange("p (s j) -> p s j", j=L_SEQ)
        apart, seconds = (hs[:].rearrange("p a b c -> p (a b c)")[:, 8 * P * w:8 * P * w + 8 * P].rearrange("p (s j e) -> p s j e", s=2, j=4)
                          for w in range(2))
        ret_gain = small[:, 32:36]
        hg_gain = small[:, 36:44]
        conv_w = small[:, 44:56].rearrange("p (w c) -> p w c", c=4)
        final_gain = small[:, 56:64]

        class Region:
            def __init__(self, start):
                self.at = start

            def take(self, *shape):
                n = int(np.prod(shape))
                v = big[:, self.at:self.at + n]
                self.at += n
                assert self.at <= N_KEYS * T, self.at
                names = " ".join("abcde"[:len(shape)])
                if len(shape) == 1:
                    return v
                sizes = {"abcde"[k]: shape[k] for k in range(1, len(shape))}
                return v.rearrange(f"p ({names}) -> p {names}", **sizes)

        base = Region(0)
        x = base.take(KC, T)
        h = base.take(KC, T)
        after_h = base.at

        r0 = Region(after_h)
        proj0 = r0.take(AB_IN, T)
        cos_t = r0.take(T)
        sin_t = r0.take(T)
        swap = r0.take(P)
        q_decay = r0.take(RET_HEADS, T)
        att_decay = r0.take(RET_HEADS, P)
        att_decay_s = r0.take(RET_HEADS, T_SAMPLE)
        key_decay = r0.take(3, RET_HEADS)
        seq_mask = r0.take(N_SEQ)
        roped = r0.take(2 * RET_HEADS, T)
        swapped = r0.take(2 * RET_HEADS, T)
        qd = r0.take(RET_HEADS, T)
        vtok = r0.take(3, RET_HEADS, P)
        ktok = r0.take(3, RET_HEADS, P)
        att = r0.take(3, RET_HEADS, P)
        ret_s1 = r0.take(RET_HEADS, P)
        ret_s2 = r0.take(RET_HEADS, P)
        ret_state = r0.take(N_SEQ, RET_HEADS, P)
        conv_z = r0.take(4, T_PROMPT + 2)
        conv_zs = r0.take(4, N_SEQ, L_SEQ + 2)
        conv_tail = r0.take(4, 2)
        conv_tails = r0.take(4, N_SEQ, 2)
        ret_vmask = swapped.rearrange("p a b -> p (a b)")[0:T_SAMPLE, 0:1024].rearrange("p (s v) -> p s v", v=P)

        r1 = Region(after_h)
        proj1 = r1.take(HG_IN, T)
        logf = r1.take(HG_HEADS, T)
        restart = r1.take(T)
        fac = r1.take(2, N_LEV + 2, T)
        qe = r1.take(2, T)
        seq_decay = r1.take(2, N_SEQ)
        stage = r1.take(2, 3, T)
        s_in = r1.take(2, N_SEQ, P)
        s_out = r1.take(2, N_SEQ, P)
        h_vtok = r1.take(3, P)
        h_ktok = r1.take(3, P)
        h_att = r1.take(2, 8, P)
        h_atts = r1.take(3, T_SAMPLE)
        h_vmask = r1.take(N_SEQ, P)
        lev_mask = r1.take(8, P)
        lev_masks = r1.take(3, T_SAMPLE)
        h_seq_mask = r1.take(N_SEQ)
        h_s1 = r1.take(P)
        h_out = r1.take(HG_HEADS, P)
        bounds = r1.take(2, HG_HEADS)
        lb = r1.take(HG_HEADS)
        one_lb = r1.take(HG_HEADS)
        lbt = r1.take(HG_HEADS)

        r2 = Region(after_h)
        query = r2.take(LISTS, T)
        keys = r2.take(LISTS, P)
        score_size = [LISTS * P, LISTS * P, 4 * P]
        r3 = Region(N_KEYS * T - sum(score_size) - LISTS * P - 12 * P)
        assert r3.at >= r2.at
        topk_row = r3.at // T
        score_of = [r3.take(n // P, P) for n in score_size]
        spare = r3.take(LISTS * P)
        topv = r3.take(LISTS, TOPK)
        topi_u = r3.take(LISTS, TOPK).bitcast(U32)
        topi = r3.take(LISTS, TOPK)
        pos_u = r3.take(P).bitcast(U32)
        half_u = r3.take(2, P).bitcast(U32)
        half = r3.take(2, P)
        sums_of = [small[:, 64 + 8 * c:72 + 8 * c] for c in range(3)]

        gates = big[:].rearrange("p (e t) -> p e t", t=T)
        ada_b = sb("ada_b", [P, LAYERS, ADA])
        norm_g = sb("norm_g", [P, 2 * LAYERS, KC])
        amp = sb("amp", [P, KC, NS])

        const_landed = sem("const_landed")
        c_landed, x_landed = sem("c_landed"), sem("x_landed")
        raw_landed = [sem(f"raw_landed{s}") for s in range(RING)]
        high_ready, low_ready, half_done = sem("high_ready"), sem("low_ready"), sem("half_done")
        lin_free = sem("lin_free")
        glue_full, glue_free = sem("glue_full"), sem("glue_free")
        chain = sem("chain")
        c_silu = sem("c_silu")
        ada_full = sem("ada_full")
        ada_row, ada_turned, ada_read = sem("ada_row"), sem("ada_turned"), sem("ada_read")
        x_ready = sem("x_ready")
        x_pair = sem("x_pair")
        sq_ready, var_ready, std_ready = sem("sq_ready"), sem("var_ready"), sem("std_ready")
        h_ready, h_high, h_low = sem("h_ready"), sem("h_high"), sem("h_low")
        ret_tables = sem("ret_tables")
        roped_ready, qd_ready, vmask_ready = sem("roped_ready"), sem("qd_ready"), sem("vmask_ready")
        state_ready, state_stored = sem("state_ready"), sem("state_stored")
        sqo_ready, varo_ready, stdo_ready = sem("sqo_ready"), sem("varo_ready"), sem("stdo_ready")
        mixer_done, keys_landed = sem("mixer_done"), sem("keys_landed")
        x_spilled, x_back = sem("x_spilled"), sem("x_back")
        exped, picks_ready = sem("exped"), sem("picks_ready")
        first_ready, second_ready = sem("first_ready"), sem("second_ready")
        onehot_free = sem("onehot_free")
        apart_ready, apart_squared = sem("apart_ready"), sem("apart_squared")
        gate_free = sem("gate_free")
        gelu_ready, topk_done, choice_ready, w_ready = sem("gelu_ready"), sem("topk_done"), sem("choice_ready"), sem("w_ready")
        w_high, w_low = sem("w_high"), sem("w_low")
        hg_tables, keep_ready, log_ready, bound_in, bound_out = sem("hg_tables"), sem("keep_ready"), sem("log_ready"), sem("bound_in"), sem("bound_out")
        gates_ready, staged, s_updated = sem("gates_ready"), sem("staged"), sem("s_updated")
        s_landed, s_stored = [sem(f"s_landed{j}") for j in range(2)], [sem(f"s_stored{j}") for j in range(2)]
        tok_full, tok_out = sem("tok_full"), sem("tok_out")
        o_full, o_out = sem("o_full"), sem("o_out")
        diff_ready, fac_ready, x_lev_ready = sem("diff_ready"), sem("fac_ready"), sem("x_lev_ready")
        h_s1_ready, h_vm_ready = sem("h_s1_ready"), sem("h_vm_ready")
        y_ready, out_done = sem("y_ready"), sem("out_done")

        x_spill = t["x_spill"]
        block = ctx.enter_context(nc.Block())

        def section(eng, name, step, first=False, groups=None):
            n = COUNT[name] // RING
            lo, hi = groups or (0, n)
            if first:
                for s in range(RING):
                    step(lo, s)
                lo += 1
            end = hi - 1 if hi == n else hi
            if end > lo:
                with eng.Fori(lo, end) as i:
                    for s in range(RING):
                        step(i, s)
            if hi == n:
                for s in range(RING):
                    step(n - 1, s)

        def of_head(head, times, more):
            pair, j = head
            return pair * (2 * times) + (j * times + more)

        def after(name, i, s, ahead=1):
            if isinstance(i, int) and 4 * i + s + ahead >= COUNT[name]:
                nxt = FOLLOWED.get(name)
                return (SPLIT[nxt], FIRST[nxt] // 4) if nxt and 4 * i + s + ahead == COUNT[name] else None
            return i * 4 + (SPLIT[name] + s + ahead), i + (FIRST[name] // 4 + (s + ahead) // 4)

        @block.sync
        def _(sp):
            def load(name, src, before=None, groups_before=0):
                def step(i, s):
                    if isinstance(i, int) and i == 0:
                        if before is not None and before.startswith("ada"):
                            sp.wait_ge(ada_full, 4 * groups_before + s - 3)
                        elif before is not None:
                            sp.wait_ge(low_ready, 2 * (SPLIT[before] + COUNT[before] + s - 3))
                    elif name.startswith("ada"):
                        sp.wait_ge(ada_full, i * 4 + (4 * groups_before + s - 3))
                    else:
                        sp.wait_ge(low_ready, i * 8 + 2 * (SPLIT[name] + s - 3))
                    sp.dma_start(raw[:, s, :], src[i * 4 + s]).then_inc(raw_landed[s], 16)
                section(sp, name, step, first=True)

            load("ada0a", t["ada_w"][0][0:16])
            load("ab_in", t["ab_w_in"], "ada0a", 4)
            load("ada0b", t["ada_w"][0][16:48], "ab_in", 4)
            load("ab_out", t["ab_w_out"], "ada0b", 12)
            load("wq0", t["peer_wq"][0], "ab_out")
            load("u0", t["peer_u"][0], "wq0")
            load("ada1", t["ada_w"][1], "u0", 12)
            load("v0", t["peer_v"][0], "ada1", 24)
            load("hg_in", t["hg_w_in"], "v0")
            load("hg_out", t["hg_w_out"], "hg_in")
            load("wq1", t["peer_wq"][1], "hg_out")
            load("u1", t["peer_u"][1], "wq1")
            load("v1", t["peer_v"][1], "u1")

        @block.gpsimd
        def _(pool):
            pool.dma_start(cs[:], t["c"]).then_inc(c_landed, 16)
            pool.dma_start(x, t["x"]).then_inc(x_landed, 16)
            for dst, src in ((ones[:], t["ones"]), (ident[:], t["ident"]), (iota[:], t["iota"]),
                             (ada_b[:], t["ada_b"]), (norm_g[:], t["norm_g"]), (small[:, 32:64], t["gains"])):
                pool.dma_start(dst, src).then_inc(const_landed, 16)
            for dst, src in ((cos_t, t["cos"]), (sin_t, t["sin"]), (swap, t["swap"]), (q_decay, t["q_decay"]),
                             (att_decay, t["att_decay"]), (att_decay_s[0:T_SAMPLE], t["att_decay_s"]),
                             (key_decay, t["key_decay"]), (seq_mask[0:T_SAMPLE], t["seq_mask"]),
                             (ret_state, t["state_ret"]), (conv_zs[:, :, :, 0:2], t["state_conv"])):
                pool.dma_start(dst, src).then_inc(ret_tables, 16)

            def peer(l):
                pool.wait_ge(mixer_done, l + 1)
                pool.dma_start(keys, t["peer_keys"][l]).then_inc(keys_landed, 16)
                pool.wait_ge(x_ready, 2 * l + 1)
                pool.dma_start(x_spill, x).then_inc(x_spilled, 16)
                pool.wait_ge(choice_ready, l + 1)
                pool.wait_ge(gelu_ready, EXP * (l + 1))
                with pool.Fori(0, T // TOKENS) as i:
                    for g in range(TOKENS // 4):
                        n = i * (TOKENS // 4) + (T // 4 * l + g)
                        pool.wait_ge(second_ready, n + 1)
                        pool.tensor_tensor(apart[:, g % 2], iota[:, None, :].broadcast_to([P, 4, P]),
                                           choice[:, 1, bass.ds(i * TOKENS + 4 * g, 4)][:, :, None].broadcast_to([P, 4, P]),
                                           ALU.subtract).then_inc(apart_ready, 1)
                pool.wait_ge(half_done, 2 * (SPLIT[f"v{l}"] + KC + 1))
                pool.dma_start(x, x_spill).then_inc(x_back, 16)

            pool.wait_ge(state_ready, 1)
            pool.dma_start(t["ret_p"], ret_s2).then_inc(state_stored, 16)
            pool.dma_start(t["ret_s"], ret_state).then_inc(state_stored, 16)
            pool.dma_start(t["conv_p"], conv_tail).then_inc(state_stored, 16)
            pool.dma_start(t["conv_s"], conv_tails).then_inc(state_stored, 16)
            peer(0)
            pool.wait_ge(half_done, 2 * (SPLIT["v0"] + EXP))
            for dst, src in ((restart, t["restart"]), (lev_mask, t["lev_mask"]), (lev_masks[0:T_SAMPLE], t["lev_masks"]),
                             (h_seq_mask[0:T_SAMPLE], t["seq_mask"]), (bounds, t["bounds"])):
                pool.dma_start(dst, src).then_inc(hg_tables, 16)

            def load_state(head, slot):
                pool.dma_start(s_in[:, slot:slot + 1], t["state_hgrn"][:, bass.ds(of_head(head, 1, 0), 1)]).then_inc(s_landed[slot], 16)

            def store_state(head, slot):
                pool.wait_ge(s_updated, of_head(head, 1, 1))
                pool.dma_start(t["hg_s"][:, bass.ds(of_head(head, 1, 0), 1)], s_out[:, slot:slot + 1]).then_inc(s_stored[slot], 16)
            for j in range(2):
                load_state((0, j), j)
            with pool.Fori(0, HG_HEADS // 2 - 1) as pair:
                for j in range(2):
                    store_state((pair, j), j)
                    pool.wait_ge(s_stored[j], pair * 16 + 16)
                    load_state((pair + 1, j), j)
            for j in range(2):
                store_state((HG_HEADS // 2 - 1, j), j)
            for j in range(2):
                pool.wait_ge(s_stored[j], 16 * (HG_HEADS // 2))
            pool.wait_ge(state_ready, 2)
            pool.dma_start(t["hg_p"], h_out).then_inc(state_stored, 16)
            peer(1)
            for half in range(2):
                chunks = slice(4 * half, 4 * half + 4)
                pool.wait_ge(y_ready, half + 1)
                pool.dma_start(t["y"][:, chunks], h[:, chunks]).then_inc(out_done, 16)
            pool.wait_ge(out_done, 32)
            pool.wait_ge(state_stored, 16 * 5)
            pool.wait_ge(x_spilled, 32)

        @block.scalar
        def _(act):
            def high_half(number, group, slot, part):
                act.wait_ge(raw_landed[slot], (group + 1) * 16)
                if not (isinstance(number, int) and number < 2):
                    act.wait_ge(half_done, number * 2 + (part - 3))
                cols = slice(HALF * part, HALF * part + HALF)
                act.activation(spl[:, slot % 2, 0, cols], raw[:, slot, cols], ACT.Copy).then_inc(high_ready, 1)

            def high(number, group, slot):
                high_half(number, group, slot, 0)
                high_half(number, group, slot, 1)

            def split_high(name, i, s, ahead=1, parts=(0, 1)):
                if (nxt := after(name, i, s, ahead)) is not None:
                    for part in parts:
                        high_half(*nxt, (s + ahead) % 4, part)

            def read_out(name, reader, groups, first=False):
                if groups[0] == 0:
                    split_high(name, 0, 0)
                    split_high(name, 0, 0, ahead=2, parts=(0,))

                def step(i, s):
                    act.wait_ge(half_done, i * 8 + 2 * (SPLIT[name] + s + 1))
                    reader(i, s)
                    split_high(name, i, s, ahead=2, parts=(1,))
                    split_high(name, i, s, ahead=3, parts=(0,))
                section(act, name, step, first=first, groups=groups)

            def cond_row(g):
                act.wait_ge(ada_full, 4 * g + 4)
                act.activation(cond_rows[g % 2], ps[0:NS, 6 + g % 2, :], ACT.Copy).then_inc(ada_row, 2)

            def cond_column(g):
                act.wait_ge(ada_turned, 2 * g + 2)
                for q in range(4):
                    c = 4 * g + q
                    ins = act.activation(mod[:, c, :], ps[:, g % 2, NS * q:NS * q + NS], ACT.Identity, bias=ada_b[:, 0, c:c + 1])
                ins.then_inc(ada_read, 2)

            def conditioning(groups):
                for g in groups:
                    cond_row(g)
                    if g > groups[0]:
                        cond_column(g - 1)
                cond_column(groups[-1])

            def next_row(g, r):
                act.wait_ge(ada_full, g * 4 + 4)
                act.activation(half_rows, ps[0:NS, 0, 256 * r:256 * r + 256], ACT.Copy).then_inc(ada_row, 1)

            def next_column(g, r, chunk):
                act.wait_ge(ada_turned, g * 2 + (r + 1))
                for q in range(2):
                    c = chunk + (2 * r + q)
                    ins = act.activation(mod[:, bass.ds(c, 1), :].rearrange("p a n -> p (a n)"), ps[:, 1, NS * q:NS * q + NS],
                                         ACT.Identity, bias=ada_b[:, 1, bass.ds(c, 1)])
                ins.then_inc(ada_read, 1)

            def copy_out(name, dst, func, groups, first=False):
                def reader(i, s):
                    act.activation(dst[:, bass.ds(i * 4 + s, 1), :], ps[:, s % 2:s % 2 + 1, 0:T], func).then_inc(lin_free, 1)
                read_out(name, reader, groups, first)

            def only_split(name):
                section(act, name, lambda i, s: split_high(name, i, s))

            def norm(j):
                if j == 0:
                    act.wait_ge(x_landed, 16)
                elif j % 2:
                    act.wait_ge(x_ready, j)
                for c in range(PAIRS):
                    if j in (2, 4):
                        act.wait_ge(x_pair, PAIRS * (j // 2 - 1) + c + 1)
                    act.activation(h[:, 2 * c:2 * c + 2, :], x[:, 2 * c:2 * c + 2, :], ACT.Square).then_inc(sq_ready, 1)
                act.wait_ge(var_ready, j + 1)
                act.activation(rstd[:], rstd[:], ACT.Sqrt).then_inc(std_ready, 1)

            def high_input(k):
                for c in range(PAIRS):
                    act.wait_ge(h_ready, PAIRS * (k - 1) + c + 1)
                    act.activation(hs[:, 0, 2 * c:2 * c + 2, :], h[:, 2 * c:2 * c + 2, :], ACT.Copy).then_inc(h_high, 1)

            def peer(l):
                norm(2 * l + 1)
                high_input(3 * l + 3)
                act.wait_ge(state_stored, 64 if l == 0 else 80)
                copy_out(f"wq{l}", query, ACT.Copy, (0, WQ // 4))
                act.wait_ge(x_spilled, 16 * (l + 1))

                def expert_in(i, s):
                    act.activation(gates[:, bass.ds(i * 4 + s, 1), :], ps[:, s % 2:s % 2 + 1, 0:T], ACT.Gelu).then_inc(gelu_ready, 1)
                read_out(f"u{l}", expert_in, groups=(0, topk_row // 4))
                act.wait_ge(topk_done, l + 1)
                act.activation(rstd[:], rstd[:], ACT.Exp).then_inc(exped, 1)
                read_out(f"u{l}", expert_in, groups=(topk_row // 4, EXP // 4))
                if l == 0:
                    act.sem_inc(second_ready, 2)
                with act.Fori(0, T // TOKENS) as i:
                    for g in range(TOKENS // 4):
                        n = i * (TOKENS // 4) + (T // 4 * l + g)
                        act.wait_ge(apart_ready, n + 1)
                        act.activation(apart[:, g % 2], apart[:, g % 2].bitcast(F32), ACT.Square).then_inc(apart_squared, 1)
                        act.wait_ge(apart_squared, n + 1)
                        act.wait_ge(onehot_free, i * TOKENS + (T * l + 4 * g + 4))
                        act.activation(seconds[:, g % 2], apart[:, g % 2].bitcast(F32), ACT.Relu, bias=1.0, scale=-1.0).then_inc(second_ready, 1)
                        if l == 0:
                            if g in (2, 4):
                                next_column(i + 12, g // 2 - 1, i * 4)
                            if g in (0, 2):
                                next_row(i + 12, g // 2)
                if l == 0:
                    high(SPLIT["v0"], FIRST["v0"] // 4, 0)

                def weight_high(e, slot):
                    act.activation(hs[:, 0, bass.ds(slot, 1), :], gates[:, bass.ds(e, 1), :], ACT.Copy).then_inc(w_high, 1)

                act.wait_ge(w_ready, (T // 4) * (l + 1))
                weight_high(0, 0)

                def expert_out(i, s):
                    split_high(f"v{l}", i, s)
                    if not (isinstance(i, int) and 4 * i + s == EXP - 1):
                        act.wait_ge(half_done, i * 8 + 2 * (SPLIT[f"v{l}"] + s))
                        weight_high(i * 4 + (s + 1), (s + 1) % 2)
                section(act, f"v{l}", expert_out)

            act.wait_ge(c_landed, 16)
            act.activation(cs[:], cs[:], ACT.Silu).then_inc(c_silu, 1)
            norm(0)
            act.wait_ge(const_landed, 16 * 6)
            conditioning(range(4))
            high(0, FIRST["ab_in"] // 4, 0)
            high_input(1)
            copy_out("ab_in", proj0, ACT.Copy, (0, 3), first=True)
            copy_out("ab_in", proj0, ACT.Silu, (3, 4))
            copy_out("ab_in", proj0, ACT.Copy, (4, 7))
            conditioning(range(4, 9))
            act.wait_ge(sqo_ready, 1)
            act.activation(swapped[:, 0:RET_HEADS, :], h[:, 0:RET_HEADS, :], ACT.Square).then_inc(sqo_ready, 1)
            for hd in range(RET_HEADS):
                act.wait_ge(varo_ready, hd + 1)
                act.activation(roped[:, hd, :], roped[:, hd, :], ACT.Sqrt).then_inc(stdo_ready, 1)
            high_input(2)
            conditioning(range(9, 12))
            high(SPLIT["ab_out"], FIRST["ab_out"] // 4, 0)
            only_split("ab_out")
            peer(0)
            norm(2)
            high_input(4)
            copy_out("hg_in", proj1, ACT.Silu, (0, 2))
            copy_out("hg_in", proj1, ACT.Sigmoid, (2, 4))
            copy_out("hg_in", proj1, ACT.Copy, (4, 6))
            copy_out("hg_in", proj1, ACT.Silu, (6, 8))
            act.wait_ge(bound_in, 1)
            act.activation(bounds, bounds, ACT.Exp).then_inc(bound_out, 1)
            act.wait_ge(keep_ready, 1)
            act.activation(logf, proj1[:, 8:16, :], ACT.Ln).then_inc(log_ready, 1)
            act.wait_ge(gates_ready, 1)

            def stage_head(head, slot):
                for k in range(3):
                    act.activation(stage[:, slot, k:k + 1, :], proj1[:, bass.ds(of_head(head, 1, 8 * k), 1), :], ACT.Copy).then_inc(staged, 1)

            def exps(head, slot):
                act.wait_ge(diff_ready, of_head(head, 1, 1))
                act.activation(fac[:, slot, 0:5, 0:T_PROMPT], fac[:, slot, 0:5, 0:T_PROMPT], ACT.Exp)
                act.activation(fac[:, slot, 5:9, :], fac[:, slot, 5:9, :], ACT.Exp).then_inc(fac_ready, 1)

            def tokens_out(head):
                for k, dst in enumerate((h_vtok, h_ktok)):
                    act.wait_ge(tok_full, of_head(head, 2, k + 1))
                    act.activation(dst[:, 0:2, :], ps[:, 6 + k, 0:2 * P].rearrange("p (c v) -> p c v", v=P), ACT.Copy)
                    act.activation(dst[0:32, 2, :], ps[0:32, 6 + k, 2 * P:3 * P], ACT.Copy).then_inc(tok_out, 1)

            def output_out(head):
                act.wait_ge(o_full, of_head(head, 1, 1))
                act.activation(h[:, bass.ds(of_head(head, 1, 0), 1), :], ps[:, 0:1, 0:T], ACT.Copy).then_inc(o_out, 1)

            for j in range(2):
                stage_head((0, j), j)
            exps((0, 0), 0)
            with act.Fori(0, HG_HEADS // 2 - 1) as pair:
                for j in range(2):
                    tokens_out((pair, j))
                    exps((pair, j + 1), 1 - j)
                    output_out((pair, j))
                    stage_head((pair, j + 2), j)
            last_pair = HG_HEADS // 2 - 1
            tokens_out((last_pair, 0))
            exps((last_pair, 1), 1)
            output_out((last_pair, 0))
            tokens_out((last_pair, 1))
            output_out((last_pair, 1))
            act.wait_ge(o_out, HG_HEADS)
            act.wait_ge(sqo_ready, 3)
            act.activation(logf, h, ACT.Square).then_inc(sqo_ready, 1)
            for hd in range(HG_HEADS):
                act.wait_ge(varo_ready, RET_HEADS + hd + 1)
                act.activation(proj1[:, 8 + hd, :], proj1[:, 8 + hd, :], ACT.Sqrt).then_inc(stdo_ready, 1)
            high_input(5)
            only_split("hg_out")
            peer(1)
            norm(4)

        @block.vector
        def _(dve):
            chained, taken = Tally(), Tally()

            def link(ins):
                chained.count()
                ins.then_inc(chain, 1)
                dve.wait_ge(chain, chained.at())

            def product():
                bank = 2 + taken.static() % 4
                taken.count()
                dve.wait_ge(glue_full, taken.at())
                return ps[:, bank, :]

            def released():
                dve.wait_ge(glue_free, taken.at())

            def low(number, slot):
                for part in range(2):
                    dve.wait_ge(high_ready, number * 2 + (part + 1))
                    cols = slice(HALF * part, HALF * part + HALF)
                    dve.tensor_tensor(spl[:, slot % 2, 1, cols], raw[:, slot, cols],
                                      spl[:, slot % 2, 0, cols].bitcast(F32), ALU.subtract).then_inc(low_ready, 1)

            def split_low(name, i, s):
                if (nxt := after(name, i, s)) is not None:
                    low(nxt[0], (s + 1) % 4)

            def only_split(name, first=False, groups=None):
                section(dve, name, lambda i, s: split_low(name, i, s), first=first, groups=groups)

            def mean_root(j):
                s = product()
                dve.tensor_scalar(rstd[:], s[:, 0:T], 1.0 / D_MODEL, None, ALU.mult).then_inc(glue_free, 1)
                released()
                dve.tensor_scalar(rstd[:], rstd[:], EPS, None, ALU.add).then_inc(var_ready, 1)
                dve.wait_ge(std_ready, j + 1)
                link(dve.reciprocal(rstd[:], rstd[:]))

            def norm(j, k):
                part = 24 * (j % 2)
                if j == 0:
                    mean_root(j)
                    dve.wait_ge(ada_read, 2 * 4)
                    low(0, 0)
                gain = norm_g[:, j, :, None].broadcast_to([P, KC, NS])
                link(dve.tensor_scalar(amp[:], mod[:, part + 8:part + 16, :], 1.0, None, ALU.add))
                link(dve.tensor_tensor(amp[:], amp[:], gain, ALU.mult))
                if j > 0:
                    mean_root(j)
                by_seq = h[:, :, T_PROMPT:T].rearrange("p k (s j) -> p k s j", j=L_SEQ)
                for c in range(PAIRS):
                    pair = slice(2 * c, 2 * c + 2)
                    link(dve.tensor_tensor(h[:, pair, :], x[:, pair, :], rstd[:, None, :].broadcast_to([P, 2, T]), ALU.mult))
                    for n in (2 * c, 2 * c + 1):
                        dve.tensor_scalar(h[:, n, 0:T_PROMPT], h[:, n, 0:T_PROMPT], amp[:, n, 0:1], mod[:, part + n, 0:1],
                                          ALU.mult, ALU.add)
                        ins = dve.tensor_tensor(by_seq[:, n], by_seq[:, n], amp[:, n, 1:9, None].broadcast_to([P, N_SEQ, L_SEQ]), ALU.mult)
                    link(ins)
                    for n in (2 * c, 2 * c + 1):
                        ins = dve.tensor_tensor(by_seq[:, n], by_seq[:, n], mod[:, part + n, 1:9, None].broadcast_to([P, N_SEQ, L_SEQ]), ALU.add)
                    ins.then_inc(h_ready, 1)
                    if c > 0:
                        low_input(k, c - 1)
                low_input(k, PAIRS - 1)

            def low_input(k, c):
                dve.wait_ge(h_high, PAIRS * (k - 1) + c + 1)
                pair = slice(2 * c, 2 * c + 2)
                dve.tensor_tensor(hs[:, 1, pair, :], h[:, pair, :], hs[:, 0, pair, :].bitcast(F32), ALU.subtract).then_inc(h_low, 1)

            def add_to_x(k, k_static, bank, gate, freed, freed_value):
                xk = x[:, k, :] if k_static else x[:, bass.ds(k, 1), :]
                xk = xk if k_static else xk.rearrange("p a t -> p (a t)")
                if k_static:
                    gp, gsq = gate[:, k, 0:1], gate[:, k, 1:9]
                else:
                    gp = mod[:, bass.ds(k + gate, 1), 0:1].rearrange("p a t -> p (a t)")
                    gsq = mod[:, bass.ds(k + gate, 1), 1:9].rearrange("p a t -> p (a t)")
                dve.scalar_tensor_tensor(out=xk[:, 0:T_PROMPT], in0=bank[:, 0:T_PROMPT], scalar=gp,
                                         in1=xk[:, 0:T_PROMPT], op0=ALU.mult, op1=ALU.add)
                dve.tensor_tensor(samp_tmp, bank[:, T_PROMPT:T].rearrange("p (s j) -> p s j", j=L_SEQ),
                                  gsq[:, :, None].broadcast_to([P, N_SEQ, L_SEQ]), ALU.mult).then_inc(freed, 1)
                dve.wait_ge(freed, freed_value)
                xs = xk[:, T_PROMPT:T].rearrange("p (s j) -> p s j", j=L_SEQ)
                return dve.tensor_tensor(xs, xs, samp_tmp, ALU.add)

            def project_out(name, gate):
                def step(i, s):
                    split_low(name, i, s)
                    dve.wait_ge(half_done, i * 8 + 2 * (SPLIT[name] + s + 1))
                    ins = add_to_x(i * 4 + s, False, ps[:, s % 2, :], gate, lin_free, i * 4 + (LINEAR[name] + s + 1))
                    link(ins)
                for i in range(OUT // RING):
                    for s in range(RING):
                        step(i, s)
                dve.sem_inc(x_ready, 1)

            def retention():
                dve.wait_ge(ret_tables, 16 * 10)
                dve.wait_ge(lin_free, LINEAR["ab_out"])
                for c in range(2 * RET_HEADS):
                    s = product()
                    dve.tensor_tensor(swapped[:, c, :], s[:, 0:T], sin_t, ALU.mult).then_inc(glue_free, 1)
                link(dve.tensor_tensor(roped, proj0[:, 0:8, :], cos_t[:, None, :].broadcast_to([P, 8, T]), ALU.mult))
                released()
                dve.tensor_tensor(roped, roped, swapped, ALU.add).then_inc(roped_ready, 1)
                dve.wait_ge(roped_ready, 1)
                dve.tensor_tensor(qd, roped[:, 0:4, :], q_decay, ALU.mult).then_inc(qd_ready, 1)
                for c, (_, n) in enumerate(TILES):
                    s = product()
                    dve.tensor_copy(vtok[0:n, c, :, :], s[0:n, :].rearrange("p (h v) -> p h v", v=P)).then_inc(glue_free, 1)
                released()
                dve.tensor_tensor(ret_vmask[:, :, :], vtok[0:32, 2, 0:1, :].broadcast_to([T_SAMPLE, N_SEQ, P]),
                                  seq_mask[0:32, :, None].broadcast_to([T_SAMPLE, N_SEQ, P]), ALU.mult).then_inc(vmask_ready, 1)
                for c, (_, n) in enumerate(TILES):
                    s = product()
                    dve.tensor_tensor(ktok[0:n, c, :, :], s[0:n, :].rearrange("p (h v) -> p h v", v=P),
                                      key_decay[0:n, c, :, None].broadcast_to([n, RET_HEADS, P]), ALU.mult).then_inc(glue_free, 1)
                for c, (_, n) in enumerate(TILES):
                    s = product()
                    mask = att_decay if n == P else att_decay_s[0:n]
                    dve.tensor_tensor(att[0:n, c, :, 0:n], s[0:n, 0:RET_HEADS * n].rearrange("p (h i) -> p h i", i=n),
                                      mask, ALU.mult).then_inc(glue_free, 1)
                s = product()
                dve.tensor_copy(ret_s1, s.rearrange("p (h v) -> p h v", v=P)).then_inc(glue_free, 1)
                released()
                s = product()
                for hd in range(RET_HEADS):
                    ins = dve.scalar_tensor_tensor(out=ret_s2[:, hd, :], in0=ret_s1[:, hd, :], scalar=float(np.exp(LOG_GAMMA[hd] * P)),
                                                   in1=s[:, hd * P:(hd + 1) * P], op0=ALU.mult, op1=ALU.add)
                ins.then_inc(glue_free, 1)
                for hd in range(RET_HEADS):
                    s = product()
                    dve.tensor_copy(h[:, hd, :], s[:, 0:T]).then_inc(glue_free, 1)
                for hd in range(RET_HEADS):
                    for half_seq in range(2):
                        s = product()
                        st = ret_state[:, 4 * half_seq:4 * half_seq + 4, hd, :]
                        dve.scalar_tensor_tensor(out=st, in0=st, scalar=float(np.exp(LOG_GAMMA[hd] * L_SEQ)),
                                                 in1=s.rearrange("p (q v) -> p q v", v=P), op0=ALU.mult, op1=ALU.add).then_inc(glue_free, 1)
                    if hd + 1 < RET_HEADS:
                        dve.tensor_tensor(ret_vmask[:, :, :], vtok[0:32, 2, hd + 1:hd + 2, :].broadcast_to([T_SAMPLE, N_SEQ, P]),
                                          seq_mask[0:32, :, None].broadcast_to([T_SAMPLE, N_SEQ, P]), ALU.mult).then_inc(vmask_ready, 1)
                released()
                dve.memset(conv_z[:, :, 0:2], 0.0)
                dve.tensor_tensor(conv_z[:, :, 2:], proj0[:, 20:24, 0:T_PROMPT], proj0[:, 24:28, 0:T_PROMPT], ALU.mult)
                for c in range(4):
                    cg = proj0[:, 20 + c, T_PROMPT:T].rearrange("p (s j) -> p s j", j=L_SEQ)
                    xin = proj0[:, 24 + c, T_PROMPT:T].rearrange("p (s j) -> p s j", j=L_SEQ)
                    ins = dve.tensor_tensor(conv_zs[:, c, :, 2:6], cg, xin, ALU.mult)
                link(ins)
                dve.tensor_copy(conv_tail, conv_z[:, :, T_PROMPT:T_PROMPT + 2])
                dve.tensor_copy(conv_tails, conv_zs[:, :, :, 4:6]).then_inc(state_ready, 1)

                def dst(c):
                    return h[:, 4 + c, 0:T_PROMPT], h[:, 4 + c, T_PROMPT:T].rearrange("p (s j) -> p s j", j=L_SEQ)
                for c in range(4):
                    a, b = dst(c)
                    dve.tensor_scalar(a, conv_z[:, c, 0:T_PROMPT], conv_w[:, 0, c:c + 1], None, ALU.mult)
                    ins = dve.tensor_scalar(b, conv_zs[:, c, :, 0:4], conv_w[:, 0, c:c + 1], None, ALU.mult)
                link(ins)
                for w in (1, 2):
                    for c in range(4):
                        a, b = dst(c)
                        dve.scalar_tensor_tensor(out=a, in0=conv_z[:, c, w:w + T_PROMPT], scalar=conv_w[:, w, c:c + 1],
                                                 in1=a, op0=ALU.mult, op1=ALU.add)
                        ins = dve.scalar_tensor_tensor(out=b, in0=conv_zs[:, c, :, w:w + 4], scalar=conv_w[:, w, c:c + 1],
                                                       in1=b, op0=ALU.mult, op1=ALU.add)
                    link(ins)
                link(dve.tensor_tensor(h[:, 4:8, :], h[:, 4:8, :], proj0[:, 16:20, :], ALU.mult))

            def head_norm(heads, mean, gate, gain, norms, k):
                dve.sem_inc(sqo_ready, 1)
                link(dve.tensor_tensor(gate, gate, gain[:, :, None].broadcast_to([P, heads, T]), ALU.mult))
                link(dve.tensor_tensor(gate, gate, h[:, 0:heads, :], ALU.mult))
                for hd in range(heads):
                    s = product()
                    dve.tensor_scalar(mean[:, hd, :], s[:, 0:T], 1.0 / P, EPS, ALU.mult, ALU.add).then_inc(glue_free, 1)
                    released()
                    dve.sem_inc(varo_ready, 1)
                for c in range(PAIRS):
                    pair = slice(2 * c, 2 * c + 2)
                    if 2 * c < heads:
                        dve.wait_ge(stdo_ready, norms + 2 * c + 2)
                        link(dve.reciprocal(mean[:, pair, :], mean[:, pair, :]))
                        dve.tensor_tensor(h[:, pair, :], gate[:, pair, :], mean[:, pair, :], ALU.mult).then_inc(h_ready, 1)
                    else:
                        dve.wait_ge(h_ready, PAIRS * (k - 1) + c)
                        dve.sem_inc(h_ready, 1)
                    if c > 0:
                        low_input(k, c - 1)
                low_input(k, PAIRS - 1)
                dve.wait_ge(h_low, PAIRS * k)
                dve.sem_inc(mixer_done, 1)

            def hgrn():
                dve.wait_ge(hg_tables, 16 * 5)
                dve.wait_ge(lin_free, LINEAR["hg_out"])
                link(dve.tensor_tensor(lbt, bounds[:, 0, :], bounds[:, 1, :], ALU.max))
                dve.tensor_tensor(bounds, bounds, lbt[:, None, :].broadcast_to([P, 2, HG_HEADS]), ALU.subtract).then_inc(bound_in, 1)
                dve.wait_ge(bound_out, 1)
                link(dve.tensor_tensor(lbt, bounds[:, 0, :], bounds[:, 1, :], ALU.add))
                link(dve.reciprocal(lbt, lbt))
                link(dve.tensor_tensor(lb, bounds[:, 1, :], lbt, ALU.mult))
                link(dve.tensor_scalar(one_lb, lb, -1.0, 1.0, ALU.mult, ALU.add))
                for hd in range(HG_HEADS):
                    f = proj1[:, 8 + hd, :]
                    ins = dve.tensor_scalar(f, f, one_lb[:, hd:hd + 1], lb[:, hd:hd + 1], ALU.mult, ALU.add)
                ins.then_inc(keep_ready, 1)
                dve.wait_ge(log_ready, 1)
                dve.tensor_scalar(proj1[:, 8:16, :], proj1[:, 8:16, :], -1.0, 1.0, ALU.mult, ALU.add).then_inc(gates_ready, 1)

                def halves(v, m):
                    n = T_PROMPT if m > 2 else T
                    w = v[:, 0:n].rearrange("p (n m) -> p n m", m=2 * m)
                    return w[:, :, 0:m], w[:, :, m:2 * m], w[:, :, m - 1:m].broadcast_to([P, n // (2 * m), m])

                def distances(head, slot):
                    b = fac[:, slot, 8, :]
                    link(dve.tensor_tensor_scan(b, restart, logf[:, bass.ds(of_head(head, 1, 0), 1), :].rearrange("p a t -> p (a t)"), 0.0, ALU.mult, ALU.add))
                    for lev, m in enumerate(LEVELS):
                        b1, b2, mid = halves(b, m)
                        d1, d2, _ = halves(fac[:, slot, lev, :], m)
                        dve.tensor_tensor(d1, mid, b1, ALU.subtract)
                        dve.tensor_tensor(d2, b2, mid, ALU.subtract)
                    for lo, hi, m in ((0, T_PROMPT, P), (T_PROMPT, T, L_SEQ)):
                        bb = b[:, lo:hi].rearrange("p (n m) -> p n m", m=m)
                        dd = fac[:, slot, 7, lo:hi].rearrange("p (n m) -> p n m", m=m)
                        ins = dve.tensor_tensor(dd, bb[:, :, m - 1:m].broadcast_to([P, (hi - lo) // m, m]), bb, ALU.subtract)
                    ins.then_inc(diff_ready, 1)

                def decayed(head, slot):
                    dve.wait_ge(fac_ready, of_head(head, 1, 1))
                    dve.wait_ge(staged, of_head(head, 3, 3))
                    dve.tensor_copy(seq_decay[:, slot], fac[:, slot, 8, T_PROMPT:T].rearrange("p (s j) -> p s j", j=L_SEQ)[:, :, L_SEQ - 1])
                    for lev, m in enumerate(LEVELS):
                        f1, f2, _ = halves(fac[:, slot, lev, :], m)
                        k1, _, _ = halves(stage[:, slot, 1, :], m)
                        _, q2, _ = halves(stage[:, slot, 0, :], m)
                        dve.tensor_tensor(f1, f1, k1, ALU.mult)
                        dve.tensor_tensor(f2, f2, q2, ALU.mult)
                    dve.tensor_tensor(fac[:, slot, 7, :], fac[:, slot, 7, :], stage[:, slot, 1, :], ALU.mult)
                    dve.tensor_tensor(qe[:, slot], fac[:, slot, 8, :], stage[:, slot, 0, :], ALU.mult).then_inc(x_lev_ready, 1)

                def scores(head, slot):
                    dve.wait_ge(tok_out, of_head(head, 2, 1))
                    dve.tensor_tensor(h_vmask[0:32], h_vtok[0:32, 2:3, :].broadcast_to([T_SAMPLE, N_SEQ, P]),
                                      h_seq_mask[0:32, :, None].broadcast_to([T_SAMPLE, N_SEQ, P]), ALU.mult).then_inc(h_vm_ready, 1)
                    for c in range(2):
                        for g in range(2):
                            s = product()
                            dve.tensor_tensor(h_att[:, c, 4 * g:4 * g + 4, :], s.rearrange("p (l i) -> p l i", i=P),
                                              lev_mask[:, 4 * g:4 * g + 4, :], ALU.mult).then_inc(glue_free, 1)
                    s = product()
                    dve.tensor_tensor(h_atts[0:32], s[0:32, 0:96].rearrange("p (l i) -> p l i", i=32), lev_masks[0:32], ALU.mult).then_inc(glue_free, 1)
                    s = product()
                    dve.tensor_copy(h_s1, s[:, 0:P]).then_inc(h_s1_ready, 1)
                    dve.wait_ge(h_s1_ready, of_head(head, 1, 1))
                    dve.scalar_tensor_tensor(out=h_out[:, bass.ds(of_head(head, 1, 0), 1), :].rearrange("p a v -> p (a v)"), in0=h_s1,
                                             scalar=fac[:, slot, 8, T_PROMPT - 1:T_PROMPT], in1=s[:, P:2 * P], op0=ALU.mult, op1=ALU.add).then_inc(glue_free, 1)

                def update_states(head, slot):
                    dve.wait_ge(s_landed[slot], head[0] * 16 + 16)
                    for g in range(2):
                        s = product()
                        for q in range(4):
                            ins = dve.scalar_tensor_tensor(out=s_out[:, slot, 4 * g + q, :], in0=s_in[:, slot, 4 * g + q, :], scalar=seq_decay[:, slot, 4 * g + q:4 * g + q + 1],
                                                           in1=s[:, P * q:P * q + P], op0=ALU.mult, op1=ALU.add)
                        ins.then_inc(glue_free, 1)
                    released()
                    dve.sem_inc(s_updated, 1)

                for j in range(2):
                    distances((0, j), j)
                decayed((0, 0), 0)
                with dve.Fori(0, HG_HEADS // 2 - 1) as pair:
                    chained.enter(pair, 2)
                    taken.enter(pair, 16)
                    for j in range(2):
                        scores((pair, j), j)
                        decayed((pair, j + 1), 1 - j)
                        released()
                        distances((pair, j + 2), j)
                        update_states((pair, j), j)
                chained.leave(HG_HEADS // 2 - 1)
                taken.leave(HG_HEADS // 2 - 1)
                last_pair = HG_HEADS // 2 - 1
                scores((last_pair, 0), 0)
                decayed((last_pair, 1), 1)
                update_states((last_pair, 0), 0)
                scores((last_pair, 1), 1)
                update_states((last_pair, 1), 1)
                dve.sem_inc(state_ready, 1)
                dve.wait_ge(o_out, HG_HEADS)

            def topk(l):
                fed = [0]

                def feed():
                    split_low(f"u{l}", fed[0] // 4, fed[0] % 4)
                    fed[0] += 1

                for c, (_, n) in enumerate(TILES):
                    for g in range(4 if n == P else 1):
                        s = product()
                        dve.tensor_copy(score_of[c][:, 4 * g:4 * g + 4, :], s.rearrange("p (l k) -> p l k", k=P)).then_inc(glue_free, 1)
                        if 4 * c + g in (1, 5, 7):
                            feed()
                released()
                for c in range(3):
                    lists = (LISTS, LISTS, 4)[c]
                    heads = lists // 2
                    sc, sc2 = score_of[c], spare[:, 0:lists * P].rearrange("p (j k) -> p j k", k=P)
                    for j in range(lists):
                        ins = dve.max(topv[:, j, 0:8], sc[:, j, :])
                        if j % 8 == 7:
                            feed()
                    link(ins)
                    for j in range(lists):
                        dve.max_index(topi_u[:, j, 0:8], topv[:, j, 0:8], sc[:, j, :])
                        ins = dve.match_replace(sc2[:, j, :], topv[:, j, 0:8], sc[:, j, :], LOWEST)
                        if j % 3 == 2:
                            feed()
                    link(ins)
                    for j in range(lists):
                        ins = dve.max(topv[:, j, 8:16], sc2[:, j, :])
                        if j % 8 == 7:
                            feed()
                    link(ins)
                    for j in range(lists):
                        ins = dve.max_index(topi_u[:, j, 8:16], topv[:, j, 8:16], sc2[:, j, :])
                        if j % 4 == 3:
                            feed()
                    link(ins)
                    dve.tensor_copy(topi[:, 0:lists], topi_u[:, 0:lists])
                    tv = topv[:, 0:lists].rearrange("p (h q) k -> p h q k", q=2)
                    comb, comb2 = (v.rearrange("p (h q) k -> p h (q k)", q=2) for v in (sc, sc2))
                    best, pos = best_of[c], pos_u[:, 0:heads * TOPK].rearrange("p (h k) -> p h k", k=TOPK)
                    for hd in range(heads):
                        ins = dve.tensor_tensor(comb[:, hd, :].rearrange("p (a b) -> p a b", b=TOPK),
                                                tv[:, hd, 0, :, None].broadcast_to([P, TOPK, TOPK]),
                                                tv[:, hd, 1:2, :].broadcast_to([P, TOPK, TOPK]), ALU.add)
                        if hd % 4 == 3:
                            feed()
                    link(ins)
                    for hd in range(heads):
                        ins = dve.max(best[:, hd, 0:8], comb[:, hd, :])
                        if hd % 4 == 3:
                            feed()
                    link(ins)
                    for hd in range(heads):
                        dve.max_index(pos[:, hd, 0:8], best[:, hd, 0:8], comb[:, hd, :])
                        ins = dve.match_replace(comb2[:, hd, :], best[:, hd, 0:8], comb[:, hd, :], LOWEST)
                        if hd % 2:
                            feed()
                    link(ins)
                    for hd in range(heads):
                        ins = dve.max(best[:, hd, 8:16], comb2[:, hd, :])
                        if hd % 4 == 3:
                            feed()
                    link(ins)
                    for hd in range(heads):
                        ins = dve.max_index(pos[:, hd, 8:16], best[:, hd, 8:16], comb2[:, hd, :])
                        if hd % 4 == 3:
                            feed()
                    link(ins)
                    top = sums_of[c][:, 0:heads]
                    link(dve.tensor_copy(top, best[:, :, 0]))
                    dve.tensor_tensor(best, best, top[:, :, None].broadcast_to([P, heads, TOPK]), ALU.subtract)
                    n = heads * TOPK
                    dve.tensor_single_scalar(half_u[:, 0, 0:n], pos_u[:, 0:n], 4, ALU.logical_shift_right)
                    link(dve.tensor_single_scalar(half_u[:, 1, 0:n], pos_u[:, 0:n], 15, ALU.bitwise_and))
                    link(dve.tensor_copy(half[:, :, 0:n], half_u[:, :, 0:n]))
                    ti = topi[:, 0:lists].rearrange("p (h q) k -> p h q k", q=2)
                    eq = spare[:, 0:n * TOPK].rearrange("p (i a) -> p i a", a=TOPK)
                    for q in range(2):
                        link(dve.tensor_tensor(eq, half[:, q, 0:n, None].broadcast_to([P, n, TOPK]),
                                               iota[:, None, 0:TOPK].broadcast_to([P, n, TOPK]), ALU.is_equal))
                        feed()
                        for hd in range(heads):
                            e = eq[:, TOPK * hd:TOPK * hd + TOPK, :]
                            ins = dve.tensor_tensor(e, e, ti[:, hd, q:q + 1, :].broadcast_to([P, TOPK, TOPK]), ALU.mult)
                        link(ins)
                        feed()
                        link(dve.tensor_reduce(pick_of[c][:, q, :], eq, AX.X, ALU.add))
                        feed()
                dve.sem_inc(topk_done, 1)
                while fed[0] % 4:
                    feed()
                assert fed[0] < topk_row // 4 * 4, (fed[0], topk_row)
                return fed[0] // 4

            def gate_picks(l):
                dve.wait_ge(exped, l + 1)
                for c in range(3):
                    heads = (8, 8, 2)[c]
                    ins = dve.tensor_reduce(sums_of[c][:, 0:heads], best_of[c], AX.X, ALU.add)
                link(ins)
                for c in range(3):
                    ins = dve.reciprocal(sums_of[c][:, 0:(8, 8, 2)[c]], sums_of[c][:, 0:(8, 8, 2)[c]])
                link(ins)
                for c in range(3):
                    heads = (8, 8, 2)[c]
                    ins = dve.tensor_tensor(pick_of[c][:, 2, :].rearrange("p (h k) -> p h k", k=TOPK), best_of[c],
                                            sums_of[c][:, 0:heads, None].broadcast_to([P, heads, TOPK]), ALU.mult)
                ins.then_inc(picks_ready, 1)

            def turn_picks(l):
                for c in range(2):
                    s = product()
                    dve.tensor_copy(choice[:, :, P * c:P * c + P], s[:, 0:3 * P].rearrange("p (q i) -> p q i", i=P)).then_inc(glue_free, 1)
                dve.wait_ge(picks_ready, l + 1)
                for q in range(3):
                    ins = dve.transpose(choice[:, q, T_PROMPT:T], pick_of[2][:, q, :])
                link(ins)
                released()
                dve.sem_inc(choice_ready, 1)

            def weigh(l):
                if l == 0:
                    dve.sem_inc(gate_free, 2)

                def firsts(i, g):
                    for j in range(4):
                        tok = i * TOKENS + (4 * g + j)
                        dve.wait_ge(onehot_free, tok + (T * l + 1))
                        dve.tensor_scalar(onehot[:, (4 * g + j) % 8, :], iota[:], choice[:, 0, bass.ds(tok, 1)], choice[:, 2, bass.ds(tok, 1)],
                                          ALU.is_equal, ALU.mult).then_inc(first_ready, 1)

                def apply(i, g):
                    dve.wait_ge(onehot_free, i * TOKENS + (T * l + 4 * g + 4 + 8))
                    w = gates[:, :, bass.ds(i * TOKENS + 4 * g, 4)]
                    dve.tensor_tensor(w, w, ps[:, 6 + g % 2, :].rearrange("p (j e) -> p e j", j=4), ALU.mult).then_inc(gate_free, 1)
                with dve.Fori(0, T // TOKENS) as i:
                    firsts(i, 0)
                    for g in range(1, TOKENS // 4):
                        firsts(i, g)
                        apply(i, g - 1)
                    apply(i, TOKENS // 4 - 1)
                dve.wait_ge(gate_free, (T // 4) * (l + 1) + 2)
                dve.sem_inc(w_ready, T // 4)

            def peer(l):
                norm(2 * l + 1, 3 * l + 3)
                only_split(f"wq{l}")
                dve.wait_ge(state_stored, 64 if l == 0 else 80)
                dve.tensor_copy(amp[:], mod[:, 40:48, :])
                group = topk(l)
                middle = topk_row // 4 + 1
                only_split(f"u{l}", groups=(group, middle))
                gate_picks(l)
                only_split(f"u{l}", groups=(middle, EXP // 4))
                turn_picks(l)
                dve.wait_ge(gelu_ready, EXP * (l + 1))
                weigh(l)
                if l == 0:
                    low(SPLIT["v0"], 0)

                def weight_low(e, slot):
                    dve.tensor_tensor(hs[:, 1, slot, :], gates[:, bass.ds(e, 1), :].rearrange("p a t -> p (a t)"),
                                      hs[:, 0, slot, :].bitcast(F32), ALU.subtract).then_inc(w_low, 1)

                dve.wait_ge(w_high, EXP * l + 1)
                weight_low(0, 0)

                def expert_out(i, s):
                    split_low(f"v{l}", i, s)
                    if not (isinstance(i, int) and 4 * i + s == EXP - 1):
                        dve.wait_ge(w_high, i * 4 + (EXP * l + s + 2))
                        weight_low(i * 4 + (s + 1), (s + 1) % 2)
                section(dve, f"v{l}", expert_out)
                dve.wait_ge(half_done, 2 * (SPLIT[f"v{l}"] + EXP))
                dve.wait_ge(x_back, 16 * (l + 1))
                for k in range(KC):
                    chained.count()
                    ins = add_to_x(k, True, ps[:, k, :], amp, chain, chained.at())
                    if k % 2:
                        ins.then_inc(x_pair, 1)
                        dve.wait_ge(x_pair, l * PAIRS + k // 2 + 1)
                    else:
                        link(ins)
                dve.sem_inc(x_ready, 1)

            norm(0, 1)
            only_split("ab_in", first=True)
            retention()
            head_norm(RET_HEADS, roped[:, 0:RET_HEADS, :], proj0[:, 12:16, :], ret_gain, 0, 2)
            low(SPLIT["ab_out"], 0)
            dve.wait_ge(ada_read, 2 * 12)
            project_out("ab_out", 16)
            peer(0)
            dve.wait_ge(ada_read, 2 * 24)
            norm(2, 4)
            only_split("hg_in")
            hgrn()
            head_norm(HG_HEADS, proj1[:, 8:16, :], proj1[:, 24:32, :], hg_gain, RET_HEADS, 5)
            project_out("hg_out", 16)
            peer(1)
            mean_root(4)
            for k in range(KC):
                ins = dve.scalar_tensor_tensor(out=h[:, k, :], in0=x[:, k, :], scalar=final_gain[:, k:k + 1], in1=rstd[:],
                                               op0=ALU.mult, op1=ALU.mult)
                if k % 4 == 3:
                    ins.then_inc(y_ready, 1)

        @block.tensor
        def _(pe):
            made = Tally()

            def bank():
                n = 2 + made.static() % 4
                if made.static() >= 4 or made.i is not None:
                    pe.wait_ge(glue_free, made.at(-3))
                made.count()
                return ps[:, n, :]

            def three(out, slot, cols, high, low, start, stop):
                pe.matmul(out, spl[:, slot, 0, cols], high, start=start, stop=False, skip_group_check=True)
                pe.matmul(out, spl[:, slot, 0, cols], low, start=False, stop=False, skip_group_check=True)
                return pe.matmul(out, spl[:, slot, 1, cols], high, start=False, stop=stop, skip_group_check=True)

            def linear(name, src, first=False, read=lin_free, read_before=None, groups=None, entry=None):
                m0 = LINEAR[name] if read_before is None else read_before

                def step(i, s):
                    if not (isinstance(i, int) and 4 * i + m0 + s < 2):
                        pe.wait_ge(read, i * 4 + (m0 + s - 1))
                    for k in range(KC):
                        if entry and s == 0 and k % 2 == 0:
                            pe.wait_ge(h_low, PAIRS * (entry - 1) + k // 2 + 1)
                        if k % 4 == 0:
                            pe.wait_ge(low_ready, i * 8 + (2 * (SPLIT[name] + s) + k // 4 + 1))
                        ins = three(ps[:, s % 2, 0:T], s % 2, slice(k * P, k * P + P), src[:, 0, k, :], src[:, 1, k, :],
                                    k == 0, k == KC - 1)
                        if k % 4 == 3:
                            ins.then_inc(half_done, 1)
                section(pe, name, step, first=first, groups=groups)

            def condition(out, group):
                for k in range(KC):
                    if k % 2 == 0:
                        pe.wait_ge(raw_landed[k // 2], (group + 1) * 16)
                    ins = pe.matmul(out, cs[:, k, :], raw[:, k // 2, ROWS * (k % 2):ROWS * (k % 2) + ROWS],
                                    start=k == 0, stop=k == KC - 1)
                    if k % 2:
                        ins.then_inc(ada_full, 1)

            def condition_first(g, start=False):
                if g > 1:
                    pe.wait_ge(ada_row, 2 * (g - 1))
                condition(ps[0:NS, 6 + g % 2, :], (FIRST["ada0a"] // 4 + g) if g < 4 else (FIRST["ada0b"] // 4 + g - 4))
                if not start:
                    turn_first(g - 1)

            def turn_first(g):
                pe.wait_ge(ada_row, 2 * (g + 1))
                if g > 1:
                    pe.wait_ge(ada_read, 2 * (g - 1))
                for q in range(4):
                    ins = pe.matmul(ps[:, g % 2, NS * q:NS * q + NS], cond_rows[g % 2][:, P * q:P * q + P], ident[0:NS, 0:NS], start=True, stop=True)
                ins.then_inc(ada_turned, 2)

            def turn(g, r):
                pe.wait_ge(ada_row, g * 2 + (r + 1))
                pe.wait_ge(ada_read, g * 2 + r)
                for q in range(2):
                    ins = pe.matmul(ps[:, 1, NS * q:NS * q + NS], half_rows[:, P * q:P * q + P], ident[0:NS, 0:NS], start=True, stop=True)
                ins.then_inc(ada_turned, 1)

            def sum_squares(src, j):
                s = bank()
                for k in range(KC):
                    if k % 2 == 0:
                        pe.wait_ge(sq_ready, PAIRS * j + k // 2 + 1)
                    ins = pe.matmul(s[:, 0:T], ones[:], src[:, k, :], start=k == 0, stop=k == KC - 1)
                ins.then_inc(glue_full, 1)

            def head_squares(heads, src, k):
                pe.wait_ge(sqo_ready, k)
                for hd in range(heads):
                    s = bank()
                    pe.matmul(s[:, 0:T], ones[:], src[:, hd, :], start=True, stop=True).then_inc(glue_full, 1)

            def retention():
                pe.wait_ge(ret_tables, 16 * 10)
                pe.wait_ge(lin_free, LINEAR["ab_out"])
                for c in range(2 * RET_HEADS):
                    s = bank()
                    pe.matmul(s[:, 0:T], swap, proj0[:, c, :], start=True, stop=True).then_inc(glue_full, 1)
                for t0, n in TILES:
                    s = bank()
                    for hd in range(RET_HEADS):
                        ins = pe.transpose(s[0:n, hd * P:hd * P + P], proj0[:, 8 + hd, t0:t0 + n], ident[:])
                    ins.then_inc(glue_full, 1)
                condition_first(4, start=True)
                condition_first(5)
                pe.wait_ge(roped_ready, 1)
                for t0, n in TILES:
                    s = bank()
                    for hd in range(RET_HEADS):
                        ins = pe.transpose(s[0:n, hd * P:hd * P + P], roped[:, 4 + hd, t0:t0 + n], ident[:])
                    ins.then_inc(glue_full, 1)
                for t0, n in TILES:
                    s = bank()
                    for hd in range(RET_HEADS):
                        ins = pe.matmul(s[0:n, hd * n:hd * n + n], roped[:, 4 + hd, t0:t0 + n], roped[:, hd, t0:t0 + n], start=True, stop=True)
                    ins.then_inc(glue_full, 1)
                condition_first(6)
                pe.wait_ge(glue_free, made.at(-3))
                for c in range(2):
                    s = bank()
                    for hd in range(RET_HEADS):
                        ins = pe.matmul(s[:, hd * P:hd * P + P], ktok[:, c, hd, :], vtok[:, c, hd, :], start=True, stop=True)
                    ins.then_inc(glue_full, 1)
                condition_first(7)
                pe.wait_ge(qd_ready, 1)
                pe.wait_ge(glue_free, made.at(-1))
                for hd in range(RET_HEADS):
                    s = bank()
                    for c in range(2):
                        pe.matmul(s[:, c * P:c * P + P], vtok[:, c, hd, :], att[:, c, hd, :], start=True, stop=c == 0, skip_group_check=True)
                    pe.matmul(s[:, P:2 * P], ret_s1[:, hd, :], qd[:, hd, P:2 * P], start=False, stop=True, skip_group_check=True)
                    pe.matmul(s[:, T_PROMPT:T], vtok[0:32, 2, hd, :], att[0:32, 2, hd, 0:32], start=True, stop=False, skip_group_check=True)
                    for q in range(N_SEQ):
                        lo = T_PROMPT + L_SEQ * q
                        ins = pe.matmul(s[:, lo:lo + L_SEQ], ret_state[:, q, hd, :], qd[:, hd, lo:lo + L_SEQ],
                                        start=False, stop=q == N_SEQ - 1, skip_group_check=True)
                    ins.then_inc(glue_full, 1)
                condition_first(8)
                for hd in range(RET_HEADS):
                    pe.wait_ge(vmask_ready, hd + 1)
                    for g in range(2):
                        s = bank()
                        pe.matmul(s, ktok[0:32, 2, hd, :], ret_vmask[:, 4 * g:4 * g + 4, :], start=True, stop=True).then_inc(glue_full, 1)
                turn_first(8)

            def hgrn():
                def head_products(head, slot):
                    pe.wait_ge(staged, of_head(head, 3, 3))
                    for c, (t0, n) in enumerate(TILES):
                        ins = pe.transpose(ps[0:n, 6, c * P:c * P + P], stage[:, slot, 2, t0:t0 + n], ident[:])
                    ins.then_inc(tok_full, 1)
                    pe.wait_ge(x_lev_ready, of_head(head, 1, 1))
                    for c, (t0, n) in enumerate(TILES):
                        ins = pe.transpose(ps[0:n, 7, c * P:c * P + P], fac[:, slot, 7, t0:t0 + n], ident[:])
                    ins.then_inc(tok_full, 1)

                    def factors(lev, cols):
                        return (fac[:, slot, lev, cols],) * 2 if lev < N_LEV else (stage[:, slot, 1, cols], stage[:, slot, 0, cols])
                    for c in range(2):
                        for g in range(2):
                            s = bank()
                            for lev in range(4 * g, 4 * g + 4):
                                lo = (lev - 4 * g) * P
                                ins = pe.matmul(s[:, lo:lo + P], *factors(lev, slice(c * P, c * P + P)), start=True, stop=True)
                            ins.then_inc(glue_full, 1)
                    s = bank()
                    for k, lev in enumerate((5, 6, 7)):
                        ins = pe.matmul(s[0:32, 32 * k:32 * k + 32], *factors(lev, slice(T_PROMPT, T)), start=True, stop=True)
                    ins.then_inc(glue_full, 1)
                    pe.wait_ge(tok_out, of_head(head, 2, 2))
                    s = bank()
                    for c in range(2):
                        ins = pe.matmul(s[:, c * P:c * P + P], h_ktok[:, c, :], h_vtok[:, c, :], start=True, stop=True)
                    ins.then_inc(glue_full, 1)
                    pe.wait_ge(s_landed[slot], head[0] * 16 + 16)
                    pe.wait_ge(h_s1_ready, of_head(head, 1, 1))
                    o = ps[:, 0, :]
                    for c in range(2):
                        for lev in range(8):
                            pe.matmul(o[:, c * P:c * P + P], h_vtok[:, c, :], h_att[:, c, lev, :], start=lev == 0,
                                      stop=lev == 7 and c == 0, skip_group_check=True)
                    pe.matmul(o[:, P:2 * P], h_s1, qe[:, slot, P:2 * P], start=False, stop=True, skip_group_check=True)
                    for lev in range(3):
                        pe.matmul(o[:, T_PROMPT:T], h_vtok[0:32, 2, :], h_atts[0:32, lev, :], start=lev == 0, stop=False, skip_group_check=True)
                    for q in range(N_SEQ):
                        lo = T_PROMPT + L_SEQ * q
                        ins = pe.matmul(o[:, lo:lo + L_SEQ], s_in[:, slot, q, :], qe[:, slot, lo:lo + L_SEQ],
                                        start=False, stop=q == N_SEQ - 1, skip_group_check=True)
                    ins.then_inc(o_full, 1)
                    pe.wait_ge(h_vm_ready, of_head(head, 1, 1))
                    for g in range(2):
                        s = bank()
                        pe.matmul(s, h_ktok[0:32, 2, :], h_vmask[0:32, 4 * g:4 * g + 4, :], start=True, stop=True).then_inc(glue_full, 1)
                    pe.wait_ge(o_out, of_head(head, 1, 1))

                with pe.Fori(0, HG_HEADS // 2) as pair:
                    made.enter(pair, 16)
                    for j in range(2):
                        head_products((pair, j), j)
                made.leave(HG_HEADS // 2)

            def peer(l):
                sum_squares(h, 2 * l + 1)
                linear(f"wq{l}", hs, entry=3 * l + 3)
                pe.wait_ge(lin_free, LINEAR[f"wq{l}"] + WQ)
                pe.wait_ge(keys_landed, 16 * (l + 1))
                for t0, n in TILES[0:2]:
                    for g in range(4):
                        s = bank()
                        for j in range(4 * g, 4 * g + 4):
                            lo = (j - 4 * g) * P
                            ins = pe.matmul(s[:, lo:lo + P], query[:, j, t0:t0 + n], keys[:, j, :], start=True, stop=True)
                        ins.then_inc(glue_full, 1)
                s = bank()
                for j in range(LISTS):
                    g, lo = 32 * (j // 4), (j % 4) * P
                    ins = pe.matmul(s[g:g + 32, lo:lo + P], query[:, j, T_PROMPT:T], keys[:, j, :], start=True, stop=True)
                ins.then_inc(glue_full, 1)
                middle = topk_row // 4 + 3
                linear(f"u{l}", hs, first=l == 0, read=gelu_ready, read_before=EXP * l, groups=(0, middle))
                pe.wait_ge(picks_ready, l + 1)
                for c in range(2):
                    s = bank()
                    for q in range(3):
                        ins = pe.transpose(s[:, q * P:q * P + P], pick_of[c][:, q, :], ident[:])
                    ins.then_inc(glue_full, 1)
                linear(f"u{l}", hs, read=gelu_ready, read_before=EXP * l, groups=(middle, EXP // 4))

                pe.wait_ge(gelu_ready, EXP * (l + 1))
                pe.wait_ge(choice_ready, l + 1)
                if l == 0:
                    pe.sem_inc(onehot_free, 8)
                with pe.Fori(0, T // TOKENS) as i:
                    if l == 0:
                        pe.wait_ge(ada_row, i * 2 + 24)
                        condition(ps[0:NS, 0, :], i + FIRST["ada1"] // 4)
                    for g in range(TOKENS // 4):
                        pe.wait_ge(gate_free, i * (TOKENS // 4) + ((T // 4) * l + g + 1))
                        for j in range(4):
                            pe.wait_ge(first_ready, i * TOKENS + (T * l + 4 * g + j + 1))
                            if j == 0:
                                pe.wait_ge(second_ready, i * (TOKENS // 4) + (T // 4 * l + g + 1 + 2))
                            pe.matmul(ps[:, 6 + g % 2, j * P:j * P + P], onehot[:, (4 * g + j) % 8, :], seconds[:, g % 2, j, :].bitcast(F32),
                                      start=True, stop=True).then_inc(onehot_free, 1)
                        if l == 0 and g in (1, 3):
                            turn(i + 12, g // 2)
                pe.wait_ge(w_ready, (T // 4) * (l + 1))
                pe.wait_ge(glue_free, made.at())
                if l == 0:
                    pe.wait_ge(ada_read, 2 * 24)

                def expert_out(i, s):
                    e = 4 * i + s if isinstance(i, int) else None
                    pe.wait_ge(w_low, i * 4 + (EXP * l + s + 1))
                    for k in range(KC):
                        if k % 4 == 0:
                            pe.wait_ge(low_ready, i * 8 + (2 * (SPLIT[f"v{l}"] + s) + k // 4 + 1))
                        ins = three(ps[:, k, 0:T], s % 2, slice(k * P, k * P + P), hs[:, 0, s % 2, :], hs[:, 1, s % 2, :],
                                    e == 0, e == EXP - 1)
                        if k % 4 == 3:
                            ins.then_inc(half_done, 1)
                section(pe, f"v{l}", expert_out, first=True)
                pe.wait_ge(x_ready, 2 * l + 2)

            pe.wait_ge(c_silu, 1)
            condition_first(0, start=True)
            pe.wait_ge(const_landed, 16 * 6)
            sum_squares(h, 0)
            for g in range(1, 4):
                condition_first(g)
            turn_first(3)
            pe.wait_ge(ada_read, 2 * 4)
            linear("ab_in", hs, first=True, entry=1)
            retention()
            head_squares(RET_HEADS, swapped, 2)
            for g in range(9, 12):
                condition_first(g, start=g == 9)
            turn_first(11)
            pe.wait_ge(ada_read, 2 * 12)
            linear("ab_out", hs, entry=2)
            peer(0)
            sum_squares(h, 2)
            linear("hg_in", hs, entry=4)
            hgrn()
            head_squares(HG_HEADS, logf, 4)
            linear("hg_out", hs, entry=5)
            peer(1)
            sum_squares(h, 4)


def tables():
    f = np.float32
    half = P // 2
    inv = (1.0 / (f(10000.0) ** np.linspace(0.0, 1.0, half, dtype=f))).astype(f)
    step = np.concatenate([np.arange(T_PROMPT), np.tile(np.arange(L_SEQ), N_SEQ) + PAST_LEN]).astype(f)
    ang = (step[:, None] * inv[None, :]).astype(f)
    cos, sin = np.cos(ang).T, np.sin(ang).T
    rows = np.arange(P)
    swap = (rows[:, None] == (rows[None, :] + half) % P).astype(f)
    in_chunk = np.concatenate([np.arange(T_PROMPT) % P, np.tile(np.arange(L_SEQ), N_SEQ)])
    lg = LOG_GAMMA
    q_decay = np.broadcast_to(np.exp(lg[:, None] * (in_chunk + 1.0))[None], (P, RET_HEADS, T)).astype(f)
    rel = rows[None, :] - rows[:, None]
    att = (np.where(rel >= 0, np.exp(lg[:, None, None] * np.maximum(rel, 0)), 0.0) * SCALE).transpose(1, 0, 2).astype(f)
    same = (rows[:32, None] // L_SEQ == rows[None, :32] // L_SEQ)
    att_s = (np.where((rel[:32, :32] >= 0) & same, np.exp(lg[:, None, None] * np.maximum(rel[:32, :32], 0)), 0.0) * SCALE)
    key = np.zeros((P, 3, RET_HEADS))
    key[:, 0:2] = (np.exp(lg[None, :] * (P - 1.0 - rows[:, None])) * SCALE)[:, None, :]
    key[:32, 2] = np.exp(lg[None, :] * (L_SEQ - 1.0 - rows[:32, None] % L_SEQ)) * SCALE
    seq_mask = (rows[:32, None] // L_SEQ == np.arange(N_SEQ)[None, :]).astype(f)
    restart = np.broadcast_to((in_chunk != 0).astype(f), (P, T)).copy()
    lev = np.zeros((P, 8, P), f)
    for n, m in enumerate(LEVELS):
        lev[:, n] = (rows[:, None] // (2 * m) == rows[None, :] // (2 * m)) & (rows[:, None] % (2 * m) < m) & (rows[None, :] % (2 * m) >= m)
    lev[:, 7] = np.eye(P)
    return {
        "ident": np.eye(P, dtype=f), "ones": np.ones((P, P), f), "iota": np.broadcast_to(np.arange(P, dtype=f), (P, P)).copy(),
        "cos": np.concatenate([cos, cos]).astype(f), "sin": np.concatenate([-sin, sin]).astype(f), "swap": swap,
        "q_decay": q_decay.copy(), "att_decay": att.copy(), "att_decay_s": att_s.transpose(1, 0, 2).astype(f).copy(),
        "key_decay": key.astype(f), "seq_mask": seq_mask, "restart": restart, "lev_mask": lev,
        "lev_masks": lev[:32, 5:8, :32].copy(),
    }


def kernel(x_prompt, x_sample, state_ret, state_conv, state_hgrn, c_prompt, c_sample,
           ada_w, ada_b, norm_mix_g, norm_ffn_g, ab_w_in, ret_norm_g, conv_w, ab_w_out,
           hg_w_in, hg_lower_bounds, hg_norm_g, hg_w_out, peer_wq, peer_keys, peer_u, peer_v,
           final_norm_g):
    import concourse.bacc as bacc
    from concourse.bass_utils import run_bass_kernel_spmd as run

    def blocks(w):
        w = np.asarray(w)
        lead, n = w.shape[:-2], w.shape[-1] // P
        w = w.reshape(*lead, KC, P, n, P)
        k = len(lead)
        return np.ascontiguousarray(w.transpose(*range(k), k + 2, k + 1, k, k + 3)).reshape(*lead, n, P, D_MODEL)

    def row_blocks(w):
        w = np.asarray(w).reshape(LAYERS, RING, 2, P, 6 * D_MODEL // ROWS, ROWS)
        return w.transpose(0, 4, 1, 3, 2, 5).reshape(LAYERS, ADA, P, D_MODEL)

    def columns(v):
        v = np.asarray(v)
        return np.ascontiguousarray(np.moveaxis(v.reshape(*v.shape[:-1], -1, P), -1, 0))

    xt = np.concatenate([np.asarray(x_prompt)[0], np.asarray(x_sample).reshape(T_SAMPLE, D_MODEL)])
    c = np.concatenate([np.asarray(c_prompt), np.asarray(c_sample), np.asarray(c_sample)[-1:]])
    u = np.asarray(peer_u).reshape(LAYERS, N_KEYS, N_KEYS, KC, P)
    gains = np.concatenate([np.asarray(ret_norm_g)[0].T, np.asarray(hg_norm_g)[0].T,
                            np.asarray(conv_w)[0].reshape(3, 4, P).transpose(2, 0, 1).reshape(P, 12),
                            np.asarray(final_norm_g).reshape(KC, P).T], axis=1)
    norm_g = np.stack([np.asarray(norm_mix_g)[0], np.asarray(norm_ffn_g)[0], np.asarray(norm_mix_g)[1], np.asarray(norm_ffn_g)[1]])
    ins = {
        "x": xt.T.reshape(KC, P, T).transpose(1, 0, 2),
        "c": c.T.reshape(KC, P, NS).transpose(1, 0, 2),
        "state_ret": np.asarray(state_ret)[0].transpose(2, 0, 1, 3),
        "state_conv": np.asarray(state_conv)[0].reshape(N_SEQ, 2, 4, P).transpose(3, 2, 0, 1),
        "state_hgrn": np.asarray(state_hgrn)[0].transpose(2, 1, 0, 3),
        "ada_w": row_blocks(ada_w), "ada_b": columns(ada_b), "norm_g": columns(norm_g), "gains": gains,
        "ab_w_in": blocks(np.asarray(ab_w_in)[0]), "ab_w_out": blocks(np.asarray(ab_w_out)[0]),
        "hg_w_in": blocks(np.asarray(hg_w_in)[0]), "hg_w_out": blocks(np.asarray(hg_w_out)[0]),
        "bounds": columns(hg_lower_bounds),
        "peer_wq": blocks(peer_wq),
        "peer_keys": np.asarray(peer_keys).reshape(LAYERS, LISTS, N_KEYS, P).transpose(0, 3, 1, 2),
        "peer_u": u.transpose(0, 2, 4, 3, 1).reshape(LAYERS, N_KEYS, P, D_MODEL),
        "peer_v": np.asarray(peer_v).reshape(LAYERS, N_KEYS, N_KEYS, D_MODEL).transpose(0, 2, 1, 3),
    }
    ins.update(tables())
    outs = {"y": (P, KC, T), "ret_p": (P, RET_HEADS, P), "ret_s": (P, N_SEQ, RET_HEADS, P), "conv_p": (P, 4, 2),
            "conv_s": (P, 4, N_SEQ, 2), "hg_p": (P, HG_HEADS, P), "hg_s": (P, HG_HEADS, N_SEQ, P)}
    nc = bacc.Bacc("TRN2", target_bir_lowering=False, num_devices=1)
    arrays, t = {}, {}
    for name, a in ins.items():
        arrays[f"in_{name}"] = np.ascontiguousarray(a)
        t[name] = nc.dram_tensor(f"in_{name}", a.shape, F32, kind="ExternalInput").ap()
    for name, shape in outs.items():
        t[name] = nc.dram_tensor(f"out_{name}", shape, F32, kind="ExternalOutput").ap()
    t["x_spill"] = nc.dram_tensor("x_spill", (P, KC, T), F32, kind="Internal").ap()
    trunk(nc, t)
    r = run(nc, [arrays], core_ids=[0]).results[0]
    y = np.asarray(r["out_y"]).transpose(2, 1, 0).reshape(T, D_MODEL)
    return (y[:T_PROMPT][None], y[T_PROMPT:].reshape(N_SEQ, L_SEQ, D_MODEL),
            np.asarray(r["out_ret_p"]).transpose(1, 0, 2)[None, None],
            np.asarray(r["out_conv_p"]).transpose(2, 1, 0).reshape(1, 1, 2, 512),
            np.asarray(r["out_hg_p"]).transpose(1, 0, 2)[None, None],
            np.asarray(r["out_ret_s"]).transpose(1, 2, 0, 3)[None],
            np.asarray(r["out_conv_s"]).transpose(2, 3, 1, 0).reshape(1, N_SEQ, 2, 512),
            np.asarray(r["out_hg_s"]).transpose(2, 1, 0, 3)[None])
```
